# Optimizing a Trainium2 kernel written in Bass

```python
import math
import jax, jax.numpy as jnp
from jax import lax
import numpy as np

D_MODEL = 1024
BATCH = 1
SEQ = 256
DEPTH = 1

N_META = 16
EPS = 1e-6
BLOCK = 128
D_RNN = D_MODEL
RG_BLOCKS = 8
RG_BS = D_RNN // RG_BLOCKS
CONV_W = 4
RG_C = 8.0
MLA_HEADS = 16
Q_LORA = 384
KV_LORA = 256
QK_NOPE = 64
QK_ROPE = 32
V_DIM = 64
ROPE_BASE = 10000.0
PEER_HEADS = 8
PEER_NKEYS = 128
PEER_EXPERTS = PEER_NKEYS * PEER_NKEYS
PEER_QDIM = 256
PEER_TOPK = 16

IN_SIZES = (D_RNN, D_RNN, Q_LORA, KV_LORA, QK_ROPE, D_MODEL, D_MODEL)
IN_SPLITS = tuple(int(s) for s in np.cumsum(IN_SIZES)[:-1])
D_IN = int(sum(IN_SIZES))


def _rmsnorm(x, g):
    xf = x.astype(jnp.float32)
    xf = xf * lax.rsqrt(jnp.mean(xf * xf, axis=-1, keepdims=True) + EPS)
    return xf.astype(x.dtype) * g

def _rope(x, pos):
    half = QK_ROPE // 2
    inv = jnp.power(ROPE_BASE, -jnp.arange(half, dtype=jnp.float32) * (2.0 / QK_ROPE))
    ang = pos[:, None] * inv[None, :]
    cos = jnp.cos(ang)[None, :, None, :].astype(x.dtype)
    sin = jnp.sin(ang)[None, :, None, :].astype(x.dtype)
    x1, x2 = x[..., :half], x[..., half:]
    return jnp.concatenate([x1 * cos - x2 * sin, x1 * sin + x2 * cos], axis=-1)

def _causal_conv(x, w, b):
    T = x.shape[1]
    xp = jnp.pad(x, ((0, 0), (CONV_W - 1, 0), (0, 0)))
    y = xp[:, 0:T] * w[0] + b
    for k in range(1, CONV_W):
        y = y + xp[:, k:k + T] * w[k]
    return y

def _lin_combine(e1, e2):
    a1, b1 = e1
    a2, b2 = e2
    return (a1 * a2, a2 * b1 + b2)

def _rg_lru(x, w_a, b_a, w_x, b_x, lam):
    B, T, _ = x.shape
    xb = x.reshape(B, T, RG_BLOCKS, RG_BS)
    r = jax.nn.sigmoid(jnp.einsum('btnc,ncd->btnd', xb, w_a).reshape(B, T, D_RNN) + b_a)
    i = jax.nn.sigmoid(jnp.einsum('btnc,ncd->btnd', xb, w_x).reshape(B, T, D_RNN) + b_x)
    log_a = RG_C * r.astype(jnp.float32) * jax.nn.log_sigmoid(lam.astype(jnp.float32))
    a = jnp.exp(log_a)
    u = jnp.sqrt(-jnp.expm1(2.0 * log_a)) * (i * x).astype(jnp.float32)
    _, h = lax.associative_scan(_lin_combine, (a, u), axis=1)
    return h.astype(x.dtype)

def _mla_attention(q_nope, q_rope, k_nope, k_rope, v):
    B, T, H, _ = q_nope.shape
    nb = T // BLOCK
    scale = (QK_NOPE + QK_ROPE) ** -0.5
    key_pos = jnp.arange(T)

    def to_blocks(t):
        return jnp.swapaxes(t.reshape((B, nb, BLOCK) + t.shape[2:]), 0, 1)

    def one_block(args):
        qn, qr, bi = args
        q_pos = bi * BLOCK + jnp.arange(BLOCK)
        s = (jnp.einsum('bqhd,bkhd->bhqk', qn, k_nope)
             + jnp.einsum('bqhd,bkd->bhqk', qr, k_rope)).astype(jnp.float32) * scale
        s = jnp.where(key_pos[None, :] <= q_pos[:, None], s, -1e30)
        p = jax.nn.softmax(s, axis=-1).astype(v.dtype)
        return jnp.einsum('bhqk,bkhd->bqhd', p, v)

    o = lax.map(one_block, (to_blocks(q_nope), to_blocks(q_rope), jnp.arange(nb)))
    return jnp.swapaxes(o, 0, 1).reshape(B, T, H * V_DIM)

def _peer(x, w_q, keys1, keys2, u, v):
    B, T, D = x.shape
    half = PEER_QDIM // 2
    xc = x.reshape(B * T // BLOCK, BLOCK, D)

    def one_chunk(xt):
        q = (xt @ w_q).reshape(BLOCK, PEER_HEADS, PEER_QDIM)
        s1 = jnp.einsum('chd,nd->chn', q[..., :half], keys1).astype(jnp.float32)
        s2 = jnp.einsum('chd,nd->chn', q[..., half:], keys2).astype(jnp.float32)
        t1, i1 = lax.top_k(s1, PEER_TOPK)
        t2, i2 = lax.top_k(s2, PEER_TOPK)
        cand = (t1[..., :, None] + t2[..., None, :]).reshape(BLOCK, PEER_HEADS, PEER_TOPK * PEER_TOPK)
        cidx = (i1[..., :, None] * PEER_NKEYS + i2[..., None, :]).reshape(BLOCK, PEER_HEADS, PEER_TOPK * PEER_TOPK)
        ts, sel = lax.top_k(cand, PEER_TOPK)
        idx = jnp.take_along_axis(cidx, sel, axis=-1)
        g = jax.nn.softmax(ts, axis=-1)
        act = jax.nn.gelu(jnp.einsum('chkd,cd->chk', u[idx], xt))
        coef = (g * act.astype(jnp.float32)).astype(xt.dtype)
        return jnp.einsum('chk,chkd->cd', coef, v[idx])

    return lax.map(one_chunk, xc).reshape(B, T, D)

def first_inputs(seed: int = 0) -> dict:
    key = jax.random.key(seed)
    ks = jax.random.split(key, 26)
    f32 = jnp.float32
    L = DEPTH

    def nrm(k, shape, scale):
        return jax.random.normal(k, shape, f32) * scale

    def gain(k, shape):
        return 1.0 + 0.01 * jax.random.normal(k, shape, f32)

    a_c = jax.random.uniform(ks[10], (L, D_RNN), f32, 0.9, 0.999)
    s = a_c ** (1.0 / RG_C)
    rg_lambda = jnp.log(s) - jnp.log1p(-s)
    return {
        'x': nrm(ks[0], (BATCH, SEQ, D_MODEL), 1.0),
        'meta_tokens': nrm(ks[1], (N_META, D_MODEL), 1.0),
        'norm1_g': gain(ks[2], (L, D_MODEL)),
        'w_in': nrm(ks[3], (L, D_MODEL, D_IN), D_MODEL ** -0.5),
        'conv_w': nrm(ks[4], (L, CONV_W, D_RNN), CONV_W ** -0.5),
        'conv_b': nrm(ks[5], (L, D_RNN), 0.01),
        'rg_wa': nrm(ks[6], (L, RG_BLOCKS, RG_BS, RG_BS), RG_BS ** -0.5),
        'rg_ba': nrm(ks[7], (L, D_RNN), 0.01),
        'rg_wx': nrm(ks[8], (L, RG_BLOCKS, RG_BS, RG_BS), RG_BS ** -0.5),
        'rg_bx': nrm(ks[9], (L, D_RNN), 0.01),
        'rg_lambda': rg_lambda,
        'w_rnn_out': nrm(ks[11], (L, D_RNN, D_MODEL), D_RNN ** -0.5),
        'q_norm_g': gain(ks[12], (L, Q_LORA)),
        'w_uq': nrm(ks[13], (L, Q_LORA, MLA_HEADS * (QK_NOPE + QK_ROPE)), Q_LORA ** -0.5),
        'kv_norm_g': gain(ks[14], (L, KV_LORA)),
        'w_ukv': nrm(ks[15], (L, KV_LORA, MLA_HEADS * (QK_NOPE + V_DIM)), KV_LORA ** -0.5),
        'w_attn_out': nrm(ks[16], (L, MLA_HEADS * V_DIM, D_MODEL), (MLA_HEADS * V_DIM) ** -0.5),
        'w_out': nrm(ks[17], (L, D_MODEL, D_MODEL), D_MODEL ** -0.5),
        'norm2_g': gain(ks[18], (L, D_MODEL)),
        'peer_wq': nrm(ks[19], (L, D_MODEL, PEER_HEADS * PEER_QDIM), D_MODEL ** -0.5),
        'peer_keys1': nrm(ks[20], (L, PEER_NKEYS, PEER_QDIM // 2), (PEER_QDIM // 2) ** -0.5),
        'peer_keys2': nrm(ks[21], (L, PEER_NKEYS, PEER_QDIM // 2), (PEER_QDIM // 2) ** -0.5),
        'peer_u': nrm(ks[22], (L, PEER_EXPERTS, D_MODEL), D_MODEL ** -0.5),
        'peer_v': nrm(ks[23], (L, PEER_EXPERTS, D_MODEL), PEER_HEADS ** -0.5),
        'final_g': gain(ks[24], (D_MODEL,)),
    }

def first_block(x, meta_tokens, norm1_g, w_in, conv_w, conv_b, rg_wa, rg_ba, rg_wx, rg_bx, rg_lambda,
              w_rnn_out, q_norm_g, w_uq, kv_norm_g, w_ukv, w_attn_out, w_out, norm2_g,
              peer_wq, peer_keys1, peer_keys2, peer_u, peer_v, final_g):
    B, S, D = x.shape
    T = N_META + S
    Tp = -(-T // BLOCK) * BLOCK
    meta = jnp.broadcast_to(meta_tokens[None].astype(x.dtype), (B, N_META, D))
    h = jnp.concatenate([meta, x], axis=1)
    h = jnp.pad(h, ((0, 0), (0, Tp - T), (0, 0)))
    pos = jnp.arange(Tp, dtype=jnp.float32)
    for l in range(DEPTH):
        n1 = _rmsnorm(h, norm1_g[l])
        xr, gr, cq, ckv, kr, g_rnn, g_att = jnp.split(n1 @ w_in[l], IN_SPLITS, axis=-1)
        hr = _rg_lru(_causal_conv(xr, conv_w[l], conv_b[l]), rg_wa[l], rg_ba[l], rg_wx[l], rg_bx[l], rg_lambda[l])
        y_rnn = (hr * jax.nn.gelu(gr)) @ w_rnn_out[l]
        q = (_rmsnorm(cq, q_norm_g[l]) @ w_uq[l]).reshape(B, Tp, MLA_HEADS, QK_NOPE + QK_ROPE)
        kv = (_rmsnorm(ckv, kv_norm_g[l]) @ w_ukv[l]).reshape(B, Tp, MLA_HEADS, QK_NOPE + V_DIM)
        q_rope = _rope(q[..., QK_NOPE:], pos)
        k_rope = _rope(kr[:, :, None, :], pos)[:, :, 0, :]
        o = _mla_attention(q[..., :QK_NOPE], q_rope, kv[..., :QK_NOPE], k_rope, kv[..., QK_NOPE:])
        y_att = o @ w_attn_out[l]
        mixed = jax.nn.sigmoid(g_rnn) * y_rnn + jax.nn.sigmoid(g_att) * y_att
        h = h + mixed @ w_out[l]
        h = h + _peer(_rmsnorm(h, norm2_g[l]), peer_wq[l], peer_keys1[l], peer_keys2[l], peer_u[l], peer_v[l])
    h = _rmsnorm(h, final_g)
    return h[:, N_META:N_META + S]


DEPTH_2 = 2

N_A_LAYERS = DEPTH_2 // 2
N_B_LAYERS = DEPTH_2 - N_A_LAYERS
HEAD_DIM = 64
SB_HEADS = D_MODEL // HEAD_DIM
SWA_Q_HEADS = D_MODEL // HEAD_DIM
SWA_KV_HEADS = 4
SWA_GROUP = SWA_Q_HEADS // SWA_KV_HEADS
WINDOW = 128
Q_BLOCK = 128
D_FF = 2816
ROPE_THETA = 10000.0
RMS_EPS = 1e-6
FFN_RES_SCALE = 0.5


def rms_norm(x, g):
    xf = x.astype(jnp.float32)
    y = xf * lax.rsqrt(jnp.mean(xf * xf, axis=-1, keepdims=True) + RMS_EPS)
    return (y * g.astype(jnp.float32)).astype(x.dtype)

def swiglu(x, w_in, w_out):
    gate, up = jnp.split(x @ w_in, 2, axis=-1)
    return (jax.nn.silu(gate) * up) @ w_out

def rotary(x, pos):
    half = HEAD_DIM // 2
    inv_freq = ROPE_THETA ** (-jnp.arange(half, dtype=jnp.float32) / half)
    ang = pos.astype(jnp.float32)[:, None] * inv_freq[None, :]
    cos = jnp.cos(ang)[None, :, None, :]
    sin = jnp.sin(ang)[None, :, None, :]
    xf = x.astype(jnp.float32)
    x1, x2 = xf[..., :half], xf[..., half:]
    return jnp.concatenate([x1 * cos - x2 * sin, x2 * cos + x1 * sin], axis=-1).astype(x.dtype)

def stick_breaking_attention(q, k, v):
    B, S, H, Dh = q.shape
    nb = S // Q_BLOCK
    scale = Dh ** -0.5
    key_pos = jnp.arange(S)
    qb = q.reshape(B, nb, Q_BLOCK, H, Dh).transpose(1, 0, 2, 3, 4)

    def block(args):
        qi, i = args
        z = jnp.einsum('bqhd,bshd->bhqs', qi, k).astype(jnp.float32) * scale
        q_pos = i * Q_BLOCK + jnp.arange(Q_BLOCK)
        strict = key_pos[None, :] < q_pos[:, None]
        log_beta = jax.nn.log_sigmoid(z)
        log_1m_beta = jnp.where(strict, log_beta - z, 0.0)
        suffix = lax.cumsum(log_1m_beta, axis=3, reverse=True) - log_1m_beta
        w = jnp.where(strict, jnp.exp(log_beta + suffix), 0.0)
        return jnp.einsum('bhqs,bshd->bqhd', w.astype(v.dtype), v)

    out = lax.map(block, (qb, jnp.arange(nb)))
    return out.transpose(1, 0, 2, 3, 4).reshape(B, S, H, Dh)

def sliding_window_sink_attention(q, k, v, sinks):
    B, S, Hq, Dh = q.shape
    nb = S // WINDOW
    qb = q.reshape(B, nb, WINDOW, SWA_KV_HEADS, SWA_GROUP, Dh)

    def band(t):
        tb = t.reshape(B, nb, WINDOW, SWA_KV_HEADS, Dh)
        prev = jnp.pad(tb[:, :-1], ((0, 0), (1, 0), (0, 0), (0, 0), (0, 0)))
        return jnp.concatenate([prev, tb], axis=2)

    kb, vb = band(k), band(v)
    s = jnp.einsum('bnqhgd,bnkhd->bnhgqk', qb, kb).astype(jnp.float32) * (Dh ** -0.5)
    qi = jnp.arange(WINDOW)[:, None]
    ki = jnp.arange(2 * WINDOW)[None, :]
    diff = qi + WINDOW - ki
    in_window = (diff >= 0) & (diff < WINDOW)
    blk = jnp.arange(nb)[:, None, None]
    valid = in_window[None] & ((blk > 0) | (ki[None] >= WINDOW))
    s = jnp.where(valid[None, :, None, None], s, -jnp.inf)
    sink = jnp.broadcast_to(
        sinks.astype(jnp.float32).reshape(SWA_KV_HEADS, SWA_GROUP)[None, None, :, :, None, None],
        s.shape[:-1] + (1,))
    p = jax.nn.softmax(jnp.concatenate([s, sink], axis=-1), axis=-1)[..., :-1]
    out = jnp.einsum('bnhgqk,bnkhd->bnqhgd', p.astype(v.dtype), vb)
    return out.reshape(B, S, Hq, Dh)

def second_inputs(seed: int = 0) -> dict:
    key = jax.random.key(seed)
    ks = jax.random.split(key, 20)
    f32 = jnp.float32

    def w(k, shape, fan_in):
        return jax.random.normal(k, shape, f32) * (fan_in ** -0.5)

    def gain(k, shape):
        return 1.0 + 0.02 * jax.random.normal(k, shape, f32)

    return {
        "x": jax.random.normal(ks[0], (BATCH, SEQ, D_MODEL), f32),
        "ffn1_norm": gain(ks[1], (DEPTH_2, D_MODEL)),
        "ffn1_w_in": w(ks[2], (DEPTH_2, D_MODEL, 2 * D_FF), D_MODEL),
        "ffn1_w_out": w(ks[3], (DEPTH_2, D_FF, D_MODEL), D_FF),
        "mix_norm": gain(ks[4], (DEPTH_2, D_MODEL)),
        "ffn2_norm": gain(ks[5], (DEPTH_2, D_MODEL)),
        "ffn2_w_in": w(ks[6], (DEPTH_2, D_MODEL, 2 * D_FF), D_MODEL),
        "ffn2_w_out": w(ks[7], (DEPTH_2, D_FF, D_MODEL), D_FF),
        "sb_w_qkv": w(ks[8], (N_A_LAYERS, D_MODEL, 3 * SB_HEADS * HEAD_DIM), D_MODEL),
        "sb_w_o": w(ks[9], (N_A_LAYERS, SB_HEADS * HEAD_DIM, D_MODEL), SB_HEADS * HEAD_DIM),
        "kv_norm": gain(ks[10], (D_MODEL,)),
        "kv_w": w(ks[11], (D_MODEL, 2 * SWA_KV_HEADS * HEAD_DIM), D_MODEL),
        "swa_w_q": w(ks[12], (N_B_LAYERS, D_MODEL, SWA_Q_HEADS * HEAD_DIM), D_MODEL),
        "swa_sinks": 0.5 * jax.random.normal(ks[13], (N_B_LAYERS, SWA_Q_HEADS), f32),
        "swa_w_o": w(ks[14], (N_B_LAYERS, SWA_Q_HEADS * HEAD_DIM, D_MODEL), SWA_Q_HEADS * HEAD_DIM),
        "final_norm": gain(ks[15], (D_MODEL,)),
    }

def second_block(x, ffn1_norm, ffn1_w_in, ffn1_w_out, mix_norm, ffn2_norm, ffn2_w_in, ffn2_w_out,
              sb_w_qkv, sb_w_o, kv_norm, kv_w, swa_w_q, swa_sinks, swa_w_o, final_norm):
    B, S, D = x.shape
    pos = jnp.arange(S)
    h = x
    k_shared = None
    v_shared = None
    for layer in range(DEPTH_2):
        h = h + FFN_RES_SCALE * swiglu(rms_norm(h, ffn1_norm[layer]), ffn1_w_in[layer], ffn1_w_out[layer])
        hn = rms_norm(h, mix_norm[layer])
        if layer < N_A_LAYERS:
            qkv = (hn @ sb_w_qkv[layer]).reshape(B, S, 3, SB_HEADS, HEAD_DIM)
            o = stick_breaking_attention(qkv[:, :, 0], qkv[:, :, 1], qkv[:, :, 2])
            h = h + o.reshape(B, S, SB_HEADS * HEAD_DIM) @ sb_w_o[layer]
        else:
            j = layer - N_A_LAYERS
            q = rotary((hn @ swa_w_q[j]).reshape(B, S, SWA_Q_HEADS, HEAD_DIM), pos)
            o = sliding_window_sink_attention(q, k_shared, v_shared, swa_sinks[j])
            h = h + o.reshape(B, S, SWA_Q_HEADS * HEAD_DIM) @ swa_w_o[j]
        h = h + FFN_RES_SCALE * swiglu(rms_norm(h, ffn2_norm[layer]), ffn2_w_in[layer], ffn2_w_out[layer])
        if layer == N_A_LAYERS - 1:
            kv = (rms_norm(h, kv_norm) @ kv_w).reshape(B, S, 2, SWA_KV_HEADS, HEAD_DIM)
            k_shared = rotary(kv[:, :, 0], pos)
            v_shared = kv[:, :, 1]
    return rms_norm(h, final_norm)


def setup_inputs(seed=0):
    out = dict(first_inputs(seed))
    for name, value in second_inputs(seed + 1).items():
        if name != "x":
            out[name + "_2"] = value
    return out


def reference(
    x, meta_tokens, norm1_g, w_in, conv_w, conv_b, rg_wa, rg_ba, rg_wx, rg_bx, rg_lambda,
    w_rnn_out, q_norm_g, w_uq, kv_norm_g, w_ukv, w_attn_out, w_out, norm2_g, peer_wq,
    peer_keys1, peer_keys2, peer_u, peer_v, final_g, ffn1_norm_2, ffn1_w_in_2, ffn1_w_out_2,
    mix_norm_2, ffn2_norm_2, ffn2_w_in_2, ffn2_w_out_2, sb_w_qkv_2, sb_w_o_2, kv_norm_2, kv_w_2,
    swa_w_q_2, swa_sinks_2, swa_w_o_2, final_norm_2,
):
    x = first_block(
        x, meta_tokens, norm1_g, w_in, conv_w, conv_b, rg_wa, rg_ba, rg_wx, rg_bx, rg_lambda,
        w_rnn_out, q_norm_g, w_uq, kv_norm_g, w_ukv, w_attn_out, w_out, norm2_g, peer_wq,
        peer_keys1, peer_keys2, peer_u, peer_v, final_g,
    )
    return second_block(
        x, ffn1_norm_2, ffn1_w_in_2, ffn1_w_out_2, mix_norm_2, ffn2_norm_2, ffn2_w_in_2,
        ffn2_w_out_2, sb_w_qkv_2, sb_w_o_2, kv_norm_2, kv_w_2, swa_w_q_2, swa_sinks_2,
        swa_w_o_2, final_norm_2,
    )


_drawn_inputs = setup_inputs


def setup_inputs(seed=0):
    import zlib

    import numpy as np

    out = dict(_drawn_inputs(seed))
    spreads = {}
    factors = {'norm1_g': 3.878,
     'rg_ba': 8.0,
     'rg_bx': 7.241,
     'q_norm_g': 7.607,
     'kv_norm_g': 7.747,
     'final_g': 4.714,
     'ffn1_norm_2': 4.788,
     'mix_norm_2': 3.901,
     'ffn2_norm_2': 5.967,
     'kv_norm_2': 8.0,
     'swa_sinks_2': 53.056,
     'final_norm_2': 8.289}
    for name, (base, spread) in spreads.items():
        noise = np.random.default_rng([zlib.crc32(name.encode()), seed]).standard_normal(out[name].shape)
        drawn = base * np.exp(spread * noise) if base else spread * noise
        out[name] = __import__('jax').numpy.asarray(drawn.astype(out[name].dtype))
    for name, factor in factors.items():
        out[name] = (out[name] * factor).astype(out[name].dtype)
    return out
```

```python
import numpy as np
import concourse.bass as bass
from concourse import mybir
from contextlib import ExitStack

F32 = mybir.dt.float32
F32R = mybir.dt.float32r
U32 = mybir.dt.uint32
ALU = mybir.AluOpType
ACT = mybir.ActivationFunctionType
AX = mybir.AxisListType

P = 128
D = 1024
C = D // P
S = 256
META = 16
T = S + META
TP = 384
EPS = 1e-6
QL, KVL = 384, 256
H, NOPE, ROPE, VD = 16, 64, 32, 64
FF = 2816
NF = FF // P
FH = NF // 2
PH, NKEY, TOPK = 8, 128, 16
RAW = 4
TILE = P * 16
MLA_SCALE = float((NOPE + ROPE) ** -0.5)
SCALE = float(64 ** -0.5)
SA, SB = P + META, T
HEAD_AT = [0, 4, 1, 5, 2, 6, 3, 7, 8, 12, 9, 13, 10, 14, 11, 15]


def ring_order():
    stages = [("xr", 4, TILE, 4), ("lat", 3, TILE, 3), ("gates", 1, TILE, 8), ("gr", 4, TILE, 4),
              ("uq", 4, 12 * P, 8), ("uk", 1, TILE, 4), ("uv", 1, TILE, 3),
              ("mix", 16, TILE, 16), ("out1", 4, TILE, 0), ("pq", PH, TILE, 0)]
    def ffn(f):
        return [(f"ffi{f}", NF, TILE, NF), (f"ffo{f}", 2 * C, FH * P, 0)]
    stages += ffn(0) + [("qk", 8, TILE, 8), ("sbv", 4, TILE, 2), ("sbo", 4, TILE, 0)]
    stages += ffn(1) + [("kvk", 1, TILE, 1), ("kvv", 1, TILE, 1)]
    stages += ffn(2) + [("sq", 4, TILE, 4), ("swo", 4, TILE, 0)] + ffn(3)
    b = r = n = m = 0
    first, width, pair, res, count, order, part, pairs_of = {}, {}, {}, {}, {}, [], {}, {}
    for name, blocks, cols, pairs in stages:
        first[name], width[name], pair[name], res[name], count[name] = b, cols, r, n, blocks
        order.append(name)
        part[name], pairs_of[name] = m, pairs
        m += C if name.startswith("ffo") else 3 if name == "sbv" else 0
        b += blocks
        r += pairs
        n += 0 if pairs or name == "pq" else C
    return first, width, pair, res, count, order, part, pairs_of


FIRST, WIDTH, PAIR, RES, BLOCKS, ORDER, PART, PAIRS_OF = ring_order()
END = FIRST[ORDER[-1]] + BLOCKS[ORDER[-1]]

NORMS = [("n1", C), ("cq", QL // P), ("ckv", KVL // P), ("n2", C), ("final1", 0), ("f0", C), ("mix0", C),
         ("f1", C), ("kv", C), ("f2", C), ("mix1", C), ("f3", C), ("final2", 0)]
NORM = {name: j for j, (name, _) in enumerate(NORMS)}
SPLIT0 = {name: sum(c for _, c in NORMS[:j]) for j, (name, _) in enumerate(NORMS)}

VECS = [("n1", C), ("cq", 3), ("ckv", 2), ("cw0", C), ("cw1", C), ("cw2", C), ("cw3", C), ("cb", C), ("ba", C),
        ("bx", C), ("lam", C), ("n2", C), ("final1", C), ("f0", C), ("f1", C), ("f2", C), ("f3", C), ("mix0", C),
        ("mix1", C), ("kv", C), ("final2", C)]
NV = sum(n for _, n in VECS)


class Chain:

    def __init__(self, eng, sem):
        self.eng, self.sem, self.n, self.off = eng, sem, 0, 0

    def link(self, ins):
        self.n += 1
        ins.then_inc(self.sem, 1)
        self.eng.wait_ge(self.sem, self.n + self.off)

    def loop(self, count, per, body):
        start = self.n
        with self.eng.Fori(0, count) as i:
            self.off = i * per
            body(i)
        self.off = 0
        assert self.n - start == per, (self.n - start, per)
        self.n = start + per * count


def program(nc, w, out, stop):
    ctx = ExitStack()
    with ctx:
        def sb(name, cols, dt=F32):
            return ctx.enter_context(nc.sbuf_tensor(name, [P, cols], dt))

        def sem(name):
            return ctx.enter_context(nc.semaphore(name))

        raw = [sb(f"raw{s}", TILE) for s in range(RAW)]
        w_hi = [sb(f"w_hi{s}", TILE, F32R) for s in range(2)]
        w_lo = [sb(f"w_lo{s}", TILE, F32R) for s in range(2)]
        xn_hi, xn_lo = sb("xn_hi", C * T, F32R), sb("xn_lo", C * T, F32R)
        op_hi, op_lo = sb("op_hi", 24 * S, F32R), sb("op_lo", 24 * S, F32R)
        h_all = sb("h_all", C * T)
        arena = sb("arena", 11520)
        half = sb("half", C * S)
        tmp = sb("tmp", 1088)
        acc = [sb(f"acc{i}", T) for i in range(2)]
        tables = sb("tables", 1280 + 3 * P)
        keys = sb("keys", 2 * NKEY)
        small = sb("small", TOPK + H)
        picks = sb("picks", 4 * 2 * TOPK)
        vecs = sb("vecs", NV)
        lam_t = sb("lam_t", 8 * C)
        soft = sb("soft", 16)
        eps = sb("eps", 1)
        bank = [ctx.enter_context(nc.psum_tensor(f"bank{i}", [P, 512], F32)) for i in range(8)]

        def chunks(t, n, width, at=0):
            return t[:, at:at + n * width].rearrange("p (c t) -> p c t", t=width)

        h_t = chunks(h_all, C, T)
        hs = h_t[:, :, META:T]
        xf = [tmp[:, 0:T], tmp[:, T:2 * T]]
        sg = [tmp[:, 544:800], tmp[:, 800:1056]]
        xn = (chunks(xn_hi, C, T), chunks(xn_lo, C, T))
        xs = (xn[0][:, :, META:T], xn[1][:, :, META:T])
        conv = (chunks(op_hi, C, T), chunks(op_lo, C, T))
        y_rnn = (chunks(op_hi, C, S), chunks(op_lo, C, S))
        o_att = (chunks(op_hi, C, S, C * S), chunks(op_lo, C, S, C * S))
        mixed = (chunks(op_hi, C, S, 2 * C * S), chunks(op_lo, C, S, 2 * C * S))
        cqn = (chunks(op_hi, 3, S, 2 * C * S), chunks(op_lo, 3, S, 2 * C * S))
        ckvn = (chunks(op_hi, 2, TP, 2 * C * S + 3 * S), chunks(op_lo, 2, TP, 2 * C * S + 3 * S))
        inner = (chunks(op_hi, NF, S), chunks(op_lo, NF, S))
        xrp = chunks(arena, C, T + 3)
        a_t = chunks(arena, C, T)
        xc = chunks(arena, C, T, 2200)
        r_t = chunks(arena, C, T, 4400)
        i_t = chunks(arena, C, T, 6600)
        cqf = chunks(arena, 3, S, 8800)
        ckvf = chunks(arena, 2, T, 9568)
        kr_raw = arena[:, 10112:10384]
        kr_rot = arena[:, 10384:10656]
        gr = chunks(half, C, S)
        qh = chunks(arena, H, S)
        kh = chunks(arena, H, T, 4096)
        vt = chunks(arena, 3, D, 8448)
        probs = [half[:, 0:640], half[:, 640:1280]]
        pt = [half[:, 1280:1920], tmp[:, 0:640]]
        mla_mask = tables[:, 0:416]
        cos_t, sin_t = tables[:, 416:416 + T], tables[:, 416 + T:416 + 2 * T]
        ones, ident, tri = (tables[:, 1280 + P * i:1280 + P * (i + 1)] for i in range(3))
        sb_mask, swa_mask = tables[:, 0:384], tables[:, 384:768]
        cos2, sin2 = tables[:, 768:1024], tables[:, 1024:1280]
        pulled = [arena[:, 2 * D * n:2 * D * (n + 1)] for n in range(4)]
        x_tok = chunks(arena, 2, D, 8 * D)
        x_f = chunks(half, C, S)
        q_s = [half[:, 512 * n:512 * (n + 1)] for n in range(2)]
        product = half[:, D:2 * D]
        scratch = arena[:, 10 * D:11520]
        diag = [tmp[:, P * n:P * (n + 1)] for n in range(2)]
        y_tok = chunks(arena, 2, D)
        gw = [picks[:, 32 * n:32 * n + 32] for n in range(2)]
        expert = [picks[:, 64 + 32 * n:96 + 32 * n].bitcast(U32) for n in range(2)]
        xq = (xn[0][:, :, 0:S], xn[1][:, :, 0:S])
        qk = chunks(arena, 2 * C, S)
        sv = chunks(arena, 2, D, 4096)
        zm, az, sp_t, wt = ([arena[:, 6144 + 768 * a + 384 * n:6528 + 768 * a + 384 * n] for n in range(2)] for a in range(4))
        o2 = y_rnn
        k_sh, v_sh, k_raw = chunks(arena, 2, S), chunks(arena, 2, S, 512), chunks(arena, 2, S, 1024)
        q_sw, q_half = chunks(arena, C, S, 2048), chunks(arena, C, S, 4096)
        sw_p = [arena[:, 6144 + 386 * n:6530 + 386 * n] for n in range(2)]
        sw_pt = [arena[:, 7168 + 384 * n:7552 + 384 * n] for n in range(2)]
        V_AT, at = {}, 0
        for name, n in VECS:
            V_AT[name] = (at, n)
            at += n
        def vec(name, c):
            return vecs[:, V_AT[name][0] + c:V_AT[name][0] + c + 1]
        cl, ncl = lam_t[:, 0:C], lam_t[:, C:2 * C]

        names, at = {}, 0
        for name, n in (("s", NKEY), ("cand", 256), ("left", 256), ("hit", 256), ("t1", 16), ("t2", 16), ("i1", 16),
                        ("i2", 16), ("f1", 16), ("f2", 16), ("best", 16), ("at", 16), ("hi", 16), ("lo", 16),
                        ("fh", 16), ("fl", 16), ("e1", 16), ("e2", 16), ("neg", 1), ("sum", 1), ("rs", 1)):
            names[name] = (at, n)
            at += n
        top = {name: scratch[:, a:a + n] for name, (a, n) in names.items()}
        dots, coef = scratch[:, at:at + 4], scratch[:, at + 4:at + 12]
        assert at + 12 <= 1264

        landed = [sem(f"landed{s}") for s in range(RAW)]
        hi_done, lo_done = sem("hi_done"), sem("lo_done")
        even_done, odd_done = sem("even_done"), sem("odd_done")
        act_read, dve_read = sem("act_read"), sem("dve_read")
        res_done = sem("res_done")
        part_done = sem("part_done")
        h_new = sem("h_new")
        ss_in, ss_done = sem("ss_in"), sem("ss_done")
        sd_done, rs_done = sem("sd_done"), sem("rs_done")
        xf_done, xhi_done, xlo_done = sem("xf_done"), sem("xhi_done"), sem("xlo_done")
        const_in, x_in = sem("const_in"), sem("x_in")
        pads = sem("pads")
        lam_e, lam_c = sem("lam_e"), sem("lam_c")
        conv_done, conv_hi, conv_lo = sem("conv_done"), sem("conv_hi"), sem("conv_lo")
        lru_act, lru_dve = sem("lru_act"), sem("lru_dve")
        y_f, y_hi, y_lo = sem("y_f"), sem("y_hi"), sem("y_lo")
        kr_in, kr_ready = sem("kr_in"), sem("kr_ready")
        lat_read = sem("lat_read")
        sc_done, sc_masked, exp_done, p_ready = sem("sc_done"), sem("sc_masked"), sem("exp_done"), sem("p_ready")
        tr_done, ptx, pty, pv_done = sem("tr_done"), sem("ptx"), sem("pty"), sem("pv_done")
        o_done, o_hi, o_lo = sem("o_done"), sem("o_hi"), sem("o_lo")
        gate_done, mix_f, mix_hi, mix_lo = sem("gate_done"), sem("mix_f"), sem("mix_hi"), sem("mix_lo")
        rope_in = sem("rope_in")
        dve_step, act_step = sem("dve_step"), sem("act_step")
        xt_ps, xt_read = sem("xt_ps"), sem("xt_read")
        q_done, q_read, key_done = sem("q_done"), sem("q_read"), sem("key_done")
        top_max, top_exp, expert_in = sem("top_max"), sem("top_exp"), sem("expert_in")
        gathered = [sem(f"gathered{s}") for s in range(4)]
        dot_done, diag_done, row_used = sem("dot_done"), sem("diag_done"), sem("row_used")
        y_tok_act, y_tok_dve, y_back = sem("y_tok_act"), sem("y_tok_dve"), sem("y_back")
        peer_h, h_scaled = sem("peer_h"), sem("h_scaled")
        in_hi, in_lo = sem("in_hi"), sem("in_lo")
        z_done, z_mask, soft_in, sp_done = sem("z_done"), sem("z_mask"), sem("soft_in"), sem("sp_done")
        suf_done, arg_done, w_done, sbo_done = sem("suf_done"), sem("arg_done"), sem("w_done"), sem("sbo_done")
        sbo_hi, sbo_lo = sem("sbo_hi"), sem("sbo_lo")
        tables2_in = sem("tables2_in")
        k_rot, q_copied, q_rot = sem("k_rot"), sem("q_copied"), sem("q_rot")
        w_sc, w_mask, w_exp, w_p = sem("w_sc"), sem("w_mask"), sem("w_exp"), sem("w_p")
        w_tr, w_pt, w_pv, w_hi_o, w_lo_o = sem("w_tr"), sem("w_pt"), sem("w_pv"), sem("w_hi_o"), sem("w_lo_o")
        stored = sem("stored")

        def each(eng, n, body, tail=0):
            turns = (n - tail) // RAW
            if turns >= 2:
                with eng.Fori(0, turns) as i:
                    for u in range(RAW):
                        body(u, i)
            else:
                turns = 0
            for k in range(RAW * turns, n):
                body(k, 0)

        block = ctx.enter_context(nc.Block())

        @block.sync
        def _(sp):
            sp.dma_start(h_t[:, :, :], w["x_t"]).then_inc(x_in, 16)
            sp.dma_start(tables[:, 0:960], w["tables1"]).then_inc(const_in, 16)
            sp.dma_start(tables[:, 1280:], w["squares"]).then_inc(const_in, 16)
            sp.dma_start(keys[:, :], w["keys"]).then_inc(const_in, 16)
            sp.dma_start(small[:, :], w["small"]).then_inc(const_in, 16)
            sp.dma_start(vecs[:, :], w["vecs"]).then_inc(const_in, 16)

            def load(name):
                src, cols = w[name], WIDTH[name]

                def body(k, i):
                    b = FIRST[name] + k
                    if b >= RAW:
                        sp.wait_ge(lo_done, b - RAW + 1 + 4 * i)
                    at = src[bass.ds(k + 4 * i, 1), :, :] if not isinstance(i, int) else src[k:k + 1, :, :]
                    sp.dma_start(raw[b % RAW][:, 0:cols], at.rearrange("a p n -> (a p) n"))\
                      .then_inc(landed[b % RAW], 16)
                each(sp, BLOCKS[name], body)

            for name in ORDER[:ORDER.index(stop) + 1]:
                load(name)
                if name == "pq":
                    sp.wait_ge(h_new, RES["out1"] + C)
                    sp.dma_start(tables[:, 0:1280], w["tables2"]).then_inc(tables2_in, 16)
            sp.wait_ge(*((h_scaled, C) if stop == "pq" else (h_scaled, 2 * C) if stop == ORDER[-1] else (h_new, RES[stop] + C)))
            sp.dma_start(out, hs).then_inc(stored, 16)
            sp.wait_ge(stored, 16)

        @block.gpsimd
        def _(pool):
            pool.memset(eps[:, :], EPS).then_inc(pads, 1)
            pool.memset(xrp[:, :, 0:3], 0.0).then_inc(pads, 1)
            for part in ckvn:
                pool.memset(part[:, :, T:TP].bitcast(F32), 0.0).then_inc(pads, 1)

            pool.wait_ge(xt_read, 4)
            for n in range(2 * PH):
                pool.wait_ge(expert_in, n + 1)
                for s in range(TOPK):
                    q = TOPK * n + s
                    if q >= 4:
                        pool.wait_ge(row_used, q - 3)
                    at = TOPK * (n % 2) + s
                    pool.indirect_dma_start(pulled[s % 4], None, w["uv_rows"],
                                            bass.IndirectOffsetOnAxis(expert[n // 2 % 2][:, at:at + 1], 0))\
                        .then_inc(gathered[s % 4], 16)

        @block.tensor
        def _(pe):
            def mm3(o, wt, x, first=True, last=True):
                nc.tensor.matmul(o, wt[0], x[1], start=first, stop=False)
                nc.tensor.matmul(o, wt[0], x[0], start=False, stop=False)
                return nc.tensor.matmul(o, wt[1], x[0], start=False, stop=last)

            def tiles(b, n):
                v = w_hi[b % 2][:, n * P:(n + 1) * P], w_lo[b % 2][:, n * P:(n + 1) * P]
                return v

            def split_ready(name, k, i):
                pe.wait_ge(lo_done, FIRST[name] + k + 1 + 4 * i)

            def even_free(r, i=0):
                if r >= 2:
                    pe.wait_ge(act_read, r - 1 + 4 * i)

            def odd_free(r, i=0):
                if r >= 2:
                    pe.wait_ge(dve_read, r - 1 + 4 * i)

            def pair_stage(name, x, n=T, norm=None):
                def body(k, i):
                    b, r = FIRST[name] + k, PAIR[name] + k
                    split_ready(name, k, i)
                    for c, free, done in ((0, even_free, even_done), (1, odd_free, odd_done)):
                        free(r, i)
                        o = bank[2 * (r % 2) + c][:, 0:n]
                        for kk in range(C):
                            if norm and k == 0 and c == 0:
                                pe.wait_ge(xlo_done, SPLIT0[norm] + kk + 1)
                            last = mm3(o, tiles(b, C * c + kk), (x[0][:, kk, :], x[1][:, kk, :]), kk == 0, kk == C - 1)
                        last.then_inc(done, 1)
                each(pe, BLOCKS[name], body)

            def norm_sum(name, n):
                j = NORM[name]
                pe.wait_ge(ss_in, j + 1)
                nc.tensor.matmul(bank[6 + j % 2][:, 0:n], ones, acc[j % 2][:, 0:n], start=True, stop=True)\
                  .then_inc(ss_done, 1)

            def residual_stage(name, x, ready):
                def body(k, i):
                    b = FIRST[name] + k
                    split_ready(name, k, i)
                    for c in range(2):
                        n = RES[name] + 2 * k + c
                        if n >= 2:
                            pe.wait_ge(h_new, n - 1 + 8 * i)
                        for kk in range(C):
                            if k == 0 and c == 0:
                                pe.wait_ge(*ready(kk))
                            last = mm3(bank[4 + n % 2][:, 0:S], tiles(b, C * c + kk), (x[0][:, kk, :], x[1][:, kk, :]),
                                       kk == 0, kk == C - 1)
                        last.then_inc(res_done, 1)
                each(pe, BLOCKS[name], body)

            pe.wait_ge(const_in, 80)
            norm_sum("n1", T)
            pair_stage("xr", xn, norm="n1")
            pair_stage("lat", xn)
            split_ready("gates", 0, 0)
            for c in range(C):
                r = PAIR["gates"] + c
                pe.wait_ge(conv_lo, c + 1)
                x = conv[0][:, c, :], conv[1][:, c, :]
                even_free(r)
                mm3(bank[2 * (r % 2)][:, 0:T], tiles(FIRST["gates"], 2 * c), x).then_inc(even_done, 1)
                odd_free(r)
                mm3(bank[2 * (r % 2) + 1][:, 0:T], tiles(FIRST["gates"], 2 * c + 1), x).then_inc(odd_done, 1)
            norm_sum("cq", S)
            norm_sum("ckv", T)
            pair_stage("gr", xs, n=S)
            for k in range(4):
                split_ready("uq", k, 0)
                for c in range(4):
                    r = PAIR["uq"] + 2 * k + c // 2
                    (odd_free if c % 2 else even_free)(r)
                    for kk in range(3):
                        if k == 0 and c == 0:
                            pe.wait_ge(xlo_done, SPLIT0["cq"] + kk + 1)
                        last = mm3(bank[2 * (r % 2) + c % 2][:, 0:S], tiles(FIRST["uq"] + k, 3 * c + kk),
                                   (cqn[0][:, kk, :], cqn[1][:, kk, :]), kk == 0, kk == 2)
                    last.then_inc(odd_done if c % 2 else even_done, 1)
            split_ready("uk", 0, 0)
            for c in range(C):
                r = PAIR["uk"] + c // 2
                (odd_free if c % 2 else even_free)(r)
                for kk in range(2):
                    if c == 0:
                        pe.wait_ge(xlo_done, SPLIT0["ckv"] + kk + 1)
                    last = mm3(bank[2 * (r % 2) + c % 2][:, 0:T], tiles(FIRST["uk"], 2 * c + kk),
                               (ckvn[0][:, kk, 0:T], ckvn[1][:, kk, 0:T]), kk == 0, kk == 1)
                last.then_inc(odd_done if c % 2 else even_done, 1)
            split_ready("uv", 0, 0)
            wv = chunks(w_hi[FIRST["uv"] % 2], 2, D), chunks(w_lo[FIRST["uv"] % 2], 2, D)
            for t in range(3):
                r = PAIR["uv"] + t
                for hf, free, done in ((0, even_free, even_done), (1, odd_free, odd_done)):
                    free(r)
                    for kk in range(2):
                        last = mm3(bank[2 * (r % 2) + hf][:, :],
                                   (ckvn[0][:, kk, P * t:P * t + P], ckvn[1][:, kk, P * t:P * t + P]),
                                   (wv[0][:, kk, 512 * hf:512 * hf + 512], wv[1][:, kk, 512 * hf:512 * hf + 512]),
                                   kk == 0, kk == 1)
                    last.then_inc(done, 1)

            def scores(h):
                if h >= 2:
                    pe.wait_ge(exp_done, 2 * (h - 1))
                nc.tensor.matmul(bank[4 + h % 2][:, 0:SA], qh[0:96, h, 0:P], kh[0:96, h, 0:SA], start=True, stop=True)
                nc.tensor.matmul(bank[4 + h % 2][:, SA:SA + SB], qh[0:96, h, P:S], kh[0:96, h, 0:SB],
                                 start=True, stop=True).then_inc(sc_done, 1)

            def transposes(h):
                pe.wait_ge(p_ready, 2 * h + 2)
                if h >= 2:
                    pe.wait_ge(ptx, h - 1)
                    pe.wait_ge(pty, h - 1)
                p = probs[h % 2]
                for n, at in enumerate((0, 256, P, 256 + P)):
                    nc.tensor.transpose(bank[6 + h % 2][:, P * n:P * n + P], p[:, at:at + P], ident)
                nc.tensor.transpose(bank[2 + h % 2][:, 0:P], p[:, 512:640], ident).then_inc(tr_done, 1)

            def values(h):
                pe.wait_ge(ptx, h + 1)
                pe.wait_ge(pty, h + 1)
                if h >= 4 and h % 2 == 0:
                    pe.wait_ge(o_lo, h // 2 - 1)
                base = 64 * (h % 2)
                o = bank[h // 2 % 2]
                q = pt[h % 2]
                cols = slice(VD * h, VD * h + VD)
                nc.tensor.matmul(o[base:base + 64, 0:S], vt[:, 0, cols], q[:, 0:S], start=True, stop=False)
                nc.tensor.matmul(o[base:base + 64, 0:S], vt[:, 1, cols], q[:, S:2 * S], start=False, stop=False)
                nc.tensor.matmul(o[base:base + 64, P:S], vt[:, 2, cols], q[:, 2 * S:2 * S + P],
                                 start=False, stop=True).then_inc(pv_done, 1)

            r = PAIR["mix"]
            pe.wait_ge(act_read, r)
            pe.wait_ge(dve_read, r)
            pe.wait_ge(kr_ready, 1)
            pe.wait_ge(rope_in, 16)
            scores(0)
            scores(1)
            transposes(0)
            for h in range(H):
                if h + 2 < H:
                    scores(h + 2)
                if h + 1 < H:
                    transposes(h + 1)
                values(h)

            def mix(k, i):
                b, r = FIRST["mix"] + k, PAIR["mix"] + k
                split_ready("mix", k, i)
                even_free(r, i)
                for kk in range(C):
                    last = mm3(bank[2 * (r % 2)][:, 0:S], tiles(b, kk), (xs[0][:, kk, :], xs[1][:, kk, :]),
                               kk == 0, kk == C - 1)
                last.then_inc(even_done, 1)
                odd_free(r, i)
                y = y_rnn if k % 2 == 0 else o_att
                for kk in range(C):
                    if k == 0 and kk == 0:
                        pe.wait_ge(y_lo, 1)
                    last = mm3(bank[2 * (r % 2) + 1][:, 0:S], tiles(b, C + kk), (y[0][:, kk, :], y[1][:, kk, :]),
                               kk == 0, kk == C - 1)
                last.then_inc(odd_done, 1)
            pe.wait_ge(o_lo, C)
            each(pe, BLOCKS["mix"], mix)
            residual_stage("out1", mixed, lambda kk: (mix_lo, kk + 1))
            norm_sum("n2", S)

            pe.wait_ge(xlo_done, SPLIT0["n2"] + C)
            for t in range(2):
                for c in range(C):
                    n = 4 * t + c // 2
                    last = nc.tensor.transpose(bank[2 * t + c // 4][:, P * (c % 4):P * (c % 4 + 1)],
                                               x_f[:, c, P * t:P * t + P], ident)
                last.then_inc(xt_ps, 1)

            def query_part(h, n):
                c, kk = n // C, n % C
                if n == 0:
                    split_ready("pq", h, 0)
                    if h >= 2:
                        pe.wait_ge(q_read, h - 1)
                    elif h == 0:
                        pe.wait_ge(xt_read, 4)
                last = mm3(bank[h % 2][:, S * c:S * c + S], tiles(FIRST["pq"] + h, n),
                           (xq[0][:, kk, :], xq[1][:, kk, :]), kk == 0, kk == C - 1)
                if n == 2 * C - 1:
                    last.then_inc(q_done, 1)

            def key_scores(h):
                pe.wait_ge(q_read, h + 1)
                if h >= 2:
                    pe.wait_ge(expert_in, 2 * (h - 1))
                for t in range(2):
                    for c in range(2):
                        last = nc.tensor.matmul(bank[2 + h % 2][:, P * (2 * t + c):P * (2 * t + c + 1)],
                                                q_s[h % 2][:, S * c + P * t:S * c + P * t + P],
                                                keys[:, NKEY * c:NKEY * (c + 1)], start=True, stop=True)
                last.then_inc(key_done, 1)

            def add_rows(n, s, i):
                q = 16 * n + s
                pe.wait_ge(diag_done, q + 1 + (0 if isinstance(i, int) else 4 * i))
                for f in range(2):
                    last = nc.tensor.matmul(bank[4 + 2 * (n % 2) + f][:, :], diag[s % 2],
                                            pulled[s % 4][:, D + 512 * f:D + 512 * (f + 1)],
                                            start=(n < 2 and s == 0), stop=True, skip_group_check=True)
                last.then_inc(row_used, 1)

            for h in range(2):
                for n in range(2 * C):
                    query_part(h, n)
                key_scores(h)
            for n in range(2 * PH):
                h = n // 2 + 2
                if n % 2 == 0 and h < PH:
                    for s in range(TOPK):
                        query_part(h, s)
                        add_rows(n, s, 0)
                elif n == 1:
                    for s in range(TOPK):
                        if s == 12:
                            key_scores(h)
                        add_rows(n, s, 0)
                else:
                    with pe.Fori(0, 3) as i:
                        for s in range(4):
                            add_rows(n, s, i)
                    if h < PH:
                        key_scores(h)
                    for s in range(12, TOPK):
                        add_rows(n, s, 0)
            for t in range(2):
                pe.wait_ge(y_tok_act, t + 1)
                pe.wait_ge(y_tok_dve, t + 1)
                for c in range(C):
                    last = nc.tensor.transpose(bank[c // 2][:, S * (c % 2) + P * t:S * (c % 2) + P * t + P],
                                               y_tok[:, t, P * c:P * c + P], ident)
            last.then_inc(y_back, 1)
            pe.wait_ge(peer_h, C)
            norm_sum("final1", S)
            if stop == "pq":
                return

            def swiglu(f, norm):
                norm_sum(norm, S)
                pair_stage(f"ffi{f}", xq, n=S, norm=norm)

                def down(k, i):
                    name = f"ffo{f}"
                    c, part = k // 2, k % 2
                    n = RES[name] + c
                    split_ready(name, k, i)
                    if part == 0:
                        pe.wait_ge(h_new, n - 1 + 2 * i)
                    for t in range(FH):
                        kk = FH * part + t
                        if k < 2:
                            pe.wait_ge(in_lo, NF * f + kk + 1)
                        last = mm3(bank[4 + n % 2][:, 0:S], tiles(FIRST[name] + k, t),
                                   (inner[0][:, kk, :], inner[1][:, kk, :]), kk == 0, kk == NF - 1)
                    last.then_inc(res_done if part else part_done, 1)
                each(pe, BLOCKS[f"ffo{f}"], down)

            def values_stage(name, blocks, width, per):
                parts = width // 512 or 1
                cols = min(width, 512)
                for k in range(blocks):
                    split_ready(name, k, 0)
                    b = FIRST[name] + k
                    for t in range(2):
                        for hf in range(parts):
                            r, c = (PAIR[name] + t, hf) if parts == 2 else (PAIR[name], t)
                            if k == 0:
                                (odd_free if c else even_free)(r)
                            for kk in range(per):
                                ci = per * k + kk
                                at = width * kk + 512 * hf
                                last = mm3(bank[2 * (r % 2) + c][:, 0:cols],
                                           (xq[0][:, ci, P * t:P * t + P], xq[1][:, ci, P * t:P * t + P]),
                                           (w_hi[b % 2][:, at:at + cols], w_lo[b % 2][:, at:at + cols]),
                                           ci == 0, ci == C - 1)
                            if k == blocks - 1:
                                last.then_inc(odd_done if c else even_done, 1)
                    if k < blocks - 1:
                        last.then_inc(part_done, 1)

            swiglu(0, "f0")
            if stop == "ffo0":
                return
            norm_sum("mix0", S)
            pair_stage("qk", xq, n=S, norm="mix0")
            values_stage("sbv", 4, D, 2)

            pe.wait_ge(act_read, PAIR["sbv"] + 2)
            pe.wait_ge(dve_read, PAIR["sbv"] + 2)
            pe.wait_ge(tables2_in, 16)

            def logits(h):
                base, c = 64 * (h % 2), h // 2
                if h >= 2:
                    pe.wait_ge(z_mask, h - 1)
                rows_ = slice(base, base + 64)
                nc.tensor.matmul(bank[4 + h % 2][:, 0:S], qk[rows_, C + c, 0:P], qk[rows_, c, :], start=True, stop=True)
                nc.tensor.matmul(bank[4 + h % 2][:, S:S + P], qk[rows_, C + c, P:S], qk[rows_, c, P:S],
                                 start=True, stop=True).then_inc(z_done, 1)

            def suffixes(h):
                pe.wait_ge(sp_done, h + 1)
                if h >= 2:
                    pe.wait_ge(arg_done, h - 1)
                s_, o = sp_t[h % 2], bank[6 + h % 2]
                nc.tensor.matmul(o[:, 0:S], tri, s_[:, 0:S], start=True, stop=False)
                nc.tensor.matmul(o[:, P:S], ones, s_[:, S:S + P], start=False, stop=True)
                nc.tensor.matmul(o[:, S:S + P], tri, s_[:, S:S + P], start=True, stop=True).then_inc(suf_done, 1)

            def sb_values(h):
                pe.wait_ge(w_done, h + 1)
                if h >= 4 and h % 2 == 0:
                    pe.wait_ge(sbo_lo, h // 2 - 1)
                base, o = 64 * (h % 2), bank[h // 2 % 2]
                cols = slice(64 * h, 64 * h + 64)
                nc.tensor.matmul(o[base:base + 64, 0:S], sv[:, 0, cols], wt[h % 2][:, 0:S], start=True, stop=False)
                nc.tensor.matmul(o[base:base + 64, P:S], sv[:, 1, cols], wt[h % 2][:, S:S + P], start=False, stop=True)\
                  .then_inc(sbo_done, 1)

            logits(0)
            for h in range(H):
                if h + 1 < H:
                    logits(h + 1)
                suffixes(h)
                if h >= 1:
                    sb_values(h - 1)
            sb_values(H - 1)
            residual_stage("sbo", o2, lambda kk: (sbo_lo, kk + 1))
            if stop == "sbo":
                return
            swiglu(1, "f1")
            norm_sum("kv", S)
            pair_stage("kvk", xq, n=S, norm="kv")
            values_stage("kvv", 1, S, C)
            swiglu(2, "f2")
            norm_sum("mix1", S)
            pair_stage("sq", xq, n=S, norm="mix1")

            pe.wait_ge(q_rot, C)
            pe.wait_ge(k_rot, 1)

            def sw_scores(h):
                base, g = 64 * (h % 2), HEAD_AT[h] // 4
                if h >= 2:
                    pe.wait_ge(w_exp, 2 * (h - 1))
                rows_, o = slice(base, base + 64), bank[4 + h % 2]
                nc.tensor.matmul(o[:, 0:P], q_sw[rows_, h // 2, 0:P], k_sh[rows_, g // 2, 0:P], start=True, stop=True)
                nc.tensor.matmul(o[:, P + 1:P + 1 + S], q_sw[rows_, h // 2, P:S], k_sh[rows_, g // 2, :],
                                 start=True, stop=True).then_inc(w_sc, 1)

            def sw_transposes(h):
                pe.wait_ge(w_p, 2 * h + 2)
                if h >= 2:
                    pe.wait_ge(w_pt, h - 1)
                for n, at in enumerate((0, P + 1, 2 * P + 1)):
                    last = nc.tensor.transpose(bank[6 + h % 2][:, P * n:P * n + P], sw_p[h % 2][:, at:at + P], ident)
                last.then_inc(w_tr, 1)

            def sw_values(h):
                pe.wait_ge(w_pt, h + 1)
                if h >= 4 and h % 2 == 0:
                    pe.wait_ge(w_lo_o, h // 2 - 1)
                base, o, g = 64 * (h % 2), bank[h // 2 % 2], HEAD_AT[h] // 4
                cols = slice(64 * g, 64 * g + 64)
                q = sw_pt[h % 2]
                nc.tensor.matmul(o[base:base + 64, 0:S], v_sh[:, 0, cols], q[:, 0:S], start=True, stop=False)
                nc.tensor.matmul(o[base:base + 64, P:S], v_sh[:, 1, cols], q[:, S:S + P], start=False, stop=True)\
                  .then_inc(w_pv, 1)

            sw_scores(0)
            sw_scores(1)
            sw_transposes(0)
            for h in range(H):
                if h + 2 < H:
                    sw_scores(h + 2)
                if h + 1 < H:
                    sw_transposes(h + 1)
                sw_values(h)
            residual_stage("swo", o2, lambda kk: (w_lo_o, kk + 1))
            swiglu(3, "f3")
            norm_sum("final2", S)

        @block.scalar
        def _(act):
            chain = Chain(act, act_step)

            def round_block(b, cols, i=0):
                act.wait_ge(landed[b % RAW], 16 * (b // RAW + 1) + 16 * i)
                nc.scalar.activation(w_hi[b % 2][:, 0:cols], raw[b % RAW][:, 0:cols], ACT.Copy).then_inc(hi_done, 1)

            def done_of(name, k, i=0):
                if name.startswith("ffo"):
                    n = RES[name] + k // 2
                    return (res_done, n + 1 + 2 * i) if k % 2 else (part_done, PART[name] + k // 2 + 1 + 2 * i)
                if name == "sbv" and k < 3:
                    return part_done, PART[name] + k + 1
                if name == "pq":
                    return q_done, k + 1
                if PAIRS_OF[name] == 0:
                    return res_done, RES[name] + 2 * (k + 1) + 8 * i
                per = max(1, PAIRS_OF[name] // BLOCKS[name])
                if name == "sbv":
                    return odd_done, PAIR[name] + 2
                return odd_done, PAIR[name] + per * (k + 1) + 4 * per * i

            def round_next(name, k, i=0):
                b = FIRST[name] + k + 1
                if b >= END or (name == stop and k == BLOCKS[name] - 1 and isinstance(i, int)):
                    return
                nxt = name if k + 1 < BLOCKS[name] else ORDER[ORDER.index(name) + 1]
                if k >= 1 or not isinstance(i, int):
                    act.wait_ge(*done_of(name, k - 1, i))
                elif b >= 2:
                    prev = ORDER[ORDER.index(name) - 1]
                    act.wait_ge(*done_of(prev, BLOCKS[prev] - 1))
                round_block(b, WIDTH[nxt], i)

            def stage_start(name):
                prev = ORDER[ORDER.index(name) - 1]
                act.wait_ge(*done_of(prev, BLOCKS[prev] - 1))

            def pair_stage(name, body, start=True, tail=0):
                if start:
                    stage_start(name)

                def step(k, i):
                    round_next(name, k, i)
                    r = PAIR[name] + k
                    act.wait_ge(even_done, r + 1 + 4 * i)
                    body(k, i, bank[2 * (r % 2)])
                each(act, BLOCKS[name], step, tail)

            def residual_stage(name):
                stage_start(name)
                each(act, BLOCKS[name], lambda k, i: round_next(name, k, i), 1)

            def copy(o, x):
                return nc.scalar.activation(o, x, ACT.Copy)

            def norm_root(name, n, size):
                j = NORM[name]
                act.wait_ge(ss_done, j + 1)
                nc.scalar.activation(acc[j % 2][:, 0:n], bank[6 + j % 2][:, 0:n], ACT.Sqrt, bias=eps[:, :],
                                     scale=1.0 / size).then_inc(sd_done, 1)

            def part(t, at, n, i=0, step=0):
                return t[:, at:at + n] if isinstance(i, int) else t[:, bass.ds(at + step * i, n)]

            def norm_hi(name, n, dst, size=D):
                norm_root(name, n, size)
                for c in range(dict(NORMS)[name]):
                    act.wait_ge(xf_done, SPLIT0[name] + c + 1)
                    copy(dst[0][:, c, 0:n], xf[c % 2][:, 0:n]).then_inc(xhi_done, 1)

            act.wait_ge(const_in, 80)
            act.wait_ge(pads, 1)
            lam = vecs[:, V_AT["lam"][0]:V_AT["lam"][0] + C]
            chain.link(nc.scalar.activation(lam_t[:, 0:C], lam, ACT.Abs))
            nc.scalar.activation(lam_t[:, 0:C], lam_t[:, 0:C], ACT.Exp, scale=-1.0).then_inc(lam_e, 1)
            round_block(0, TILE)
            norm_hi("n1", T, xn)

            def xr(k, i, ps):
                if k == 0:
                    act.wait_ge(pads, 2)
                copy(xrp[:, 2 * k, 3:3 + T], ps[:, 0:T]).then_inc(act_read, 1)
            pair_stage("xr", xr, start=False)

            def lat(k, i, ps):
                dst = (ckvf[:, 0, :], kr_raw, cqf[:, 1, :])[k]
                src = ps[:, 0:T] if k < 2 else ps[:, META:T]
                copy(dst, src).then_inc(act_read, 1)
            pair_stage("lat", lat)
            for c in range(C):
                act.wait_ge(conv_done, c + 1)
                copy(conv[0][:, c, :], xc[:, c, :]).then_inc(conv_hi, 1)
            round_next("gates", 0)
            for c in range(C):
                r = PAIR["gates"] + c
                act.wait_ge(even_done, r + 1)
                nc.scalar.activation(r_t[:, c, :], bank[2 * (r % 2)][:, 0:T], ACT.Sigmoid, bias=vec("ba", c))\
                  .then_inc(act_read, 1)
            act.wait_ge(dve_read, PAIR["gr"])
            nc.scalar.activation(i_t[:, :, :], i_t[:, :, :], ACT.Sigmoid).then_inc(lru_act, 1)
            norm_hi("cq", S, cqn, QL)
            norm_hi("ckv", T, ckvn, KVL)

            def gr_in(k, i, ps):
                copy(gr[:, 2 * k, :], ps[:, 0:S]).then_inc(act_read, 1)
            act.wait_ge(lam_c, 1)
            act.wait_ge(act_read, PAIR["gr"])
            for c in range(C):
                nc.scalar.activation(a_t[:, c, :], r_t[:, c, :], ACT.Exp, scale=cl[:, c:c + 1]).then_inc(act_step, 1)
                chain.n += 1
            act.wait_ge(act_step, chain.n)
            for c in range(C):
                last = nc.scalar.activation(r_t[:, c, :], r_t[:, c, :], ACT.Tanh, scale=ncl[:, c:c + 1])
            last.then_inc(lru_act, 1)
            pair_stage("gr", gr_in)
            act.wait_ge(lru_dve, 1)
            nc.scalar.activation(r_t[:, :, :], r_t[:, :, :], ACT.Sqrt).then_inc(lru_act, 1)
            act.wait_ge(act_read, PAIR["uq"])
            act.wait_ge(dve_read, PAIR["uq"])
            nc.scalar.activation(gr[:, :, :], gr[:, :, :], ACT.Gelu_apprx_tanh).then_inc(lru_act, 1)
            round_next("uq", 0)
            act.wait_ge(y_f, 1)
            copy(y_rnn[0], gr[:, :, :]).then_inc(y_hi, 1)

            for k in range(4):
                if k:
                    round_next("uq", k)
                for c in (0, 2):
                    r = PAIR["uq"] + 2 * k + c // 2
                    act.wait_ge(even_done, r + 1)
                    ps = bank[2 * (r % 2)]
                    if k < 2:
                        m = 4 * k + c
                        copy(qh[0:64, 2 * m, :], ps[0:64, 0:S])
                        copy(qh[0:64, 2 * m + 1, :], ps[64:128, 0:S]).then_inc(act_read, 1)
                    else:
                        if r - PAIR["uq"] >= 5:
                            act.wait_ge(rope_in, 4 * (r - PAIR["uq"] - 4))
                        copy(sg[0], ps[:, 0:S]).then_inc(act_read, 1)
            round_next("uk", 0)
            for m in range(4):
                r = PAIR["uk"] + m
                act.wait_ge(even_done, r + 1)
                ps = bank[2 * (r % 2)]
                copy(kh[0:64, 4 * m, :], ps[0:64, 0:T])
                copy(kh[0:64, 4 * m + 1, :], ps[64:128, 0:T]).then_inc(act_read, 1)
            round_next("uv", 0)
            act.wait_ge(kr_ready, 1)
            for t in range(3):
                r = PAIR["uv"] + t
                act.wait_ge(even_done, r + 1)
                copy(vt[:, t, 0:512], bank[2 * (r % 2)][:, :]).then_inc(act_read, 1)
            stage_start("mix")


            def exps(h, i):
                u = h % 2
                p, s = probs[u], bank[4 + u]
                act.wait_ge(sc_masked, h + 1 + 4 * i)
                for t, (at, n, dst) in enumerate(((0, SA, 0), (SA, SB, 256))):
                    nc.scalar.activation(p[:, dst:dst + n], s[:, at:at + n], ACT.Exp, bias=soft[:, 2 * u + t:2 * u + t + 1],
                                         accum_out=soft[:, 4 + 2 * u + t:5 + 2 * u + t]).then_inc(exp_done, 1)

            def copy_pt(h, i):
                u = h % 2
                act.wait_ge(tr_done, h + 1 + 4 * i)
                if h >= 2:
                    act.wait_ge(pv_done, h - 1 + 4 * i)
                copy(pt[u][:, 0:512], bank[6 + u][:, :]).then_inc(ptx, 1)
                if h >= 2 and h % 2 == 0:
                    take_o(h // 2 - 1, i)

            def take_o(m, i):
                act.wait_ge(pv_done, 2 * m + 2 + 4 * i)
                copy(part(op_hi, C * S + S * m, S, i, 2 * S), bank[m % 2][:, 0:S]).then_inc(o_hi, 1)

            def turn(t, i):
                for u in range(4):
                    exps(4 * t + u, i)
                    if 4 * t + u >= 1:
                        copy_pt(4 * t + u - 1, i)
            act.wait_ge(y_lo, 1)
            turn(0, 0)
            with act.Fori(0, 3) as i:
                turn(1, i)
            copy_pt(H - 1, 0)
            take_o(H // 2 - 1, 0)

            def mix(k, i, ps):
                r = PAIR["mix"] + k
                act.wait_ge(dve_read, r - 1 + 4 * i)
                nc.scalar.activation(sg[k % 2], ps[:, 0:S], ACT.Sigmoid).then_inc(act_read, 1)
                if k % 2:
                    act.wait_ge(mix_f, k // 2 + 1 + 2 * i)
                    copy(part(op_hi, 2 * C * S + S * (k // 2), S, i, 2 * S), xf[1][:, 0:S]).then_inc(mix_hi, 1)
            pair_stage("mix", mix, start=False)
            residual_stage("out1")
            if stop == "out1":
                return

            def norm_hi_of(name, src, dst):
                norm_root(name, S, D)
                for c in range(C):
                    act.wait_ge(xf_done, SPLIT0[name] + c + 1)
                    copy(dst[0][:, c, :], src[:, c, :]).then_inc(xhi_done, 1)
            norm_hi_of("n2", x_f, xq)
            for t in range(2):
                act.wait_ge(xt_ps, t + 1)
                copy(x_tok[:, t, 0:512], bank[2 * t][:, :]).then_inc(xt_read, 1)

            def take_queries(h):
                act.wait_ge(q_done, h + 1)
                if h >= 2:
                    act.wait_ge(key_done, h - 1)
                elif h == 0:
                    act.wait_ge(xt_read, 4)
                copy(q_s[h % 2], bank[h % 2][:, :]).then_inc(q_read, 1)

            def expert_weights(n):
                h, t = n // 2, n % 2
                act.wait_ge(top_max, n + 1)
                nc.scalar.activation(gw[h % 2][:, 16 * t:16 * t + 16], top["best"], ACT.Exp, bias=top["neg"],
                                     accum_out=top["sum"]).then_inc(top_exp, 1)

            def coefficient(n, s, i):
                q = TOPK * n + s
                i4 = 0 if isinstance(i, int) else 4 * i
                act.wait_ge(dot_done, q + 1 + i4)
                chain.link(nc.scalar.activation(coef[:, s % 4:s % 4 + 1], dots[:, s % 4:s % 4 + 1], ACT.Gelu_apprx_tanh))
                at = TOPK * (n % 2) + s
                g = gw[n // 2 % 2]
                weight = g[:, at:at + 1] if isinstance(i, int) else g[:, bass.ds(at + i4, 1)]
                chain.link(nc.scalar.activation(coef[:, 4 + s % 4:5 + s % 4], coef[:, s % 4:s % 4 + 1], ACT.Copy, scale=weight))
                if q >= 2:
                    act.wait_ge(row_used, q - 1 + i4)
                nc.scalar.activation(diag[s % 2], ident, ACT.Copy, scale=coef[:, 4 + s % 4:5 + s % 4]).then_inc(diag_done, 1)

            round_next("pq", 0)
            take_queries(0)
            take_queries(1)
            round_next("pq", 1)
            expert_weights(0)
            for n in range(2 * PH):
                for s in range(8):
                    if n == 0 and s == 5:
                        expert_weights(1)
                    if n == 0:
                        coefficient(n, s, 0)
                if n > 0:
                    chain.loop(2, 8, lambda i: [coefficient(n, s, i) for s in range(4)])
                if n % 2 and n // 2 + 2 < PH:
                    take_queries(n // 2 + 2)
                if 1 <= n < 2 * PH - 2:
                    expert_weights(n + 2)
                for s in range(8, 16):
                    if n == 0 and s == 13:
                        expert_weights(2)
                    if n == 0:
                        coefficient(n, s, 0)
                if n > 0:
                    chain.loop(2, 8, lambda i: [coefficient(n, 8 + s, i) for s in range(4)])
                if n % 2 and n // 2 + 2 < PH:
                    round_next("pq", n // 2 + 2)
            for t in range(2):
                act.wait_ge(row_used, 16 * (2 * PH - 1 + t))
                copy(y_tok[:, t, 0:512], bank[4 + 2 * t][:, :]).then_inc(y_tok_act, 1)
            norm_root("final1", S, D)
            if stop == "pq":
                return

            def swiglu(f, norm, first=False):
                norm_hi(norm, S, xq)

                def up(k, i, ps):
                    r = PAIR[f"ffi{f}"] + k
                    act.wait_ge(dve_read, r - 1 + 4 * i)
                    nc.scalar.activation(sg[k % 2], ps[:, 0:S], ACT.Silu).then_inc(act_read, 1)
                    act.wait_ge(dve_read, r + 1 + 4 * i)
                    copy(part(op_hi, S * k, S, i, 4 * S), xf[k % 2][:, 0:S]).then_inc(in_hi, 1)
                pair_stage(f"ffi{f}", up)
                residual_stage(f"ffo{f}")

            swiglu(0, "f0")
            if stop == "ffo0":
                return
            norm_hi("mix0", S, xq)

            def qk_in(k, i, ps):
                copy(part(arena, 2 * S * k, S, i, 8 * S), ps[:, 0:S]).then_inc(act_read, 1)
            pair_stage("qk", qk_in)
            stage_start("sbv")
            for k in range(4):
                round_next("sbv", k)
            for t in range(2):
                r = PAIR["sbv"] + t
                act.wait_ge(even_done, r + 1)
                copy(sv[:, t, 0:512], bank[2 * (r % 2)][:, :]).then_inc(act_read, 1)

            def softplus(h, i):
                a = az[h % 2]
                act.wait_ge(z_mask, h + 1 + 4 * i)
                chain.link(nc.scalar.activation(a, a, ACT.Exp))
                nc.scalar.activation(a, a, ACT.Ln, bias=1.0).then_inc(soft_in, 1)

            def weights(h, i):
                act.wait_ge(arg_done, h + 1 + 4 * i)
                if h >= 2:
                    act.wait_ge(sbo_done, h - 1 + 4 * i)
                nc.scalar.activation(wt[h % 2], zm[h % 2], ACT.Exp).then_inc(w_done, 1)
                if h >= 3 and h % 2 == 1:
                    sb_take((h - 3) // 2, i)

            def sb_take(m, i):
                act.wait_ge(sbo_done, 2 * m + 2 + 4 * i)
                copy(part(op_hi, S * m, S, i, 2 * S), bank[m % 2][:, 0:S]).then_inc(sbo_hi, 1)

            def sb_turn(t, i):
                for u in range(4):
                    softplus(4 * t + u, i)
                    if 4 * t + u >= 1:
                        weights(4 * t + u - 1, i)
            sb_turn(0, 0)
            chain.loop(3, 4, lambda i: sb_turn(1, i))
            weights(H - 1, 0)
            sb_take(H // 2 - 1, 0)
            residual_stage("sbo")
            if stop == "sbo":
                return
            swiglu(1, "f1")
            norm_hi("kv", S, xq)
            pair_stage("kvk", lambda k, i, ps: copy(k_raw[:, 0, :], ps[:, 0:S]).then_inc(act_read, 1))
            pair_stage("kvv", lambda k, i, ps: copy(v_sh[:, 0, :], ps[:, 0:S]).then_inc(act_read, 1))
            swiglu(2, "f2")
            norm_hi("mix1", S, xq)
            pair_stage("sq", lambda k, i, ps: copy(q_sw[:, 2 * k, :], ps[:, 0:S]).then_inc(act_read, 1))
            act.wait_ge(act_read, PAIR["ffi3"])
            act.wait_ge(dve_read, PAIR["ffi3"])
            for dst, src in ((0, 32), (32, 0)):
                copy(q_half[dst:dst + 32, :, :], q_sw[src:src + 32, :, :]).then_inc(q_copied, 1)

            def sw_exps(h, i):
                u = h % 2
                act.wait_ge(w_mask, h + 1 + 4 * i)
                for t, (at, n) in enumerate(((0, P + 1), (P + 1, S + 1))):
                    nc.scalar.activation(sw_p[u][:, at:at + n], bank[4 + u][:, at:at + n], ACT.Exp,
                                         bias=soft[:, 2 * u + t:2 * u + t + 1],
                                         accum_out=soft[:, 4 + 2 * u + t:5 + 2 * u + t]).then_inc(w_exp, 1)

            def sw_copy(h, i):
                act.wait_ge(w_tr, h + 1 + 4 * i)
                if h >= 2:
                    act.wait_ge(w_pv, h - 1 + 4 * i)
                copy(sw_pt[h % 2], bank[6 + h % 2][:, 0:384]).then_inc(w_pt, 1)
                if h >= 2 and h % 2 == 0:
                    sw_take(h // 2 - 1, i)

            def sw_take(m, i):
                act.wait_ge(w_pv, 2 * m + 2 + 4 * i)
                copy(part(op_hi, S * m, S, i, 2 * S), bank[m % 2][:, 0:S]).then_inc(w_hi_o, 1)

            def sw_turn(t, i):
                for u in range(4):
                    sw_exps(4 * t + u, i)
                    if 4 * t + u >= 1:
                        sw_copy(4 * t + u - 1, i)
            sw_turn(0, 0)
            with act.Fori(0, 3) as i:
                sw_turn(1, i)
            sw_copy(H - 1, 0)
            sw_take(H // 2 - 1, 0)
            residual_stage("swo")
            swiglu(3, "f3")
            norm_root("final2", S, D)

        @block.vector
        def _(dve):
            v = nc.vector
            chain = Chain(dve, dve_step)
            link = chain.link

            def part(t, at, n, i=0, step=0):
                return t[:, at:at + n] if isinstance(i, int) else t[:, bass.ds(at + step * i, n)]

            def rest_of_block(b, cols, i=0):
                dve.wait_ge(hi_done, b + 1 + 4 * i)
                v.tensor_tensor(w_lo[b % 2][:, 0:cols], raw[b % RAW][:, 0:cols], w_hi[b % 2][:, 0:cols].bitcast(F32),
                                ALU.subtract).then_inc(lo_done, 1)

            def rest_next(name, k, i=0):
                b = FIRST[name] + k + 1
                if b >= END or (name == stop and k == BLOCKS[name] - 1 and isinstance(i, int)):
                    return
                nxt = name if k + 1 < BLOCKS[name] else ORDER[ORDER.index(name) + 1]
                rest_of_block(b, WIDTH[nxt], i)

            def pair_stage(name, body, tail=0):
                def step(k, i):
                    rest_next(name, k, i)
                    r = PAIR[name] + k
                    dve.wait_ge(odd_done, r + 1 + 4 * i)
                    body(k, i, bank[2 * (r % 2) + 1])
                each(dve, BLOCKS[name], step, tail)

            def square_sum(name, src, n, c, count):
                j = NORM[name]
                a = acc[j % 2][:, 0:n]
                if c == 0:
                    ins = v.tensor_tensor(a, src, src, ALU.mult)
                else:
                    link(v.tensor_tensor(xf[0][:, 0:n], src, src, ALU.mult))
                    ins = v.tensor_tensor(a, a, xf[0][:, 0:n], ALU.add)
                if c == count - 1:
                    ins.then_inc(ss_in, 1)
                else:
                    link(ins)

            def norm_apply(name, src, n, dst, full=None):
                def whole(c):
                    return xf[c % 2][:, 0:n] if full is None else full[:, c, :]
                j, s0 = NORM[name], SPLIT0[name]
                a = acc[j % 2][:, 0:n]
                dve.wait_ge(sd_done, j + 1)
                v.reciprocal(a, a).then_inc(rs_done, 1)
                dve.wait_ge(rs_done, j + 1)
                count = dict(NORMS)[name]

                def rest(c):
                    dve.wait_ge(xhi_done, s0 + c + 1)
                    v.tensor_tensor(dst[1][:, c, 0:n], whole(c), dst[0][:, c, 0:n].bitcast(F32), ALU.subtract)\
                     .then_inc(xlo_done, 1)
                for c in range(count):
                    if c >= 2:
                        rest(c - 2)
                        dve.wait_ge(xlo_done, s0 + c - 1)
                    v.scalar_tensor_tensor(whole(c), src[:, c, :], vec(name, c), a, ALU.mult, ALU.mult)\
                     .then_inc(xf_done, 1)
                for c in range(max(0, count - 2), count):
                    rest(c)
                dve.wait_ge(xlo_done, s0 + count)

            def residual_stage(name, norm, scale=1.0):
                j = NORM[norm]
                a = acc[j % 2][:, 0:S]
                link(v.memset(a, 0.0))
                blocks = BLOCKS[name] // C if BLOCKS[name] > C else 1
                per = 1 if blocks == 2 else 2

                def step(k, i):
                    rest_next(name, k, i)
                    if blocks == 2 and k % 2 == 0:
                        return
                    for c in range(per):
                        m = per * k + c if blocks == 1 else k // 2
                        n = RES[name] + m
                        dve.wait_ge(res_done, n + 1 + 2 * i)
                        hc = h_t[:, m, META:T] if isinstance(i, int) else h_all[:, bass.ds(T * m + META + 2 * T * i, S)]
                        v.scalar_tensor_tensor(hc, bank[4 + n % 2][:, 0:S], scale, hc, ALU.mult, ALU.add).then_inc(h_new, 1)
                        dve.wait_ge(h_new, n + 1 + 2 * i)
                        link(v.tensor_tensor(xf[0][:, 0:S], hc, hc, ALU.mult))
                        ins = v.tensor_tensor(a, a, xf[0][:, 0:S], ALU.add)
                        if m == C - 1 and isinstance(i, int):
                            ins.then_inc(ss_in, 1)
                        else:
                            link(ins)
                turns = 0 if blocks == 1 else (BLOCKS[name] - 1) // RAW
                if turns:
                    chain.loop(turns, 4, lambda i: [step(k, i) for k in range(RAW)])
                for k in range(RAW * turns, BLOCKS[name]):
                    step(k, 0)

            dve.wait_ge(const_in, 80)
            dve.wait_ge(lam_e, 1)
            e, z, z2, q, lam = (lam_t[:, C * n:C * n + C] for n in (0, 2, 3, 4, 5))
            link(v.tensor_scalar(z2, e, 2.0, None, ALU.add))
            link(v.reciprocal(z2, z2))
            link(v.tensor_tensor(z, z2, e, ALU.mult))
            link(v.tensor_tensor(z2, z, z, ALU.mult))
            link(v.tensor_scalar(q, z2, 1.0 / 17, None, ALU.mult))
            for n in (15, 13, 11, 9, 7, 5, 3):
                link(v.scalar_tensor_tensor(q, q, 1.0 / n, z2, ALU.add, ALU.mult))
            link(v.scalar_tensor_tensor(q, q, 1.0, z, ALU.add, ALU.mult))
            link(v.tensor_scalar(lam, vecs[:, V_AT["lam"][0]:V_AT["lam"][0] + C], -1.0, 0.0, ALU.mult, ALU.max))
            link(v.scalar_tensor_tensor(lam, q, 2.0, lam, ALU.mult, ALU.add))
            v.tensor_scalar(ncl, lam, 8.0, None, ALU.mult).then_inc(lam_c, 1)
            v.tensor_scalar(cl, lam, -8.0, None, ALU.mult).then_inc(lam_c, 1)

            dve.wait_ge(x_in, 16)
            for c in range(C):
                square_sum("n1", h_t[:, c, :], T, c, C)
            rest_of_block(0, TILE)
            norm_apply("n1", h_t, T, xn)

            def xr(k, i, ps):
                v.tensor_copy(xrp[:, 2 * k + 1, 3:3 + T], ps[:, 0:T]).then_inc(dve_read, 1)
            pair_stage("xr", xr)

            def lat(k, i, ps):
                dst = (ckvf[:, 1, :], cqf[:, 0, :], cqf[:, 2, :])[k]
                v.tensor_copy(dst, ps[:, 0:T] if k < 1 else ps[:, META:T]).then_inc(dve_read, 1)
            pair_stage("lat", lat)
            dve.wait_ge(dve_read, PAIR["gates"])
            dve.wait_ge(act_read, PAIR["gates"])
            for c in range(3):
                square_sum("cq", cqf[:, c, :], S, c, 3)
            for c in range(2):
                square_sum("ckv", ckvf[:, c, :], T, c, 2)
            dve.wait_ge(pads, 2)
            for c in range(C):
                y = xc[:, c, :]
                link(v.tensor_scalar(y, xrp[:, c, 0:T], vec("cw0", c), vec("cb", c), ALU.mult, ALU.add))
                for t in (1, 2, 3):
                    ins = v.scalar_tensor_tensor(y, xrp[:, c, t:t + T], vec(f"cw{t}", c), y, ALU.mult, ALU.add)
                    ins.then_inc(conv_done, 1) if t == 3 else link(ins)
                if c >= 1:
                    conv_rest(dve, v, c - 1, conv, xc, conv_hi, conv_lo)
            conv_rest(dve, v, C - 1, conv, xc, conv_hi, conv_lo)
            rest_next("gates", 0)
            for c in range(C):
                r = PAIR["gates"] + c
                dve.wait_ge(odd_done, r + 1)
                v.tensor_scalar(i_t[:, c, :], bank[2 * (r % 2) + 1][:, 0:T], vec("bx", c), None, ALU.add)\
                 .then_inc(dve_read, 1)
            dve.wait_ge(pads, 4)
            norm_apply("cq", cqf, S, cqn)
            norm_apply("ckv", ckvf, T, ckvn)
            link(v.tensor_tensor(kr_rot[0:32, :], kr_raw[0:32, :], cos_t[0:32, :], ALU.mult))
            link(v.tensor_tensor(xf[0][0:32, :], kr_raw[32:64, :], sin_t[32:64, :], ALU.mult))
            link(v.tensor_tensor(kr_rot[0:32, :], kr_rot[0:32, :], xf[0][0:32, :], ALU.add))
            dve.wait_ge(lru_act, 1)
            link(v.tensor_tensor(i_t[:, :, :], i_t[:, :, :], xc[:, :, :], ALU.mult))
            dve.wait_ge(lru_act, 2)
            link(v.tensor_tensor(xc[:, :, :], a_t[:, :, :], a_t[:, :, :], ALU.mult))
            v.scalar_tensor_tensor(r_t[:, :, :], xc[:, :, :], 1.0, r_t[:, :, :], ALU.add, ALU.mult).then_inc(lru_dve, 1)

            def gr_in(k, i, ps):
                v.tensor_copy(gr[:, 2 * k + 1, :], ps[:, 0:S]).then_inc(dve_read, 1)
            pair_stage("gr", gr_in)
            dve.wait_ge(lru_act, 3)
            link(v.tensor_tensor(i_t[:, :, :], i_t[:, :, :], r_t[:, :, :], ALU.mult))
            for c in range(C):
                ins = v.tensor_tensor_scan(xc[:, c, :], a_t[:, c, :], i_t[:, c, :], 0.0, ALU.mult, ALU.add)
            link(ins)
            dve.wait_ge(lru_act, 4)
            v.tensor_tensor(gr[:, :, :], gr[:, :, :], xc[:, :, META:T], ALU.mult).then_inc(y_f, 1)
            dve.wait_ge(y_hi, 1)
            v.tensor_tensor(y_rnn[1], gr[:, :, :], y_rnn[0].bitcast(F32), ALU.subtract).then_inc(y_lo, 1)
            for g in range(H // 8):
                ins = v.tensor_copy(kh[64:96, 8 * g:8 * g + 8, :],
                                    kr_rot[0:32, :].unsqueeze(1).to_broadcast([32, 8, T]))
            ins.then_inc(kr_ready, 1)

            for k in range(4):
                if k:
                    rest_next("uq", k)
                else:
                    rest_next("uq", 0)
                for c in (1, 3):
                    r = PAIR["uq"] + 2 * k + c // 2
                    dve.wait_ge(odd_done, r + 1)
                    ps = bank[2 * (r % 2) + 1]
                    if k < 2:
                        m = 4 * k + c
                        v.tensor_copy(qh[0:64, 2 * m, :], ps[0:64, 0:S])
                        v.tensor_copy(qh[0:64, 2 * m + 1, :], ps[64:128, 0:S]).then_inc(dve_read, 1)
                    else:
                        g = r - PAIR["uq"] - 4
                        v.tensor_tensor(sg[1], ps[:, 0:S], sin_t[:, META:T], ALU.mult).then_inc(dve_read, 1)
                        dve.wait_ge(act_read, r + 1)
                        link(v.tensor_tensor(xf[0][:, 0:S], sg[0], cos_t[:, META:T], ALU.mult))
                        dve.wait_ge(dve_read, r + 1)
                        for a in range(4):
                            rows = slice(32 * a, 32 * a + 32)
                            v.tensor_tensor(qh[64:96, 4 * g + a, :], xf[0][rows, 0:S], sg[1][rows, :], ALU.add)\
                             .then_inc(rope_in, 1)
                        dve.wait_ge(rope_in, 4 * g + 4)
            rest_next("uk", 0)
            for m in range(4):
                r = PAIR["uk"] + m
                dve.wait_ge(odd_done, r + 1)
                ps = bank[2 * (r % 2) + 1]
                v.tensor_copy(kh[0:64, 4 * m + 2, :], ps[0:64, 0:T])
                v.tensor_copy(kh[0:64, 4 * m + 3, :], ps[64:128, 0:T]).then_inc(dve_read, 1)
            for t in range(3):
                r = PAIR["uv"] + t
                dve.wait_ge(odd_done, r + 1)
                v.tensor_copy(vt[:, t, 512:1024], bank[2 * (r % 2) + 1][:, :]).then_inc(dve_read, 1)
            rest_next("uv", 0)
            dve.wait_ge(y_lo, 1)
            for p in probs:
                link(v.memset(p[:, SA:S], 0.0))
                link(v.memset(p[:, S + SB:640], 0.0))

            def mask(h, i):
                u = h % 2
                s = bank[4 + u]
                dve.wait_ge(sc_done, h + 1 + 4 * i)
                link(v.scalar_tensor_tensor(s[:, 0:416], s[:, 0:416], MLA_SCALE, mla_mask, ALU.mult, ALU.add))
                link(v.tensor_reduce(soft[:, 2 * u:2 * u + 1], s[:, 0:SA], AX.X, ALU.max, negate=True))
                v.tensor_reduce(soft[:, 2 * u + 1:2 * u + 2], s[:, SA:SA + SB], AX.X, ALU.max, negate=True)\
                 .then_inc(sc_masked, 1)

            def normalise(h, i):
                u = h % 2
                p = probs[u]
                dve.wait_ge(exp_done, 2 * h + 2 + 8 * i)
                link(v.reciprocal(soft[:, 8 + 2 * u:10 + 2 * u], soft[:, 4 + 2 * u:6 + 2 * u]))
                v.tensor_scalar(p[:, 0:SA], p[:, 0:SA], soft[:, 8 + 2 * u:9 + 2 * u], None, ALU.mult).then_inc(p_ready, 1)
                v.tensor_scalar(p[:, 256:256 + SB], p[:, 256:256 + SB], soft[:, 9 + 2 * u:10 + 2 * u], None, ALU.mult)\
                 .then_inc(p_ready, 1)
                dve.wait_ge(tr_done, h + 1 + 4 * i)
                if h >= 2:
                    dve.wait_ge(pv_done, h - 1 + 4 * i)
                v.tensor_copy(pt[u][:, 512:640], bank[2 + u][:, 0:P]).then_inc(pty, 1)
                if h >= 2 and h % 2 == 0:
                    rest_o(h // 2 - 1, i)

            def rest_o(m, i):
                dve.wait_ge(o_hi, m + 1 + 2 * i)
                v.tensor_tensor(part(op_lo, C * S + S * m, S, i, 2 * S), bank[m % 2][:, 0:S],
                                part(op_hi, C * S + S * m, S, i, 2 * S).bitcast(F32), ALU.subtract).then_inc(o_lo, 1)

            def turn(t, i):
                for u in range(4):
                    mask(4 * t + u, i)
                    if 4 * t + u >= 1:
                        normalise(4 * t + u - 1, i)
            turn_links = 12
            turn(0, 0)
            chain.loop(3, turn_links, lambda i: turn(1, i))
            normalise(H - 1, 0)
            rest_o(H // 2 - 1, 0)

            def mix(k, i, ps):
                r = PAIR["mix"] + k
                dve.wait_ge(act_read, r + 1 + 4 * i)
                if k % 2 == 0:
                    v.tensor_tensor(xf[0][:, 0:S], sg[0], ps[:, 0:S], ALU.mult).then_inc(dve_read, 1)
                    return
                v.tensor_tensor(acc[0][:, 0:S], sg[1], ps[:, 0:S], ALU.mult).then_inc(dve_read, 1)
                dve.wait_ge(dve_read, r + 1 + 4 * i)
                v.tensor_tensor(xf[1][:, 0:S], xf[0][:, 0:S], acc[0][:, 0:S], ALU.add).then_inc(mix_f, 1)
                dve.wait_ge(mix_hi, k // 2 + 1 + 2 * i)
                at = 2 * C * S + S * (k // 2)
                v.tensor_tensor(part(op_lo, at, S, i, 2 * S), xf[1][:, 0:S], part(op_hi, at, S, i, 2 * S).bitcast(F32),
                                ALU.subtract).then_inc(mix_lo, 1)
                dve.wait_ge(mix_lo, k // 2 + 1 + 2 * i)
            pair_stage("mix", mix)
            residual_stage("out1", "n2")
            if stop == "out1":
                return

            norm_apply("n2", hs, S, xq, full=x_f)
            for t in range(2):
                dve.wait_ge(xt_ps, t + 1)
                v.tensor_copy(x_tok[:, t, 512:D], bank[2 * t + 1][:, :]).then_inc(xt_read, 1)

            def top16(values, n, best, index, left):
                link(v.max(best[:, 0:8], values))
                yield
                link(v.max_index(index[:, 0:8], best[:, 0:8], values))
                yield
                link(v.match_replace(left, best[:, 0:8], values, -3.0e38))
                yield
                link(v.max(best[:, 8:16], left))
                yield
                link(v.max_index(index[:, 8:16], best[:, 8:16], left))
                yield

            iota = small[:, 0:TOPK]

            def pick(dst, which, values):
                hit = top["hit"].rearrange("p (k a) -> p k a", a=TOPK)
                link(v.tensor_tensor(hit, which.unsqueeze(2).to_broadcast([P, TOPK, TOPK]),
                                     iota.unsqueeze(1).to_broadcast([P, TOPK, TOPK]), ALU.is_equal))
                yield
                link(v.tensor_tensor(hit, hit, values.unsqueeze(1).to_broadcast([P, TOPK, TOPK]), ALU.mult))
                yield
                link(v.tensor_reduce(dst, hit, AX.X, ALU.add))
                yield

            def experts(n):
                h, t = n // 2, n % 2
                ps = bank[2 + h % 2]
                dve.wait_ge(key_done, h + 1)
                for c, (tv, ti, tf) in enumerate((("t1", "i1", "f1"), ("t2", "i2", "f2"))):
                    yield from top16(ps[:, P * (2 * t + c):P * (2 * t + c + 1)], NKEY, top[tv], top[ti].bitcast(U32), top["s"])
                    link(v.tensor_copy(top[tf], top[ti].bitcast(U32)))
                    yield
                cand = top["cand"].rearrange("p (a b) -> p a b", b=TOPK)
                link(v.tensor_tensor(cand, top["t1"].unsqueeze(2).to_broadcast([P, TOPK, TOPK]),
                                     top["t2"].unsqueeze(1).to_broadcast([P, TOPK, TOPK]), ALU.add))
                yield
                if n >= 1:
                    dve.wait_ge(top_exp, n)
                yield from top16(top["cand"], 256, top["best"], top["at"].bitcast(U32), top["left"])
                v.tensor_scalar(top["neg"], top["best"][:, 0:1], -1.0, None, ALU.mult).then_inc(top_max, 1)
                for to, op, by, f in (("hi", ALU.logical_shift_right, 4, "fh"), ("lo", ALU.bitwise_and, 15, "fl")):
                    link(v.tensor_scalar(top[to].bitcast(U32), top["at"].bitcast(U32), by, None, op))
                    yield
                    link(v.tensor_copy(top[f], top[to].bitcast(U32)))
                    yield
                yield from pick(top["e1"], top["fh"], top["f1"])
                yield from pick(top["e2"], top["fl"], top["f2"])
                if n >= 4:
                    dve.wait_ge(row_used, TOPK * (n - 3))
                dve.wait_ge(top_exp, n + 1)
                link(v.reciprocal(top["rs"], top["sum"]))
                yield
                g = gw[h % 2][:, 16 * t:16 * t + 16]
                link(v.tensor_scalar(g, g, top["rs"], None, ALU.mult))
                yield
                v.scalar_tensor_tensor(expert[h % 2][:, 16 * t:16 * t + 16], top["e1"], float(NKEY), top["e2"],
                                       ALU.mult, ALU.add).then_inc(expert_in, 1)
                dve.wait_ge(expert_in, n + 1)

            def dot(n, s, i):
                q = 16 * n + s
                i4 = 0 if isinstance(i, int) else 4 * i
                turns = q // 4 + 1
                dve.wait_ge(gathered[s % 4], 16 * turns + (0 if isinstance(i, int) else 16 * i))
                if q >= 1:
                    dve.wait_ge(dot_done, q + i4)
                v.tensor_tensor_reduce(out=product, in0=pulled[s % 4][:, 0:D], in1=x_tok[:, n % 2, :], scale=1.0, scalar=0.0,
                                       op0=ALU.mult, op1=ALU.add, accum_out=dots[:, s % 4:s % 4 + 1]).then_inc(dot_done, 1)

            def advance(steps, count):
                for _ in range(count):
                    next(steps, None)

            rest_next("pq", 0)
            advance(experts(0), 40)
            rest_next("pq", 1)
            for n in range(2 * PH):
                if n < 2 * PH - 2:
                    steps = experts(1 if n == 0 else n + 2)
                    for s in range(TOPK):
                        if n == 0 and s == 8:
                            steps = experts(2)
                        dot(n, s, 0)
                        advance(steps, 5 if n == 0 else 3)
                else:
                    with dve.Fori(0, 4) as i:
                        for s in range(4):
                            dot(n, s, i)
                if n % 2 and n // 2 + 2 < PH:
                    rest_next("pq", n // 2 + 2)
            for t in range(2):
                dve.wait_ge(row_used, 16 * (2 * PH - 1 + t))
                v.tensor_copy(y_tok[:, t, 512:D], bank[5 + 2 * t][:, :]).then_inc(y_tok_dve, 1)
            dve.wait_ge(y_back, 1)
            a = acc[NORM["final1"] % 2][:, 0:S]
            link(v.memset(a, 0.0))
            for c in range(C):
                hc = hs[:, c, :]
                v.tensor_tensor(hc, hc, bank[c // 2][:, S * (c % 2):S * (c % 2) + S], ALU.add).then_inc(peer_h, 1)
                dve.wait_ge(peer_h, c + 1)
                link(v.tensor_tensor(xf[0][:, 0:S], hc, hc, ALU.mult))
                ins = v.tensor_tensor(a, a, xf[0][:, 0:S], ALU.add)
                ins.then_inc(ss_in, 1) if c == C - 1 else link(ins)
            def norm_in_place(name):
                j = NORM[name]
                a = acc[j % 2][:, 0:S]
                dve.wait_ge(sd_done, j + 1)
                v.reciprocal(a, a).then_inc(rs_done, 1)
                dve.wait_ge(rs_done, j + 1)
                for c in range(C):
                    v.scalar_tensor_tensor(hs[:, c, :], hs[:, c, :], vec(name, c), a, ALU.mult, ALU.mult).then_inc(h_scaled, 1)

            norm_in_place("final1")
            if stop == "pq":
                return
            for c in range(C):
                dve.wait_ge(h_scaled, c + 1)
                square_sum("f0", hs[:, c, :], S, c, C)

            def swiglu(f, norm, following):
                norm_apply(norm, hs, S, xq)

                def up(k, i, ps):
                    r, n = PAIR[f"ffi{f}"] + k, NF * f + k
                    dve.wait_ge(act_read, r + 1 + 4 * i)
                    v.tensor_tensor(xf[k % 2][:, 0:S], sg[k % 2], ps[:, 0:S], ALU.mult).then_inc(dve_read, 1)
                    dve.wait_ge(in_hi, n + 1 + 4 * i)
                    v.tensor_tensor(part(op_lo, S * k, S, i, 4 * S), xf[k % 2][:, 0:S],
                                    part(op_hi, S * k, S, i, 4 * S).bitcast(F32), ALU.subtract).then_inc(in_lo, 1)
                    dve.wait_ge(in_lo, n + 1 + 4 * i)
                pair_stage(f"ffi{f}", up)
                residual_stage(f"ffo{f}", following, 0.5)

            swiglu(0, "f0", "mix0")
            if stop == "ffo0":
                return
            norm_apply("mix0", hs, S, xq)

            def qk_in(k, i, ps):
                v.tensor_scalar(part(arena, 2 * S * k + S, S, i, 8 * S), ps[:, 0:S], 1.0, None, ALU.mult).then_inc(dve_read, 1)
            pair_stage("qk", qk_in)
            for k in range(4):
                rest_next("sbv", k)
            for t in range(2):
                r = PAIR["sbv"] + t
                dve.wait_ge(odd_done, r + 1)
                v.tensor_copy(sv[:, t, 512:D], bank[2 * (r % 2) + 1][:, :]).then_inc(dve_read, 1)
            dve.wait_ge(tables2_in, 16)

            def masked_logits(h, i):
                u = h % 2
                dve.wait_ge(z_done, h + 1 + 4 * i)
                if h >= 2:
                    dve.wait_ge(w_done, h - 1 + 4 * i)
                link(v.scalar_tensor_tensor(zm[u], bank[4 + u][:, 0:384], SCALE, sb_mask, ALU.mult, ALU.add))
                if h >= 2:
                    dve.wait_ge(sp_done, h - 1 + 4 * i)
                v.scalar_tensor_tensor(az[u], zm[u], -1.0, zm[u], ALU.mult, ALU.min).then_inc(z_mask, 1)

            def exponents(h, i):
                u = h % 2
                dve.wait_ge(suf_done, h + 1 + 4 * i)
                v.tensor_tensor(zm[u], zm[u], bank[6 + u][:, 0:384], ALU.subtract).then_inc(arg_done, 1)

            def softplus(h, i):
                u = h % 2
                dve.wait_ge(soft_in, h + 1 + 4 * i)
                v.scalar_tensor_tensor(sp_t[u], zm[u], 0.0, az[u], ALU.max, ALU.add).then_inc(sp_done, 1)

            def sb_rest(m, i):
                dve.wait_ge(sbo_hi, m + 1 + 2 * i)
                v.tensor_tensor(part(op_lo, S * m, S, i, 2 * S), bank[m % 2][:, 0:S],
                                part(op_hi, S * m, S, i, 2 * S).bitcast(F32), ALU.subtract).then_inc(sbo_lo, 1)

            def sb_head(h, i):
                masked_logits(h, i)
                if h >= 1:
                    exponents(h - 1, i)
                softplus(h, i)
                if h >= 4 and h % 2 == 0:
                    sb_rest((h - 4) // 2, i)

            for h in range(4):
                sb_head(h, 0)
            chain.loop(3, 4, lambda i: [sb_head(4 + u, i) for u in range(4)])
            exponents(H - 1, 0)
            sb_rest(H // 2 - 2, 0)
            sb_rest(H // 2 - 1, 0)
            residual_stage("sbo", "f1")
            if stop == "sbo":
                return
            swiglu(1, "f1", "kv")
            norm_apply("kv", hs, S, xq)
            pair_stage("kvk", lambda k, i, ps: v.tensor_copy(k_raw[:, 1, :], ps[:, 0:S]).then_inc(dve_read, 1))
            pair_stage("kvv", lambda k, i, ps: v.tensor_copy(v_sh[:, 1, :], ps[:, 0:S]).then_inc(dve_read, 1))

            dve.wait_ge(act_read, PAIR["kvk"] + 1)
            dve.wait_ge(dve_read, PAIR["kvk"] + 1)
            for base in (0, 64):
                for dst, src in ((base, base + 32), (base + 32, base)):
                    link(v.tensor_copy(k_sh[dst:dst + 32, :, :], k_raw[src:src + 32, :, :]))
            for c in range(2):
                link(v.tensor_tensor(k_sh[:, c, :], k_sh[:, c, :], sin2, ALU.mult))
                link(v.tensor_tensor(k_raw[:, c, :], k_raw[:, c, :], cos2, ALU.mult))
                link(v.tensor_tensor(k_sh[:, c, :], k_sh[:, c, :], k_raw[:, c, :], ALU.add))
            v.tensor_copy(soft[:, 15:16], k_sh[:, 1, 0:1]).then_inc(k_rot, 1)
            a = acc[NORM["f2"] % 2][:, 0:S]
            for c in range(C):
                square_sum("f2", hs[:, c, :], S, c, C)
            swiglu(2, "f2", "mix1")
            norm_apply("mix1", hs, S, xq)
            pair_stage("sq", lambda k, i, ps: v.tensor_copy(q_sw[:, 2 * k + 1, :], ps[:, 0:S]).then_inc(dve_read, 1))
            dve.wait_ge(act_read, PAIR["ffi3"])
            dve.wait_ge(dve_read, PAIR["ffi3"])
            for dst, src in ((64, 96), (96, 64)):
                link(v.tensor_copy(q_half[dst:dst + 32, :, :], q_sw[src:src + 32, :, :]))
            dve.wait_ge(q_copied, 2)
            for c in range(C):
                link(v.tensor_tensor(q_half[:, c, :], q_half[:, c, :], sin2, ALU.mult))
                link(v.tensor_tensor(q_sw[:, c, :], q_sw[:, c, :], cos2, ALU.mult))
                v.tensor_tensor(q_sw[:, c, :], q_sw[:, c, :], q_half[:, c, :], ALU.add).then_inc(q_rot, 1)

            def sw_mask(h, i):
                u = h % 2
                s_ = bank[4 + u]
                dve.wait_ge(w_sc, h + 1 + 4 * i)
                sink = small[:, TOPK + h:TOPK + h + 1] if isinstance(i, int) else small[:, bass.ds(TOPK + h + 4 * i, 1)]
                link(v.scalar_tensor_tensor(s_[:, 0:P], s_[:, 0:P], SCALE, swa_mask[:, 0:P], ALU.mult, ALU.add))
                link(v.tensor_scalar(s_[:, P:P + 1], sink, 1.0, None, ALU.mult))
                link(v.scalar_tensor_tensor(s_[:, P + 1:P + 1 + S], s_[:, P + 1:P + 1 + S], SCALE, swa_mask[:, P:P + S],
                                            ALU.mult, ALU.add))
                link(v.tensor_scalar(s_[:, P + 1 + S:P + 2 + S], sink, 1.0, None, ALU.mult))
                link(v.tensor_reduce(soft[:, 2 * u:2 * u + 1], s_[:, 0:P + 1], AX.X, ALU.max, negate=True))
                v.tensor_reduce(soft[:, 2 * u + 1:2 * u + 2], s_[:, P + 1:P + 2 + S], AX.X, ALU.max, negate=True)\
                 .then_inc(w_mask, 1)

            def sw_normalise(h, i):
                u = h % 2
                dve.wait_ge(w_exp, 2 * h + 2 + 8 * i)
                if h >= 2:
                    dve.wait_ge(w_p, 2 * h - 2 + 8 * i)
                link(v.reciprocal(soft[:, 8 + 2 * u:10 + 2 * u], soft[:, 4 + 2 * u:6 + 2 * u]))
                for t, (at, n) in enumerate(((0, P + 1), (P + 1, S + 1))):
                    p = sw_p[u][:, at:at + n]
                    v.tensor_scalar(p, p, soft[:, 8 + 2 * u + t:9 + 2 * u + t], None, ALU.mult).then_inc(w_p, 1)
                if h >= 3 and h % 2 == 1:
                    sw_rest((h - 3) // 2, i)

            def sw_rest(m, i):
                dve.wait_ge(w_hi_o, m + 1 + 2 * i)
                v.tensor_tensor(part(op_lo, S * m, S, i, 2 * S), bank[m % 2][:, 0:S],
                                part(op_hi, S * m, S, i, 2 * S).bitcast(F32), ALU.subtract).then_inc(w_lo_o, 1)

            def sw_turn(t, i):
                for u in range(4):
                    sw_mask(4 * t + u, i)
                    if 4 * t + u >= 1:
                        sw_normalise(4 * t + u - 1, i)
            sw_turn(0, 0)
            chain.loop(3, 24, lambda i: sw_turn(1, i))
            sw_normalise(H - 1, 0)
            sw_rest(H // 2 - 1, 0)
            residual_stage("swo", "f3")
            swiglu(3, "f3", "final2")
            norm_in_place("final2")

def conv_rest(dve, v, c, conv, xc, conv_hi, conv_lo):
    dve.wait_ge(conv_hi, c + 1)
    v.tensor_tensor(conv[1][:, c, :], xc[:, c, :], conv[0][:, c, :].bitcast(F32), ALU.subtract).then_inc(conv_lo, 1)


def tiles_of(m, per):
    k, n = m.shape
    return np.ascontiguousarray(m.reshape(k // P, P, n // P // per, per, P).transpose(2, 1, 3, 0, 4)
                                .reshape(n // P // per, P, -1))


def rows_of(m):
    k, n = m.shape
    return m.reshape(k // P, P, n).transpose(1, 0, 2).reshape(P, -1)


def swap_halves(m, width):
    k, n = m.shape
    return m.reshape(k, n // width, 2, width // 2)[:, :, ::-1, :].reshape(k, n)


def rope_tables(n, dim, base, reps):
    half = dim // 2
    inv = np.power(np.float32(base), -np.arange(half, dtype=np.float32) * np.float32(2.0 / dim)).astype(np.float32)
    ang = (np.arange(n, dtype=np.float32)[None, :] * inv[:, None]).astype(np.float32)
    cos, sin = np.cos(ang).astype(np.float32), np.sin(ang).astype(np.float32)
    return np.tile(np.concatenate([cos, cos]), (reps, 1)), np.tile(np.concatenate([-sin, sin]), (reps, 1))


def arrange(a):
    f = np.float32
    w = {}
    x_t = np.concatenate([a["meta_tokens"].T, a["x"][0].T], axis=1)
    w["x_t"] = np.ascontiguousarray(x_t.reshape(C, P, T).transpose(1, 0, 2))
    cuts = np.cumsum([D, D, QL, KVL, ROPE, D, D])
    xr, gr, cq, ckv, kr, g_rnn, g_att, _ = np.split(a["w_in"][0], cuts, axis=1)
    w["xr"] = tiles_of(xr, 2)
    kr4 = np.tile(np.concatenate([kr, swap_halves(kr, ROPE)], axis=1), (1, 2))
    w["lat"] = tiles_of(np.concatenate([ckv, kr4, cq], axis=1), 2)
    w["gates"] = np.stack([a["rg_wa"][0], a["rg_wx"][0]], axis=1).reshape(16, P, P).transpose(1, 0, 2).reshape(1, P, TILE)
    w["gr"] = tiles_of(gr, 2)
    uq = a["w_uq"][0].reshape(QL, H, NOPE + ROPE)
    nope, rope = uq[:, :, :NOPE].reshape(QL, -1), uq[:, :, NOPE:].reshape(QL, -1)
    both = np.stack([rope.reshape(QL, 4, P), swap_halves(rope, ROPE).reshape(QL, 4, P)], axis=2).reshape(QL, -1)
    w["uq"] = tiles_of(np.concatenate([nope, both], axis=1), 4)
    ukv = a["w_ukv"][0].reshape(KVL, H, NOPE + VD)
    w["uk"] = tiles_of(ukv[:, :, :NOPE].reshape(KVL, -1), C)
    w["uv"] = rows_of(ukv[:, :, NOPE:].reshape(KVL, -1))[None]
    g1, y1, g2, y2 = (tiles_of(m, 1) for m in (g_rnn, a["w_rnn_out"][0], g_att, a["w_attn_out"][0]))
    w["mix"] = np.stack([np.concatenate([g1, y1], axis=2), np.concatenate([g2, y2], axis=2)], axis=1).reshape(16, P, TILE)
    w["out1"] = tiles_of(a["w_out"][0], 2)
    w["pq"] = tiles_of(a["peer_wq"][0], 2)
    w["keys"] = np.concatenate([a["peer_keys1"][0].T, a["peer_keys2"][0].T], axis=1)
    w["uv_rows"] = np.concatenate([a["peer_u"][0], a["peer_v"][0]], axis=1)
    for n in range(4):
        layer, which = n // 2, n % 2 + 1
        gate, up = np.split(a[f"ffn{which}_w_in_2"][layer], 2, axis=1)
        w[f"ffi{n}"] = tiles_of(np.stack([gate.reshape(D, NF, P), up.reshape(D, NF, P)], axis=2).reshape(D, -1), 2)
        down = tiles_of(a[f"ffn{which}_w_out_2"][layer], 1)
        w[f"ffo{n}"] = down.reshape(C, P, 2, FH * P).transpose(0, 2, 1, 3).reshape(2 * C, P, FH * P)
    q, k, v2 = np.split(a["sb_w_qkv_2"][0], 3, axis=1)
    w["qk"] = tiles_of(np.concatenate([q, k], axis=1), 2)
    w["sbv"] = v2.reshape(4, 2, P, D).transpose(0, 2, 1, 3).reshape(4, P, TILE)
    w["sbo"] = tiles_of(a["sb_w_o_2"][0], 2)
    kk, kv = np.split(a["kv_w_2"], 2, axis=1)
    w["kvk"] = tiles_of(kk, 2)
    w["kvv"] = rows_of(kv)[None]
    w["sq"] = tiles_of(a["swa_w_q_2"][0].reshape(D, H, 64)[:, HEAD_AT].reshape(D, D), 2)
    w["swo"] = tiles_of(a["swa_w_o_2"][0].reshape(H, 64, D)[HEAD_AT].reshape(D, D), 2)

    cols = lambda m: m.reshape(-1, P).T
    v = {"n1": a["norm1_g"][0], "cq": a["q_norm_g"][0], "ckv": a["kv_norm_g"][0], "cb": a["conv_b"][0],
         "ba": a["rg_ba"][0], "bx": a["rg_bx"][0], "lam": a["rg_lambda"][0], "n2": a["norm2_g"][0],
         "final1": a["final_g"], "f0": a["ffn1_norm_2"][0], "f1": a["ffn2_norm_2"][0], "f2": a["ffn1_norm_2"][1],
         "f3": a["ffn2_norm_2"][1], "mix0": a["mix_norm_2"][0], "mix1": a["mix_norm_2"][1], "kv": a["kv_norm_2"],
         "final2": a["final_norm_2"], **{f"cw{t}": a["conv_w"][0][t] for t in range(4)}}
    w["vecs"] = np.concatenate([cols(v[name]) for name, _ in VECS], axis=1)
    p = np.arange(P)[:, None]
    no = f(-1e30)
    mask = np.concatenate([np.where(np.arange(SA)[None] <= p + META, f(0), no),
                           np.where(np.arange(SB)[None] <= p + META + P, f(0), no)], axis=1)
    cos, sin = rope_tables(T, ROPE, 10000.0, 4)
    w["tables1"] = np.concatenate([mask, cos, sin], axis=1).astype(f)
    w["squares"] = np.concatenate([np.ones((P, P)), np.eye(P), p >= p.T], axis=1).astype(f)
    sinks = a["swa_sinks_2"][0][HEAD_AT]
    w["small"] = np.concatenate([np.tile(np.arange(TOPK, dtype=f), (P, 1)), np.tile(sinks, (P, 1))], axis=1)
    before = np.where(p < p.T, f(0), no)
    sb_mask = np.concatenate([before, np.zeros((P, P), f), before], axis=1)
    j = np.arange(S)[None]
    swa_mask = np.concatenate([np.where(p.T <= p, f(0), no), np.where((j > p) & (j <= p + P), f(0), no)], axis=1)
    w["tables2"] = np.concatenate([sb_mask, swa_mask, *rope_tables(S, 64, 10000.0, 2)], axis=1).astype(f)
    return {k: np.ascontiguousarray(m) for k, m in w.items()}


STOP = ORDER[-1]


def kernel(**inputs):
    import concourse.bacc as bacc
    from concourse.bass_utils import run_bass_kernel_spmd

    w = arrange({k: np.asarray(m) for k, m in inputs.items()})
    nc = bacc.Bacc("TRN2", target_bir_lowering=False, num_devices=1)
    aps = {k: nc.dram_tensor(f"in_{k}", m.shape, mybir.dt.from_np(m.dtype), kind="ExternalInput").ap() for k, m in w.items()}
    out = nc.dram_tensor("out_t", (P, C, S), F32, kind="ExternalOutput").ap()
    program(nc, aps, out, STOP)
    r = run_bass_kernel_spmd(nc, [{f"in_{k}": m for k, m in w.items()}], core_ids=[0])
    return r.results[0]["out_t"].transpose(2, 1, 0).reshape(1, S, D)
```

```python
import numpy as np
import concourse.bass as bass
from concourse import mybir
from contextlib import ExitStack

F32 = mybir.dt.float32
F32R = mybir.dt.float32r
U32 = mybir.dt.uint32
ALU = mybir.AluOpType
ACT = mybir.ActivationFunctionType
AX = mybir.AxisListType

P = 128
D = 1024
C = D // P
S = 256
META = 16
T = S + META
TP = 384
EPS = 1e-6
QL, KVL = 384, 256
H, NOPE, ROPE, VD = 16, 64, 32, 64
FF = 2816
NF = FF // P
FH = NF // 2
PH, NKEY, TOPK = 8, 128, 16
TAB = 1281
RAW = 4
TILE = P * 16
MLA_SCALE = float((NOPE + ROPE) ** -0.5)
SCALE = float(64 ** -0.5)
SA, SB = P + META, T
HEAD_AT = [0, 4, 1, 5, 2, 6, 3, 7, 8, 12, 9, 13, 10, 14, 11, 15]


def ring_order():
    stages = [("xr", 4, TILE, 4), ("gates", 1, TILE, 8), ("lat", 3, TILE, 3), ("gr", 4, TILE, 4),
              ("uq", 4, 12 * P, 8), ("uk", 1, TILE, 4), ("uv", 1, TILE, 3),
              ("mix", 16, TILE, 16), ("out1", 4, TILE, 0), ("pq", PH, TILE, 0)]
    def ffn(f):
        return [(f"ffi{f}", NF, TILE, NF), (f"ffo{f}", 2 * C, FH * P, 0)]
    stages += ffn(0) + [("qk", 8, TILE, 8), ("sbv", 4, TILE, 2), ("sbo", 4, TILE, 0)]
    stages += ffn(1) + [("kvk", 1, TILE, 1), ("kvv", 1, TILE, 1)]
    stages += ffn(2) + [("sq", 4, TILE, 4), ("swo", 4, TILE, 0)] + ffn(3)
    b = r = n = m = 0
    first, width, pair, res, count, order, part, pairs_of = {}, {}, {}, {}, {}, [], {}, {}
    for name, blocks, cols, pairs in stages:
        first[name], width[name], pair[name], res[name], count[name] = b, cols, r, n, blocks
        order.append(name)
        part[name], pairs_of[name] = m, pairs
        m += C if name.startswith("ffo") else 3 if name == "sbv" else 0
        b += blocks
        r += pairs
        n += 0 if pairs or name == "pq" else C
    return first, width, pair, res, count, order, part, pairs_of


FIRST, WIDTH, PAIR, RES, BLOCKS, ORDER, PART, PAIRS_OF = ring_order()
END = FIRST[ORDER[-1]] + BLOCKS[ORDER[-1]]

NORMS = [("n1", C), ("cq", QL // P), ("ckv", KVL // P), ("n2", C), ("final1", 0), ("f0", C), ("mix0", C),
         ("f1", C), ("kv", C), ("f2", C), ("mix1", C), ("f3", C), ("final2", 0)]
NORM = {name: j for j, name in enumerate([name for name, _ in NORMS if name != "f2"])}
NORM["f2"] = NORM["kv"]
SPLIT0 = {name: sum(c for _, c in NORMS[:j]) for j, (name, _) in enumerate(NORMS)}

VECS = [("n1", C), ("cq", 3), ("ckv", 2), ("cw0", C), ("cw1", C), ("cw2", C), ("cw3", C), ("cb", C), ("ba", C),
        ("bx", C), ("lam", C), ("n2", C), ("final1", C), ("f0", C), ("f1", C), ("f2", C), ("f3", C), ("mix0", C),
        ("mix1", C), ("kv", C), ("final2", C)]
NV = sum(n for _, n in VECS)


class Chain:

    def __init__(self, eng, sem):
        self.eng, self.sem, self.n, self.off = eng, sem, 0, 0

    def link(self, ins):
        self.n += 1
        ins.then_inc(self.sem, 1)
        self.eng.wait_ge(self.sem, self.n + self.off)

    def loop(self, count, per, body):
        start = self.n
        with self.eng.Fori(0, count) as i:
            self.off = i * per
            body(i)
        self.off = 0
        assert self.n - start == per, (self.n - start, per)
        self.n = start + per * count


def program(nc, w, out, stop):
    ctx = ExitStack()
    with ctx:
        def sb(name, cols, dt=F32):
            return ctx.enter_context(nc.sbuf_tensor(name, [P, cols], dt))

        def sem(name):
            return ctx.enter_context(nc.semaphore(name))

        raw = [sb(f"raw{s}", TILE) for s in range(RAW)]
        w_hi = [sb(f"w_hi{s}", TILE, F32R) for s in range(2)]
        w_lo = [sb(f"w_lo{s}", TILE, F32R) for s in range(2)]
        xn_hi, xn_lo = sb("xn_hi", C * T, F32R), sb("xn_lo", C * T, F32R)
        op_hi, op_lo = sb("op_hi", 24 * S, F32R), sb("op_lo", 24 * S, F32R)
        h_all = sb("h_all", C * T)
        arena = sb("arena", 11520)
        half = sb("half", C * S)
        tmp = sb("tmp", 1088)
        acc = [sb(f"acc{i}", T) for i in range(2)]
        tables = sb("tables", TAB + 4 * P)
        keys = sb("keys", 2 * NKEY)
        small = sb("small", TOPK + H)
        picks = sb("picks", 4 * 2 * TOPK)
        vecs = sb("vecs", NV)
        lam_t = sb("lam_t", 8 * C)
        soft = sb("soft", 24 + 1 + H)
        eps = sb("eps", 1)
        bank = [ctx.enter_context(nc.psum_tensor(f"bank{i}", [P, 512], F32)) for i in range(8)]

        def chunks(t, n, width, at=0):
            return t[:, at:at + n * width].rearrange("p (c t) -> p c t", t=width)

        h_t = chunks(h_all, C, T)
        hs = h_t[:, :, META:T]
        xf = [tmp[:, 0:T], tmp[:, T:2 * T]]
        sg = [tmp[:, 544:800], tmp[:, 800:1056]]
        xn = (chunks(xn_hi, C, T), chunks(xn_lo, C, T))
        xs = (xn[0][:, :, META:T], xn[1][:, :, META:T])
        conv = (chunks(op_hi, C, T), chunks(op_lo, C, T))
        y_rnn = (chunks(op_hi, C, S), chunks(op_lo, C, S))
        o_att = (chunks(op_hi, C, S, C * S), chunks(op_lo, C, S, C * S))
        mixed = (chunks(op_hi, C, S, 2 * C * S), chunks(op_lo, C, S, 2 * C * S))
        cqn = (chunks(op_hi, 3, S, 2 * C * S), chunks(op_lo, 3, S, 2 * C * S))
        ckvn = (chunks(op_hi, 2, TP, 2 * C * S + 3 * S), chunks(op_lo, 2, TP, 2 * C * S + 3 * S))
        inner = (chunks(op_hi, NF, S), chunks(op_lo, NF, S))
        xrp = chunks(arena, C, T + 3)
        a_t = chunks(arena, C, T)
        xc = chunks(arena, C, T, 2200)
        r_t = chunks(arena, C, T, 4400)
        i_t = chunks(arena, C, T, 6600)
        cqf = chunks(arena, 3, S, 8800)
        ckvf = chunks(arena, 2, T, 9568)
        kr_raw = arena[:, 10112:10384]
        kr_rot = arena[:, 10384:10656]
        gr = chunks(half, C, S)
        qh = chunks(arena, H, S)
        kh = chunks(arena, H, T, 4096)
        vt = chunks(arena, 3, D, 8448)
        probs = [half[:, 0:640], half[:, 640:1280]]
        pt = [half[:, 1280:1920], tmp[:, 0:640]]
        mla_mask = tables[:, 0:416]
        cos_t, sin_t = tables[:, 416:416 + T], tables[:, 416 + T:416 + 2 * T]
        ones, ident, tri, swap = (tables[:, TAB + P * i:TAB + P * (i + 1)] for i in range(4))
        sb_mask, swa_mask = tables[:, 0:384], tables[:, 384:769]
        cos2, sin2 = tables[:, 769:769 + S], tables[:, 769 + S:TAB]
        pulled = [arena[:, 2 * D * n:2 * D * (n + 1)] for n in range(4)]
        x_tok = chunks(arena, 2, D, 8 * D)
        x_f = chunks(half, C, S)
        q_s = [half[:, 512 * n:512 * (n + 1)] for n in range(2)]
        q_at = [pulled[3][:, 0:512], q_s[1]] + [q_s[n % 2] for n in range(2, PH)]
        product = half[:, D:2 * D]
        scratch = arena[:, 10 * D:11520]
        diag = [tmp[:, P * n:P * (n + 1)] for n in range(2)]
        y_tok = chunks(arena, 2, D)
        gw = [picks[:, 32 * n:32 * n + 32] for n in range(2)]
        expert = [picks[:, 64 + 32 * n:96 + 32 * n].bitcast(U32) for n in range(2)]
        xq = (xn[0][:, :, 0:S], xn[1][:, :, 0:S])
        qk = chunks(arena, 2 * C, S)
        sv = chunks(arena, 2, D, 4096)
        zm = [arena[:, 6144 + 384 * n:6528 + 384 * n] for n in range(4)]
        az, sp_t, wt = ([arena[:, 7680 + 768 * a + 384 * n:8064 + 768 * a + 384 * n] for n in range(2)] for a in range(3))
        four = (bank[4], bank[5], bank[2], bank[3])
        o2 = y_rnn
        k_sh, v_sh, k_raw = chunks(arena, 2, S), chunks(arena, 2, S, 512), chunks(arena, 2, S, 1024)
        q_sw, q_half = chunks(arena, C, S, 2048), chunks(arena, C, S, 4096)
        sw_p = [arena[:, 6144 + 386 * n:6530 + 386 * n] for n in range(4)]
        sw_pt = [arena[:, 7688 + 384 * n:8072 + 384 * n] for n in range(2)]
        V_AT, at = {}, 0
        for name, n in VECS:
            V_AT[name] = (at, n)
            at += n
        def vec(name, c):
            return vecs[:, V_AT[name][0] + c:V_AT[name][0] + c + 1]
        sinks = soft[:, 25:25 + H]
        cl, ncl = lam_t[:, 0:C], lam_t[:, C:2 * C]

        names, at = {}, 0
        for name, n in (("s", NKEY), ("cand", 256), ("left", 256), ("hit", 256), ("t1", 16), ("t2", 16), ("i1", 16),
                        ("i2", 16), ("f1", 16), ("f2", 16), ("best", 16), ("at", 16), ("hi", 16), ("lo", 16),
                        ("fh", 16), ("fl", 16), ("e1", 16), ("e2", 16), ("neg", 1), ("sum", 1), ("rs", 1)):
            names[name] = (at, n)
            at += n
        top = {name: scratch[:, a:a + n] for name, (a, n) in names.items()}
        dots, coef = scratch[:, at:at + 4], scratch[:, at + 4:at + 12]
        assert at + 12 <= 1264

        landed = [sem(f"landed{s}") for s in range(RAW)]
        hi_done, lo_done = sem("hi_done"), sem("lo_done")
        even_done, odd_done = sem("even_done"), sem("odd_done")
        act_read, dve_read = sem("act_read"), sem("dve_read")
        res_done = sem("res_done")
        part_done = sem("part_done")
        h_new = sem("h_new")
        ss_in, ss_done = sem("ss_in"), sem("ss_done")
        sd_done, rs_done = sem("sd_done"), sem("rs_done")
        xf_done, xhi_done, xlo_done = sem("xf_done"), sem("xhi_done"), sem("xlo_done")
        const_in, x_in = sem("const_in"), sem("x_in")
        pads = sem("pads")
        lam_e, lam_c = sem("lam_e"), sem("lam_c")
        conv_done, conv_hi, conv_lo = sem("conv_done"), sem("conv_hi"), sem("conv_lo")
        lru_act, lru_dve, lru_pool = sem("lru_act"), sem("lru_dve"), sem("lru_pool")
        y_f, y_hi, y_lo = sem("y_f"), sem("y_hi"), sem("y_lo")
        kr_in, kr_ready = sem("kr_in"), sem("kr_ready")
        lat_read = sem("lat_read")
        sc_done, sc_masked, exp_done, p_ready = sem("sc_done"), sem("sc_masked"), sem("exp_done"), sem("p_ready")
        tr_done, ptx, pty, pv_done = sem("tr_done"), sem("ptx"), sem("pty"), sem("pv_done")
        o_done, o_hi, o_lo = sem("o_done"), sem("o_hi"), sem("o_lo")
        gate_done, mix_f, mix_hi, mix_lo = sem("gate_done"), sem("mix_f"), sem("mix_hi"), sem("mix_lo")
        rope_in = sem("rope_in")
        dve_step, act_step = sem("dve_step"), sem("act_step")
        xt_ps, xt_read = sem("xt_ps"), sem("xt_read")
        q_done, q_read, key_done = sem("q_done"), sem("q_read"), sem("key_done")
        top_max, top_exp, expert_in = sem("top_max"), sem("top_exp"), sem("expert_in")
        gathered = [sem(f"gathered{s}") for s in range(4)]
        dot_done, diag_done, row_used = sem("dot_done"), sem("diag_done"), sem("row_used")
        y_tok_act, y_tok_dve, y_back = sem("y_tok_act"), sem("y_tok_dve"), sem("y_back")
        peer_h, h_scaled = sem("peer_h"), sem("h_scaled")
        in_hi, in_lo = sem("in_hi"), sem("in_lo")
        z_done, z_mask, soft_in, sp_done = sem("z_done"), sem("z_mask"), sem("soft_in"), sem("sp_done")
        suf_done, arg_done, w_done, sbo_done = sem("suf_done"), sem("arg_done"), sem("w_done"), sem("sbo_done")
        sbo_hi, sbo_lo = sem("sbo_hi"), sem("sbo_lo")
        tables2_in = sem("tables2_in")
        k_half, k_rot, q_swap, q_rot = sem("k_half"), sem("k_rot"), sem("q_swap"), sem("q_rot")
        sink_in = sem("sink_in")
        w_sc, w_mask, w_exp, w_p = sem("w_sc"), sem("w_mask"), sem("w_exp"), sem("w_p")
        w_tr, w_pt, w_pv, w_hi_o, w_lo_o = sem("w_tr"), sem("w_pt"), sem("w_pv"), sem("w_hi_o"), sem("w_lo_o")
        stored = sem("stored")

        def each(eng, n, body, tail=0, per=RAW):
            turns = (n - tail) // per
            if turns >= 2:
                with eng.Fori(0, turns) as i:
                    for u in range(per):
                        body(u, i * (per // RAW) if per > RAW else i)
            else:
                turns = 0
            for k in range(per * turns, n):
                body(k, 0)

        block = ctx.enter_context(nc.Block())

        @block.sync
        def _(sp):
            sp.dma_start(h_t[:, :, :], w["x_t"]).then_inc(x_in, 16)
            sp.dma_start(tables[:, 0:960], w["tables1"]).then_inc(const_in, 16)
            sp.dma_start(tables[:, TAB:], w["squares"]).then_inc(const_in, 16)
            sp.dma_start(keys[:, :], w["keys"]).then_inc(const_in, 16)
            sp.dma_start(small[:, :], w["small"]).then_inc(const_in, 16)
            sp.dma_start(vecs[:, :], w["vecs"]).then_inc(const_in, 16)

            def load(name):
                src, cols = w[name], WIDTH[name]

                def body(k, i):
                    b = FIRST[name] + k
                    if b >= RAW:
                        sp.wait_ge(lo_done, b - RAW + 1 + 4 * i)
                    at = src[bass.ds(k + 4 * i, 1), :, :] if not isinstance(i, int) else src[k:k + 1, :, :]
                    sp.dma_start(raw[b % RAW][:, 0:cols], at.rearrange("a p n -> (a p) n"))\
                      .then_inc(landed[b % RAW], 16)
                each(sp, BLOCKS[name], body)

            for name in ORDER[:ORDER.index(stop) + 1]:
                load(name)
                if name == "pq":
                    sp.wait_ge(h_new, RES["out1"] + C)
                    sp.dma_start(tables[:, 0:TAB], w["tables2"]).then_inc(tables2_in, 16)
            sp.wait_ge(*((h_scaled, C) if stop == "pq" else (h_scaled, 2 * C) if stop == ORDER[-1] else (h_new, RES[stop] + C)))
            sp.dma_start(out, hs).then_inc(stored, 16)
            sp.wait_ge(stored, 16)

        @block.gpsimd
        def _(pool):
            pool.memset(eps[:, :], EPS).then_inc(pads, 1)
            pool.memset(xrp[:, :, 0:3], 0.0).then_inc(pads, 1)
            for part in ckvn:
                pool.memset(part[:, :, T:TP].bitcast(F32), 0.0).then_inc(pads, 1)

            pool.wait_ge(lru_act, 1)
            nc.gpsimd.tensor_tensor(i_t[:, :, :], i_t[:, :, :], xc[:, :, :], ALU.mult).then_inc(lru_pool, 1)
            pool.wait_ge(lru_pool, 1)
            pool.wait_ge(conv_lo, C)
            pool.wait_ge(lru_act, 2)
            nc.gpsimd.tensor_tensor(xc[:, :, :], a_t[:, :, :], a_t[:, :, :], ALU.mult).then_inc(lru_pool, 1)

            pool.wait_ge(ss_in, NORM["n2"] + 1)
            for n in range(2 * PH):
                pool.wait_ge(expert_in, n + 1)
                for s in range(TOPK):
                    q = TOPK * n + s
                    if q >= 4:
                        pool.wait_ge(row_used, q - 3)
                    at = TOPK * (n % 2) + s
                    pool.indirect_dma_start(pulled[s % 4], None, w["uv_rows"],
                                            bass.IndirectOffsetOnAxis(expert[n // 2 % 2][:, at:at + 1], 0))\
                        .then_inc(gathered[s % 4], 16)

        @block.tensor
        def _(pe):
            def mm3(o, wt, x, first=True, last=True):
                nc.tensor.matmul(o, wt[0], x[1], start=first, stop=False)
                nc.tensor.matmul(o, wt[0], x[0], start=False, stop=False)
                return nc.tensor.matmul(o, wt[1], x[0], start=False, stop=last)

            def tiles(b, n):
                v = w_hi[b % 2][:, n * P:(n + 1) * P], w_lo[b % 2][:, n * P:(n + 1) * P]
                return v

            def split_ready(name, k, i):
                pe.wait_ge(lo_done, FIRST[name] + k + 1 + 4 * i)

            def even_free(r, i=0):
                if r >= 2:
                    pe.wait_ge(act_read, r - 1 + 4 * i)

            def odd_free(r, i=0):
                if r >= 2:
                    pe.wait_ge(dve_read, r - 1 + 4 * i)

            def pair_stage(name, x, n=T, norm=None, after=None):
                def body(k, i):
                    b, r = FIRST[name] + k, PAIR[name] + k
                    split_ready(name, k, i)
                    for c, free, done in ((0, even_free, even_done), (1, odd_free, odd_done)):
                        free(r, i)
                        o = bank[2 * (r % 2) + c][:, 0:n]
                        for kk in range(C):
                            if norm and k == 0 and c == 0:
                                pe.wait_ge(xlo_done, SPLIT0[norm] + kk + 1)
                            last = mm3(o, tiles(b, C * c + kk), (x[0][:, kk, :], x[1][:, kk, :]), kk == 0, kk == C - 1)
                        last.then_inc(done, 1)
                    if after:
                        after(k)
                each(pe, BLOCKS[name], body, per=2 * RAW)

            def norm_sum(name, n):
                j = NORM[name]
                pe.wait_ge(ss_in, j + 1)
                nc.tensor.matmul(bank[6 + j % 2][:, 0:n], ones, acc[j % 2][:, 0:n], start=True, stop=True)\
                  .then_inc(ss_done, 1)

            def residual_stage(name, x, ready):
                def body(k, i):
                    b = FIRST[name] + k
                    split_ready(name, k, i)
                    for c in range(2):
                        n = RES[name] + 2 * k + c
                        if n >= 2:
                            pe.wait_ge(h_new, n - 1 + 8 * i)
                        for kk in range(C):
                            if k == 0 and c == 0:
                                pe.wait_ge(*ready(kk))
                            last = mm3(bank[4 + n % 2][:, 0:S], tiles(b, C * c + kk), (x[0][:, kk, :], x[1][:, kk, :]),
                                       kk == 0, kk == C - 1)
                        last.then_inc(res_done, 1)
                each(pe, BLOCKS[name], body, per=2 * RAW)

            pe.wait_ge(const_in, 80)
            norm_sum("n1", T)
            pair_stage("xr", xn, norm="n1")
            split_ready("gates", 0, 0)
            for c in range(C):
                r = PAIR["gates"] + c
                pe.wait_ge(conv_lo, c + 1)
                x = conv[0][:, c, :], conv[1][:, c, :]
                even_free(r)
                mm3(bank[2 * (r % 2)][:, 0:T], tiles(FIRST["gates"], 2 * c), x).then_inc(even_done, 1)
                odd_free(r)
                mm3(bank[2 * (r % 2) + 1][:, 0:T], tiles(FIRST["gates"], 2 * c + 1), x).then_inc(odd_done, 1)
            pair_stage("lat", xn)
            pair_stage("gr", xs, n=S, after=lambda k: (norm_sum("cq", S), norm_sum("ckv", T)) if k == 1 else None)
            for k in range(4):
                split_ready("uq", k, 0)
                for c in range(4):
                    r = PAIR["uq"] + 2 * k + c // 2
                    (odd_free if c % 2 else even_free)(r)
                    for kk in range(3):
                        if k == 0 and c == 0:
                            pe.wait_ge(xlo_done, SPLIT0["cq"] + kk + 1)
                        last = mm3(bank[2 * (r % 2) + c % 2][:, 0:S], tiles(FIRST["uq"] + k, 3 * c + kk),
                                   (cqn[0][:, kk, :], cqn[1][:, kk, :]), kk == 0, kk == 2)
                    last.then_inc(odd_done if c % 2 else even_done, 1)
            split_ready("uk", 0, 0)
            for c in range(C):
                r = PAIR["uk"] + c // 2
                (odd_free if c % 2 else even_free)(r)
                for kk in range(2):
                    if c == 0:
                        pe.wait_ge(xlo_done, SPLIT0["ckv"] + kk + 1)
                    last = mm3(bank[2 * (r % 2) + c % 2][:, 0:T], tiles(FIRST["uk"], 2 * c + kk),
                               (ckvn[0][:, kk, 0:T], ckvn[1][:, kk, 0:T]), kk == 0, kk == 1)
                last.then_inc(odd_done if c % 2 else even_done, 1)
            split_ready("uv", 0, 0)
            wv = chunks(w_hi[FIRST["uv"] % 2], 2, D), chunks(w_lo[FIRST["uv"] % 2], 2, D)
            for t in range(3):
                r = PAIR["uv"] + t
                for hf, free, done in ((0, even_free, even_done), (1, odd_free, odd_done)):
                    free(r)
                    for kk in range(2):
                        last = mm3(bank[2 * (r % 2) + hf][:, :],
                                   (ckvn[0][:, kk, P * t:P * t + P], ckvn[1][:, kk, P * t:P * t + P]),
                                   (wv[0][:, kk, 512 * hf:512 * hf + 512], wv[1][:, kk, 512 * hf:512 * hf + 512]),
                                   kk == 0, kk == 1)
                    last.then_inc(done, 1)

            def scores(h):
                if h >= 2:
                    pe.wait_ge(exp_done, 2 * (h - 1))
                nc.tensor.matmul(bank[4 + h % 2][:, 0:SA], qh[0:96, h, 0:P], kh[0:96, h, 0:SA], start=True, stop=True)
                nc.tensor.matmul(bank[4 + h % 2][:, SA:SA + SB], qh[0:96, h, P:S], kh[0:96, h, 0:SB],
                                 start=True, stop=True).then_inc(sc_done, 1)

            def transposes(h):
                pe.wait_ge(p_ready, 2 * h + 2)
                if h >= 2:
                    pe.wait_ge(ptx, h - 1)
                    pe.wait_ge(pty, h - 1)
                p = probs[h % 2]
                for n, at in enumerate((0, 256, P, 256 + P)):
                    nc.tensor.transpose(bank[6 + h % 2][:, P * n:P * n + P], p[:, at:at + P], ident)
                nc.tensor.transpose(bank[2 + h % 2][:, 0:P], p[:, 512:640], ident).then_inc(tr_done, 1)

            def values(h):
                pe.wait_ge(ptx, h + 1)
                pe.wait_ge(pty, h + 1)
                if h >= 4 and h % 2 == 0:
                    pe.wait_ge(o_lo, h // 2 - 1)
                base = 64 * (h % 2)
                o = bank[h // 2 % 2]
                q = pt[h % 2]
                cols = slice(VD * h, VD * h + VD)
                nc.tensor.matmul(o[base:base + 64, 0:S], vt[:, 0, cols], q[:, 0:S], start=True, stop=False)
                nc.tensor.matmul(o[base:base + 64, 0:S], vt[:, 1, cols], q[:, S:2 * S], start=False, stop=False)
                nc.tensor.matmul(o[base:base + 64, P:S], vt[:, 2, cols], q[:, 2 * S:2 * S + P],
                                 start=False, stop=True).then_inc(pv_done, 1)

            r = PAIR["mix"]
            pe.wait_ge(act_read, r)
            pe.wait_ge(dve_read, r)
            pe.wait_ge(kr_ready, 1)
            pe.wait_ge(rope_in, 16)
            for h in range(3):
                scores(h)
            transposes(0)
            for h in range(H):
                if h + 3 < H:
                    scores(h + 3)
                if h + 1 < H:
                    transposes(h + 1)
                values(h)

            def mix(k, i):
                b, r = FIRST["mix"] + k, PAIR["mix"] + k
                split_ready("mix", k, i)
                even_free(r, i)
                for kk in range(C):
                    last = mm3(bank[2 * (r % 2)][:, 0:S], tiles(b, kk), (xs[0][:, kk, :], xs[1][:, kk, :]),
                               kk == 0, kk == C - 1)
                last.then_inc(even_done, 1)
                odd_free(r, i)
                y = y_rnn if k % 2 == 0 else o_att
                for kk in range(C):
                    if k == 0 and kk == 0:
                        pe.wait_ge(y_lo, 1)
                    last = mm3(bank[2 * (r % 2) + 1][:, 0:S], tiles(b, C + kk), (y[0][:, kk, :], y[1][:, kk, :]),
                               kk == 0, kk == C - 1)
                last.then_inc(odd_done, 1)
            pe.wait_ge(o_lo, C)
            each(pe, BLOCKS["mix"], mix, per=2 * RAW)
            residual_stage("out1", mixed, lambda kk: (mix_lo, kk + 1))
            norm_sum("n2", S)

            def token_major():
                for t in range(2):
                    for c in range(C):
                        last = nc.tensor.transpose(bank[4 + 2 * t + c // 4][:, P * (c % 4):P * (c % 4 + 1)],
                                                   x_f[:, c, P * t:P * t + P], ident)
                    last.then_inc(xt_ps, 1)

            def query_part(h, n):
                c, kk = n // C, n % C
                if n == 0:
                    split_ready("pq", h, 0)
                    if h >= 2:
                        pe.wait_ge(q_read, h - 1)
                last = mm3(bank[h % 2][:, S * c:S * c + S], tiles(FIRST["pq"] + h, n),
                           (xq[0][:, kk, :], xq[1][:, kk, :]), kk == 0, kk == C - 1)
                if n == 2 * C - 1:
                    last.then_inc(q_done, 1)

            def key_scores(h):
                pe.wait_ge(q_read, h + 1)
                if h >= 2:
                    pe.wait_ge(expert_in, 2 * (h - 1))
                for t in range(2):
                    for c in range(2):
                        last = nc.tensor.matmul(bank[2 + h % 2][:, P * (2 * t + c):P * (2 * t + c + 1)],
                                                q_at[h][:, S * c + P * t:S * c + P * t + P],
                                                keys[:, NKEY * c:NKEY * (c + 1)], start=True, stop=True)
                last.then_inc(key_done, 1)

            def add_rows(n, s, i):
                q = 16 * n + s
                pe.wait_ge(diag_done, q + 1 + (0 if isinstance(i, int) else 4 * i))
                for f in range(2):
                    last = nc.tensor.matmul(bank[4 + 2 * (n % 2) + f][:, :], diag[s % 2],
                                            pulled[s % 4][:, D + 512 * f:D + 512 * (f + 1)],
                                            start=(n < 2 and s == 0), stop=True, skip_group_check=True)
                last.then_inc(row_used, 1)

            for h in range(2):
                for n in range(2 * C):
                    if h == 0 and n < C:
                        pe.wait_ge(xlo_done, SPLIT0["n2"] + n + 1)
                    query_part(h, n)
                key_scores(h)
                if h == 0:
                    token_major()
            for n in range(2 * PH):
                h = n // 2 + 2
                if n % 2 == 0 and h < PH:
                    for s in range(TOPK):
                        query_part(h, s)
                        add_rows(n, s, 0)
                elif n == 1:
                    for s in range(TOPK):
                        if s == 12:
                            key_scores(h)
                        add_rows(n, s, 0)
                else:
                    with pe.Fori(0, 3) as i:
                        for s in range(4):
                            add_rows(n, s, i)
                    if h < PH:
                        key_scores(h)
                    for s in range(12, TOPK):
                        add_rows(n, s, 0)
            for t in range(2):
                pe.wait_ge(y_tok_act, t + 1)
                pe.wait_ge(y_tok_dve, t + 1)
                for c in range(C):
                    last = nc.tensor.transpose(bank[c // 2][:, S * (c % 2) + P * t:S * (c % 2) + P * t + P],
                                               y_tok[:, t, P * c:P * c + P], ident)
            last.then_inc(y_back, 1)
            pe.wait_ge(peer_h, C)
            norm_sum("final1", S)
            if stop == "pq":
                return

            def swiglu(f, norm):
                if norm != "f2":
                    norm_sum(norm, S)
                pair_stage(f"ffi{f}", xq, n=S, norm=norm)

                def down(k, i):
                    name = f"ffo{f}"
                    c, part = k // 2, k % 2
                    n = RES[name] + c
                    split_ready(name, k, i)
                    if part == 0:
                        pe.wait_ge(h_new, n - 1 + 2 * i)
                    for t in range(FH):
                        kk = FH * part + t
                        if k < 2:
                            pe.wait_ge(in_lo, NF * f + kk + 1)
                        last = mm3(bank[4 + n % 2][:, 0:S], tiles(FIRST[name] + k, t),
                                   (inner[0][:, kk, :], inner[1][:, kk, :]), kk == 0, kk == NF - 1)
                    last.then_inc(res_done if part else part_done, 1)
                each(pe, BLOCKS[f"ffo{f}"], down, per=2 * RAW)

            def values_stage(name, blocks, width, per):
                parts = width // 512 or 1
                cols = min(width, 512)
                for k in range(blocks):
                    split_ready(name, k, 0)
                    b = FIRST[name] + k
                    for t in range(2):
                        for hf in range(parts):
                            r, c = (PAIR[name] + t, hf) if parts == 2 else (PAIR[name], t)
                            if k == 0:
                                (odd_free if c else even_free)(r)
                            for kk in range(per):
                                ci = per * k + kk
                                at = width * kk + 512 * hf
                                last = mm3(bank[2 * (r % 2) + c][:, 0:cols],
                                           (xq[0][:, ci, P * t:P * t + P], xq[1][:, ci, P * t:P * t + P]),
                                           (w_hi[b % 2][:, at:at + cols], w_lo[b % 2][:, at:at + cols]),
                                           ci == 0, ci == C - 1)
                            if k == blocks - 1:
                                last.then_inc(odd_done if c else even_done, 1)
                    if k < blocks - 1:
                        last.then_inc(part_done, 1)

            swiglu(0, "f0")
            if stop == "ffo0":
                return
            norm_sum("mix0", S)
            pair_stage("qk", xq, n=S, norm="mix0")
            values_stage("sbv", 4, D, 2)

            pe.wait_ge(act_read, PAIR["sbv"] + 2)
            pe.wait_ge(dve_read, PAIR["sbv"] + 2)
            pe.wait_ge(tables2_in, 16)

            def logits(h):
                base, c = 64 * (h % 2), h // 2
                if h >= 4:
                    pe.wait_ge(z_mask, h - 3)
                rows_ = slice(base, base + 64)
                nc.tensor.matmul(four[h % 4][:, 0:S], qk[rows_, C + c, 0:P], qk[rows_, c, :], start=True, stop=True)
                nc.tensor.matmul(four[h % 4][:, S:S + P], qk[rows_, C + c, P:S], qk[rows_, c, P:S],
                                 start=True, stop=True).then_inc(z_done, 1)

            def suffixes(h):
                pe.wait_ge(sp_done, h + 1)
                if h >= 2:
                    pe.wait_ge(arg_done, h - 1)
                s_, o = sp_t[h % 2], bank[6 + h % 2]
                nc.tensor.matmul(o[:, 0:S], tri, s_[:, 0:S], start=True, stop=False)
                nc.tensor.matmul(o[:, P:S], ones, s_[:, S:S + P], start=False, stop=True)
                nc.tensor.matmul(o[:, S:S + P], tri, s_[:, S:S + P], start=True, stop=True).then_inc(suf_done, 1)

            def sb_values(h):
                pe.wait_ge(w_done, h + 1)
                if h >= 4 and h % 2 == 0:
                    pe.wait_ge(sbo_lo, h // 2 - 1)
                base, o = 64 * (h % 2), bank[h // 2 % 2]
                cols = slice(64 * h, 64 * h + 64)
                nc.tensor.matmul(o[base:base + 64, 0:S], sv[:, 0, cols], wt[h % 2][:, 0:S], start=True, stop=False)
                nc.tensor.matmul(o[base:base + 64, P:S], sv[:, 1, cols], wt[h % 2][:, S:S + P], start=False, stop=True)\
                  .then_inc(sbo_done, 1)

            for h in range(3):
                logits(h)
            for h in range(H):
                if h + 3 < H:
                    logits(h + 3)
                suffixes(h)
                if h >= 2:
                    sb_values(h - 2)
            sb_values(H - 2)
            sb_values(H - 1)
            residual_stage("sbo", o2, lambda kk: (sbo_lo, kk + 1))
            if stop == "sbo":
                return
            swiglu(1, "f1")
            norm_sum("kv", S)
            pair_stage("kvk", xq, n=S, norm="kv")
            values_stage("kvv", 1, S, C)
            swiglu(2, "f2")
            norm_sum("mix1", S)

            def swap_halves_of(k):
                pe.wait_ge(act_read, PAIR["sq"] + k + 1)
                pe.wait_ge(dve_read, PAIR["sq"] + k + 1)
                if k >= 2:
                    pe.wait_ge(q_rot, k - 1)
                for c in range(2):
                    last = nc.tensor.matmul(bank[4 + k % 2][:, S * c:S * c + S], swap, q_sw[:, 2 * k + c, :],
                                            start=True, stop=True)
                last.then_inc(q_swap, 1)
            pair_stage("sq", xq, n=S, norm="mix1", after=lambda k: swap_halves_of(k - 1) if k else None)
            swap_halves_of(3)

            pe.wait_ge(q_rot, 4)
            pe.wait_ge(k_rot, 1)

            def sw_scores(h):
                base, g = 64 * (h % 2), HEAD_AT[h] // 4
                if h >= 4:
                    pe.wait_ge(w_exp, 2 * (h - 3))
                rows_, o = slice(base, base + 64), four[h % 4]
                nc.tensor.matmul(o[:, 0:P], q_sw[rows_, h // 2, 0:P], k_sh[rows_, g // 2, 0:P], start=True, stop=True)
                nc.tensor.matmul(o[:, P + 1:P + 1 + S], q_sw[rows_, h // 2, P:S], k_sh[rows_, g // 2, :],
                                 start=True, stop=True).then_inc(w_sc, 1)

            def sw_transposes(h):
                pe.wait_ge(w_p, 2 * h + 2)
                if h >= 2:
                    pe.wait_ge(w_pt, h - 1)
                for n, at in enumerate((0, P + 2, 2 * P + 2)):
                    last = nc.tensor.transpose(bank[6 + h % 2][:, P * n:P * n + P], sw_p[h % 4][:, at:at + P], ident)
                last.then_inc(w_tr, 1)

            def sw_values(h):
                pe.wait_ge(w_pt, h + 1)
                if h >= 4 and h % 2 == 0:
                    pe.wait_ge(w_lo_o, h // 2 - 1)
                base, o, g = 64 * (h % 2), bank[h // 2 % 2], HEAD_AT[h] // 4
                cols = slice(64 * g, 64 * g + 64)
                q = sw_pt[h % 2]
                nc.tensor.matmul(o[base:base + 64, 0:S], v_sh[:, 0, cols], q[:, 0:S], start=True, stop=False)
                nc.tensor.matmul(o[base:base + 64, P:S], v_sh[:, 1, cols], q[:, S:S + P], start=False, stop=True)\
                  .then_inc(w_pv, 1)

            for h in range(3):
                sw_scores(h)
            sw_transposes(0)
            for h in range(H):
                if h + 3 < H:
                    sw_scores(h + 3)
                if h + 1 < H:
                    sw_transposes(h + 1)
                sw_values(h)
            residual_stage("swo", o2, lambda kk: (w_lo_o, kk + 1))
            swiglu(3, "f3")
            norm_sum("final2", S)

        @block.scalar
        def _(act):
            chain = Chain(act, act_step)

            def round_block(b, cols, i=0):
                act.wait_ge(landed[b % RAW], 16 * (b // RAW + 1) + 16 * i)
                nc.scalar.activation(w_hi[b % 2][:, 0:cols], raw[b % RAW][:, 0:cols], ACT.Copy).then_inc(hi_done, 1)

            def done_of(name, k, i=0):
                if name.startswith("ffo"):
                    n = RES[name] + k // 2
                    return (res_done, n + 1 + 2 * i) if k % 2 else (part_done, PART[name] + k // 2 + 1 + 2 * i)
                if name == "sbv" and k < 3:
                    return part_done, PART[name] + k + 1
                if name == "pq":
                    return q_done, k + 1
                if PAIRS_OF[name] == 0:
                    return res_done, RES[name] + 2 * (k + 1) + 8 * i
                per = max(1, PAIRS_OF[name] // BLOCKS[name])
                if name == "sbv":
                    return odd_done, PAIR[name] + 2
                return odd_done, PAIR[name] + per * (k + 1) + 4 * per * i

            def round_next(name, k, i=0):
                b = FIRST[name] + k + 1
                if b >= END or (name == stop and k == BLOCKS[name] - 1 and isinstance(i, int)):
                    return
                nxt = name if k + 1 < BLOCKS[name] else ORDER[ORDER.index(name) + 1]
                if k >= 1 or not isinstance(i, int):
                    act.wait_ge(*done_of(name, k - 1, i))
                elif b >= 2:
                    prev = ORDER[ORDER.index(name) - 1]
                    act.wait_ge(*done_of(prev, BLOCKS[prev] - 1))
                round_block(b, WIDTH[nxt], i)

            def stage_start(name):
                prev = ORDER[ORDER.index(name) - 1]
                act.wait_ge(*done_of(prev, BLOCKS[prev] - 1))

            def pair_stage(name, body, start=True, tail=0, before=None, after=None):
                if start:
                    stage_start(name)

                def step(k, i):
                    round_next(name, k, i)
                    if before:
                        before(k)
                    r = PAIR[name] + k
                    act.wait_ge(even_done, r + 1 + 4 * i)
                    body(k, i, bank[2 * (r % 2)])
                    if after:
                        after(k)
                each(act, BLOCKS[name], step, tail)

            def residual_stage(name):
                stage_start(name)
                each(act, BLOCKS[name], lambda k, i: round_next(name, k, i), 1)

            def copy(o, x):
                return nc.scalar.activation(o, x, ACT.Copy)

            def norm_root(name, n, size):
                j = NORM[name]
                act.wait_ge(ss_done, j + 1)
                nc.scalar.activation(acc[j % 2][:, 0:n], bank[6 + j % 2][:, 0:n], ACT.Sqrt, bias=eps[:, :],
                                     scale=1.0 / size).then_inc(sd_done, 1)

            def part(t, at, n, i=0, step=0):
                return t[:, at:at + n] if isinstance(i, int) else t[:, bass.ds(at + step * i, n)]

            def norm_hi(name, n, dst, size=D):
                if name != "f2":
                    norm_root(name, n, size)
                for c in range(dict(NORMS)[name]):
                    act.wait_ge(xf_done, SPLIT0[name] + c + 1)
                    copy(dst[0][:, c, 0:n], xf[c % 2][:, 0:n]).then_inc(xhi_done, 1)

            act.wait_ge(const_in, 80)
            act.wait_ge(pads, 1)
            lam = vecs[:, V_AT["lam"][0]:V_AT["lam"][0] + C]
            chain.link(nc.scalar.activation(lam_t[:, 0:C], lam, ACT.Abs))
            nc.scalar.activation(lam_t[:, 0:C], lam_t[:, 0:C], ACT.Exp, scale=-1.0).then_inc(lam_e, 1)
            round_block(0, TILE)
            norm_hi("n1", T, xn)

            def xr(k, i, ps):
                if k == 0:
                    act.wait_ge(pads, 2)
                copy(xrp[:, 2 * k, 3:3 + T], ps[:, 0:T]).then_inc(act_read, 1)

            def conv_parts(k):
                for c in (2 * k, 2 * k + 1):
                    act.wait_ge(conv_done, c + 1)
                    copy(conv[0][:, c, :], xc[:, c, :]).then_inc(conv_hi, 1)
            pair_stage("xr", xr, start=False, after=lambda k: conv_parts(k - 2) if k >= 2 else None)
            conv_parts(2)
            conv_parts(3)
            round_next("gates", 0)
            for c in range(C):
                r = PAIR["gates"] + c
                act.wait_ge(even_done, r + 1)
                nc.scalar.activation(r_t[:, c, :], bank[2 * (r % 2)][:, 0:T], ACT.Sigmoid, bias=vec("ba", c))\
                  .then_inc(act_read, 1)
            act.wait_ge(dve_read, PAIR["lat"])
            nc.scalar.activation(i_t[:, :, :], i_t[:, :, :], ACT.Sigmoid).then_inc(lru_act, 1)

            def lat(k, i, ps):
                dst = (ckvf[:, 0, :], kr_raw, cqf[:, 1, :])[k]
                src = ps[:, 0:T] if k < 2 else ps[:, META:T]
                copy(dst, src).then_inc(act_read, 1)

            def decay(k):
                if k == 0:
                    act.wait_ge(lam_c, 1)
                    act.wait_ge(act_read, PAIR["lat"])
                    for c in range(C):
                        last = nc.scalar.activation(a_t[:, c, :], r_t[:, c, :], ACT.Exp, scale=cl[:, c:c + 1])
                    last.then_inc(lru_act, 1)
                if k == 1:
                    act.wait_ge(lru_act, 2)
                    for c in range(C):
                        last = nc.scalar.activation(r_t[:, c, :], r_t[:, c, :], ACT.Tanh, scale=ncl[:, c:c + 1])
                    last.then_inc(lru_act, 1)
            pair_stage("lat", lat, before=decay)

            def gr_in(k, i, ps):
                copy(gr[:, 2 * k, :], ps[:, 0:S]).then_inc(act_read, 1)

            def root(k):
                if k == 1:
                    act.wait_ge(lru_dve, 1)
                    nc.scalar.activation(r_t[:, :, :], r_t[:, :, :], ACT.Sqrt).then_inc(lru_act, 1)
            pair_stage("gr", gr_in, before=root, after=lambda k: norm_hi("cq", S, cqn, QL) if k == 2 else None)
            act.wait_ge(act_read, PAIR["uq"])
            act.wait_ge(dve_read, PAIR["uq"])
            nc.scalar.activation(gr[:, :, :], gr[:, :, :], ACT.Gelu_apprx_tanh).then_inc(lru_act, 1)
            round_next("uq", 0)
            norm_hi("ckv", T, ckvn, KVL)
            act.wait_ge(y_f, 1)
            copy(y_rnn[0], gr[:, :, :]).then_inc(y_hi, 1)

            for k in range(4):
                if k:
                    round_next("uq", k)
                for c in (0, 2):
                    r = PAIR["uq"] + 2 * k + c // 2
                    act.wait_ge(even_done, r + 1)
                    ps = bank[2 * (r % 2)]
                    if k < 2:
                        m = 4 * k + c
                        copy(qh[0:64, 2 * m, :], ps[0:64, 0:S])
                        copy(qh[0:64, 2 * m + 1, :], ps[64:128, 0:S]).then_inc(act_read, 1)
                    else:
                        if r - PAIR["uq"] >= 5:
                            act.wait_ge(rope_in, 4 * (r - PAIR["uq"] - 4))
                        copy(sg[0], ps[:, 0:S]).then_inc(act_read, 1)
            round_next("uk", 0)
            for m in range(4):
                r = PAIR["uk"] + m
                act.wait_ge(even_done, r + 1)
                ps = bank[2 * (r % 2)]
                copy(kh[0:64, 4 * m, :], ps[0:64, 0:T])
                copy(kh[0:64, 4 * m + 1, :], ps[64:128, 0:T]).then_inc(act_read, 1)
            round_next("uv", 0)
            act.wait_ge(kr_ready, 1)
            for t in range(3):
                r = PAIR["uv"] + t
                act.wait_ge(even_done, r + 1)
                copy(vt[:, t, 0:512], bank[2 * (r % 2)][:, :]).then_inc(act_read, 1)
            stage_start("mix")


            def exps(h, i):
                u = h % 2
                p, s = probs[u], bank[4 + u]
                act.wait_ge(sc_masked, h + 1 + 4 * i)
                if h >= 2:
                    act.wait_ge(tr_done, h - 1 + 4 * i)
                for t, (at, n, dst) in enumerate(((0, SA, 0), (SA, SB, 256))):
                    nc.scalar.activation(p[:, dst:dst + n], s[:, at:at + n], ACT.Exp, bias=soft[:, 2 * u + t:2 * u + t + 1],
                                         accum_out=soft[:, 4 + 2 * u + t:5 + 2 * u + t]).then_inc(exp_done, 1)

            def copy_pt(h, i):
                u = h % 2
                act.wait_ge(tr_done, h + 1 + 4 * i)
                if h >= 2:
                    act.wait_ge(pv_done, h - 1 + 4 * i)
                copy(pt[u][:, 0:512], bank[6 + u][:, :]).then_inc(ptx, 1)
                if h >= 2 and h % 2 == 0:
                    take_o(h // 2 - 1, i)

            def take_o(m, i):
                act.wait_ge(pv_done, 2 * m + 2 + 4 * i)
                copy(part(op_hi, C * S + S * m, S, i, 2 * S), bank[m % 2][:, 0:S]).then_inc(o_hi, 1)

            def turn(t, i):
                for u in range(4):
                    exps(4 * t + u, i)
                    if 4 * t + u >= 1:
                        copy_pt(4 * t + u - 1, i)
            act.wait_ge(y_lo, 1)
            turn(0, 0)
            with act.Fori(0, 3) as i:
                turn(1, i)
            copy_pt(H - 1, 0)
            take_o(H // 2 - 1, 0)

            def mix(k, i, ps):
                r = PAIR["mix"] + k
                act.wait_ge(dve_read, r - 1 + 4 * i)
                nc.scalar.activation(sg[k % 2], ps[:, 0:S], ACT.Sigmoid).then_inc(act_read, 1)
                if k % 2:
                    act.wait_ge(mix_f, k // 2 + 1 + 2 * i)
                    copy(part(op_hi, 2 * C * S + S * (k // 2), S, i, 2 * S), xf[1][:, 0:S]).then_inc(mix_hi, 1)
            pair_stage("mix", mix, start=False)
            residual_stage("out1")
            if stop == "out1":
                return

            def norm_hi_of(name, src, dst):
                norm_root(name, S, D)
                for c in range(C):
                    act.wait_ge(xf_done, SPLIT0[name] + c + 1)
                    copy(dst[0][:, c, :], src[:, c, :]).then_inc(xhi_done, 1)
            norm_hi_of("n2", x_f, xq)
            def take_queries(h):
                act.wait_ge(q_done, h + 1)
                if h >= 2:
                    act.wait_ge(key_done, h - 1)
                copy(q_at[h], bank[h % 2][:, :]).then_inc(q_read, 1)

            def expert_weights(n):
                h, t = n // 2, n % 2
                act.wait_ge(top_max, n + 1)
                nc.scalar.activation(gw[h % 2][:, 16 * t:16 * t + 16], top["best"], ACT.Exp, bias=top["neg"],
                                     accum_out=top["sum"]).then_inc(top_exp, 1)

            def coefficient(n, s, i):
                q = TOPK * n + s
                i4 = 0 if isinstance(i, int) else 4 * i
                act.wait_ge(dot_done, q + 1 + i4)
                chain.link(nc.scalar.activation(coef[:, s % 4:s % 4 + 1], dots[:, s % 4:s % 4 + 1], ACT.Gelu_apprx_tanh))
                at = TOPK * (n % 2) + s
                g = gw[n // 2 % 2]
                weight = g[:, at:at + 1] if isinstance(i, int) else g[:, bass.ds(at + i4, 1)]
                chain.link(nc.scalar.activation(coef[:, 4 + s % 4:5 + s % 4], coef[:, s % 4:s % 4 + 1], ACT.Copy, scale=weight))
                if q >= 2:
                    act.wait_ge(row_used, q - 1 + i4)
                nc.scalar.activation(diag[s % 2], ident, ACT.Copy, scale=coef[:, 4 + s % 4:5 + s % 4]).then_inc(diag_done, 1)

            round_next("pq", 0)
            take_queries(0)
            for t in range(2):
                act.wait_ge(xt_ps, t + 1)
                copy(x_tok[:, t, 0:512], bank[4 + 2 * t][:, :]).then_inc(xt_read, 1)
            take_queries(1)
            round_next("pq", 1)
            expert_weights(0)
            for n in range(2 * PH):
                for s in range(8):
                    if n == 0 and s == 5:
                        expert_weights(1)
                    if n == 0:
                        coefficient(n, s, 0)
                if n > 0:
                    chain.loop(2, 8, lambda i: [coefficient(n, s, i) for s in range(4)])
                if n % 2 and n // 2 + 2 < PH:
                    take_queries(n // 2 + 2)
                if 1 <= n < 2 * PH - 2:
                    expert_weights(n + 2)
                for s in range(8, 16):
                    if n == 0 and s == 13:
                        expert_weights(2)
                    if n == 0:
                        coefficient(n, s, 0)
                if n > 0:
                    chain.loop(2, 8, lambda i: [coefficient(n, 8 + s, i) for s in range(4)])
                if n % 2 and n // 2 + 2 < PH:
                    round_next("pq", n // 2 + 2)
            for t in range(2):
                act.wait_ge(row_used, 16 * (2 * PH - 1 + t))
                copy(y_tok[:, t, 0:512], bank[4 + 2 * t][:, :]).then_inc(y_tok_act, 1)
            norm_root("final1", S, D)
            if stop == "pq":
                return

            def swiglu(f, norm, first=False):
                norm_hi(norm, S, xq)

                def up(k, i, ps):
                    r = PAIR[f"ffi{f}"] + k
                    act.wait_ge(dve_read, r - 1 + 4 * i)
                    nc.scalar.activation(sg[k % 2], ps[:, 0:S], ACT.Silu).then_inc(act_read, 1)
                    act.wait_ge(dve_read, r + 1 + 4 * i)
                    copy(part(op_hi, S * k, S, i, 4 * S), xf[k % 2][:, 0:S]).then_inc(in_hi, 1)
                pair_stage(f"ffi{f}", up)
                residual_stage(f"ffo{f}")

            swiglu(0, "f0")
            if stop == "ffo0":
                return
            norm_hi("mix0", S, xq)

            def qk_in(k, i, ps):
                copy(part(arena, 2 * S * k, S, i, 8 * S), ps[:, 0:S]).then_inc(act_read, 1)
            pair_stage("qk", qk_in)
            stage_start("sbv")
            for k in range(4):
                round_next("sbv", k)
            for t in range(2):
                r = PAIR["sbv"] + t
                act.wait_ge(even_done, r + 1)
                copy(sv[:, t, 0:512], bank[2 * (r % 2)][:, :]).then_inc(act_read, 1)

            def softplus(h, i):
                a = az[h % 2]
                act.wait_ge(z_mask, h + 1 + 4 * i)
                chain.link(nc.scalar.activation(a, a, ACT.Exp))
                nc.scalar.activation(a, a, ACT.Ln, bias=1.0).then_inc(soft_in, 1)

            def weights(h, i):
                act.wait_ge(arg_done, h + 1 + 4 * i)
                if h >= 2:
                    act.wait_ge(sbo_done, h - 1 + 4 * i)
                nc.scalar.activation(wt[h % 2], zm[h % 4], ACT.Exp).then_inc(w_done, 1)
                if h >= 3 and h % 2 == 1:
                    sb_take((h - 3) // 2, i)

            def sb_take(m, i):
                act.wait_ge(sbo_done, 2 * m + 2 + 4 * i)
                copy(part(op_hi, S * m, S, i, 2 * S), bank[m % 2][:, 0:S]).then_inc(sbo_hi, 1)

            def sb_turn(t, i):
                for u in range(4):
                    softplus(4 * t + u, i)
                    if 4 * t + u >= 2:
                        weights(4 * t + u - 2, i)
            sb_turn(0, 0)
            chain.loop(3, 4, lambda i: sb_turn(1, i))
            weights(H - 2, 0)
            weights(H - 1, 0)
            sb_take(H // 2 - 1, 0)
            residual_stage("sbo")
            if stop == "sbo":
                return
            swiglu(1, "f1")
            norm_hi("kv", S, xq)
            pair_stage("kvk", lambda k, i, ps: copy(k_raw[:, 0, :], ps[:, 0:S]).then_inc(act_read, 1))
            pair_stage("kvv", lambda k, i, ps: copy(v_sh[:, 0, :], ps[:, 0:S]).then_inc(act_read, 1))
            swiglu(2, "f2")
            norm_hi("mix1", S, xq)
            pair_stage("sq", lambda k, i, ps: copy(q_sw[:, 2 * k, :], ps[:, 0:S]).then_inc(act_read, 1))
            act.wait_ge(k_rot, 2)

            def sink(h, i):
                act.wait_ge(w_sc, h + 1 + 4 * i)
                src = sinks[:, h:h + 1] if isinstance(i, int) else soft[:, bass.ds(25 + h + 4 * i, 1)]
                copy(four[h % 4][:, P:P + 1], src).then_inc(sink_in, 1)

            def sw_exps(h, i):
                u = h % 4
                act.wait_ge(w_mask, h + 1 + 4 * i)
                if h >= 4:
                    act.wait_ge(w_tr, h - 3 + 4 * i)
                for t, (at, n, dst) in enumerate(((0, P + 1, 0), (P, S + 1, P + 1))):
                    nc.scalar.activation(sw_p[u][:, dst:dst + n], four[u][:, at:at + n], ACT.Exp,
                                         bias=soft[:, 2 * u + t:2 * u + t + 1],
                                         accum_out=soft[:, 8 + 2 * u + t:9 + 2 * u + t]).then_inc(w_exp, 1)

            def sw_copy(h, i):
                act.wait_ge(w_tr, h + 1 + 4 * i)
                if h >= 2:
                    act.wait_ge(w_pv, h - 1 + 4 * i)
                copy(sw_pt[h % 2], bank[6 + h % 2][:, 0:384]).then_inc(w_pt, 1)
                if h >= 2 and h % 2 == 0:
                    sw_take(h // 2 - 1, i)

            def sw_take(m, i):
                act.wait_ge(w_pv, 2 * m + 2 + 4 * i)
                copy(part(op_hi, S * m, S, i, 2 * S), bank[m % 2][:, 0:S]).then_inc(w_hi_o, 1)

            def sw_head(h, i):
                sw_exps(h, i)
                sink(h + 2, i)
                if h >= 1:
                    sw_copy(h - 1, i)
            sink(0, 0)
            sink(1, 0)
            for h in range(4):
                sw_head(h, 0)
            with act.Fori(0, 2) as i:
                for h in range(4, 8):
                    sw_head(h, i)
            for h in range(H - 4, H):
                sw_exps(h, 0)
                if h + 2 < H:
                    sink(h + 2, 0)
                sw_copy(h - 1, 0)
            sw_copy(H - 1, 0)
            sw_take(H // 2 - 1, 0)
            residual_stage("swo")
            swiglu(3, "f3")
            norm_root("final2", S, D)

        @block.vector
        def _(dve):
            v = nc.vector
            chain = Chain(dve, dve_step)
            link = chain.link

            def part(t, at, n, i=0, step=0):
                return t[:, at:at + n] if isinstance(i, int) else t[:, bass.ds(at + step * i, n)]

            def rest_of_block(b, cols, i=0):
                dve.wait_ge(hi_done, b + 1 + 4 * i)
                v.tensor_tensor(w_lo[b % 2][:, 0:cols], raw[b % RAW][:, 0:cols], w_hi[b % 2][:, 0:cols].bitcast(F32),
                                ALU.subtract).then_inc(lo_done, 1)

            def rest_next(name, k, i=0):
                b = FIRST[name] + k + 1
                if b >= END or (name == stop and k == BLOCKS[name] - 1 and isinstance(i, int)):
                    return
                nxt = name if k + 1 < BLOCKS[name] else ORDER[ORDER.index(name) + 1]
                rest_of_block(b, WIDTH[nxt], i)

            def pair_stage(name, body, tail=0, after=None):
                def step(k, i):
                    rest_next(name, k, i)
                    r = PAIR[name] + k
                    dve.wait_ge(odd_done, r + 1 + 4 * i)
                    body(k, i, bank[2 * (r % 2) + 1])
                    if after:
                        after(k)
                each(dve, BLOCKS[name], step, tail)

            def square_sum(name, src, n, c, count):
                j = NORM[name]
                a = acc[j % 2][:, 0:n]
                if c == 0:
                    ins = v.tensor_tensor(a, src, src, ALU.mult)
                else:
                    link(v.tensor_tensor(xf[0][:, 0:n], src, src, ALU.mult))
                    ins = v.tensor_tensor(a, a, xf[0][:, 0:n], ALU.add)
                if c == count - 1:
                    ins.then_inc(ss_in, 1)
                else:
                    link(ins)

            def norm_apply(name, src, n, dst, full=None):
                def whole(c):
                    return xf[c % 2][:, 0:n] if full is None else full[:, c, :]
                j, s0 = NORM[name], SPLIT0[name]
                a = acc[j % 2][:, 0:n]
                if name != "f2":
                    dve.wait_ge(sd_done, j + 1)
                    v.reciprocal(a, a).then_inc(rs_done, 1)
                    dve.wait_ge(rs_done, j + 1)
                count = dict(NORMS)[name]

                def rest(c):
                    dve.wait_ge(xhi_done, s0 + c + 1)
                    v.tensor_tensor(dst[1][:, c, 0:n], whole(c), dst[0][:, c, 0:n].bitcast(F32), ALU.subtract)\
                     .then_inc(xlo_done, 1)
                for c in range(count):
                    if c >= 2:
                        rest(c - 2)
                        dve.wait_ge(xlo_done, s0 + c - 1)
                    v.scalar_tensor_tensor(whole(c), src[:, c, :], vec(name, c), a, ALU.mult, ALU.mult)\
                     .then_inc(xf_done, 1)
                for c in range(max(0, count - 2), count):
                    rest(c)
                dve.wait_ge(xlo_done, s0 + count)

            def residual_stage(name, norm, scale=1.0):
                j = NORM[norm]
                a = acc[j % 2][:, 0:S]
                link(v.memset(a, 0.0))
                blocks = BLOCKS[name] // C if BLOCKS[name] > C else 1
                per = 1 if blocks == 2 else 2

                def step(k, i):
                    rest_next(name, k, i)
                    if blocks == 2 and k % 2 == 0:
                        return
                    for c in range(per):
                        m = per * k + c if blocks == 1 else k // 2
                        n = RES[name] + m
                        dve.wait_ge(res_done, n + 1 + 2 * i)
                        hc = h_t[:, m, META:T] if isinstance(i, int) else h_all[:, bass.ds(T * m + META + 2 * T * i, S)]
                        v.scalar_tensor_tensor(hc, bank[4 + n % 2][:, 0:S], scale, hc, ALU.mult, ALU.add).then_inc(h_new, 1)
                        dve.wait_ge(h_new, n + 1 + 2 * i)
                        link(v.tensor_tensor(xf[0][:, 0:S], hc, hc, ALU.mult))
                        ins = v.tensor_tensor(a, a, xf[0][:, 0:S], ALU.add)
                        if m == C - 1 and isinstance(i, int):
                            ins.then_inc(ss_in, 1)
                        else:
                            link(ins)
                turns = 0 if blocks == 1 else (BLOCKS[name] - 1) // RAW
                if turns:
                    chain.loop(turns, 4, lambda i: [step(k, i) for k in range(RAW)])
                for k in range(RAW * turns, BLOCKS[name]):
                    step(k, 0)

            dve.wait_ge(const_in, 80)
            dve.wait_ge(lam_e, 1)
            e, z, z2, q, lam = (lam_t[:, C * n:C * n + C] for n in (0, 2, 3, 4, 5))
            link(v.tensor_scalar(z2, e, 2.0, None, ALU.add))
            link(v.reciprocal(z2, z2))
            link(v.tensor_tensor(z, z2, e, ALU.mult))
            link(v.tensor_tensor(z2, z, z, ALU.mult))
            link(v.tensor_scalar(q, z2, 1.0 / 17, None, ALU.mult))
            for n in (15, 13, 11, 9, 7, 5, 3):
                link(v.scalar_tensor_tensor(q, q, 1.0 / n, z2, ALU.add, ALU.mult))
            link(v.scalar_tensor_tensor(q, q, 1.0, z, ALU.add, ALU.mult))
            link(v.tensor_scalar(lam, vecs[:, V_AT["lam"][0]:V_AT["lam"][0] + C], -1.0, 0.0, ALU.mult, ALU.max))
            link(v.scalar_tensor_tensor(lam, q, 2.0, lam, ALU.mult, ALU.add))
            v.tensor_scalar(ncl, lam, 8.0, None, ALU.mult).then_inc(lam_c, 1)
            v.tensor_scalar(cl, lam, -8.0, None, ALU.mult).then_inc(lam_c, 1)

            dve.wait_ge(x_in, 16)
            for c in range(C):
                square_sum("n1", h_t[:, c, :], T, c, C)
            rest_of_block(0, TILE)
            norm_apply("n1", h_t, T, xn)

            def xr(k, i, ps):
                v.tensor_copy(xrp[:, 2 * k + 1, 3:3 + T], ps[:, 0:T]).then_inc(dve_read, 1)

            def convolve(k):
                dve.wait_ge(act_read, PAIR["xr"] + k + 1)
                dve.wait_ge(dve_read, PAIR["xr"] + k + 1)
                dve.wait_ge(pads, 2)
                for c in (2 * k, 2 * k + 1):
                    y = xc[:, c, :]
                    link(v.tensor_scalar(y, xrp[:, c, 0:T], vec("cw0", c), vec("cb", c), ALU.mult, ALU.add))
                    for t in (1, 2, 3):
                        ins = v.scalar_tensor_tensor(y, xrp[:, c, t:t + T], vec(f"cw{t}", c), y, ALU.mult, ALU.add)
                        ins.then_inc(conv_done, 1) if t == 3 else link(ins)

            def conv_rest(k):
                for c in (2 * k, 2 * k + 1):
                    dve.wait_ge(conv_hi, c + 1)
                    v.tensor_tensor(conv[1][:, c, :], xc[:, c, :], conv[0][:, c, :].bitcast(F32), ALU.subtract)\
                     .then_inc(conv_lo, 1)

            def after_xr(k):
                if k >= 1:
                    convolve(k - 1)
                if k >= 2:
                    conv_rest(k - 2)
            pair_stage("xr", xr, after=after_xr)
            convolve(3)
            conv_rest(2)
            conv_rest(3)
            rest_next("gates", 0)
            for c in range(C):
                r = PAIR["gates"] + c
                dve.wait_ge(odd_done, r + 1)
                v.tensor_scalar(i_t[:, c, :], bank[2 * (r % 2) + 1][:, 0:T], vec("bx", c), None, ALU.add)\
                 .then_inc(dve_read, 1)

            def lat(k, i, ps):
                dst = (ckvf[:, 1, :], cqf[:, 0, :], cqf[:, 2, :])[k]
                v.tensor_copy(dst, ps[:, 0:T] if k < 1 else ps[:, META:T]).then_inc(dve_read, 1)
            pair_stage("lat", lat)

            def recurrence(k):
                if k == 0:
                    dve.wait_ge(lru_act, 3)
                    dve.wait_ge(lru_pool, 2)
                    v.scalar_tensor_tensor(r_t[:, :, :], xc[:, :, :], 1.0, r_t[:, :, :], ALU.add, ALU.mult)\
                     .then_inc(lru_dve, 1)
                    dve.wait_ge(dve_read, PAIR["gr"])
                    dve.wait_ge(act_read, PAIR["gr"])
                    for c in range(3):
                        square_sum("cq", cqf[:, c, :], S, c, 3)
                    for c in range(2):
                        square_sum("ckv", ckvf[:, c, :], T, c, 2)
                if k == 1:
                    dve.wait_ge(lru_act, 4)
                    link(v.tensor_tensor(i_t[:, :, :], i_t[:, :, :], r_t[:, :, :], ALU.mult))
                    for c in range(C):
                        ins = v.tensor_tensor_scan(xc[:, c, :], a_t[:, c, :], i_t[:, c, :], 0.0, ALU.mult, ALU.add)
                    link(ins)
                if k == 2:
                    dve.wait_ge(pads, 4)
                    norm_apply("cq", cqf, S, cqn)

            def gr_in(k, i, ps):
                v.tensor_copy(gr[:, 2 * k + 1, :], ps[:, 0:S]).then_inc(dve_read, 1)
            pair_stage("gr", gr_in, after=recurrence)
            dve.wait_ge(lru_act, 5)
            v.tensor_tensor(gr[:, :, :], gr[:, :, :], xc[:, :, META:T], ALU.mult).then_inc(y_f, 1)
            rest_next("uq", 0)
            norm_apply("ckv", ckvf, T, ckvn)
            link(v.tensor_tensor(kr_rot[0:32, :], kr_raw[0:32, :], cos_t[0:32, :], ALU.mult))
            link(v.tensor_tensor(xf[0][0:32, :], kr_raw[32:64, :], sin_t[32:64, :], ALU.mult))
            link(v.tensor_tensor(kr_rot[0:32, :], kr_rot[0:32, :], xf[0][0:32, :], ALU.add))
            for g in range(H // 8):
                ins = v.tensor_copy(kh[64:96, 8 * g:8 * g + 8, :],
                                    kr_rot[0:32, :].unsqueeze(1).to_broadcast([32, 8, T]))
            ins.then_inc(kr_ready, 1)
            dve.wait_ge(y_hi, 1)
            v.tensor_tensor(y_rnn[1], gr[:, :, :], y_rnn[0].bitcast(F32), ALU.subtract).then_inc(y_lo, 1)

            for k in range(4):
                if k:
                    rest_next("uq", k)
                for c in (1, 3):
                    r = PAIR["uq"] + 2 * k + c // 2
                    dve.wait_ge(odd_done, r + 1)
                    ps = bank[2 * (r % 2) + 1]
                    if k < 2:
                        m = 4 * k + c
                        v.tensor_copy(qh[0:64, 2 * m, :], ps[0:64, 0:S])
                        v.tensor_copy(qh[0:64, 2 * m + 1, :], ps[64:128, 0:S]).then_inc(dve_read, 1)
                    else:
                        g = r - PAIR["uq"] - 4
                        v.tensor_tensor(sg[1], ps[:, 0:S], sin_t[:, META:T], ALU.mult).then_inc(dve_read, 1)
                        dve.wait_ge(act_read, r + 1)
                        link(v.tensor_tensor(xf[0][:, 0:S], sg[0], cos_t[:, META:T], ALU.mult))
                        dve.wait_ge(dve_read, r + 1)
                        for a in range(4):
                            rows = slice(32 * a, 32 * a + 32)
                            v.tensor_tensor(qh[64:96, 4 * g + a, :], xf[0][rows, 0:S], sg[1][rows, :], ALU.add)\
                             .then_inc(rope_in, 1)
                        dve.wait_ge(rope_in, 4 * g + 4)
            rest_next("uk", 0)
            for m in range(4):
                r = PAIR["uk"] + m
                dve.wait_ge(odd_done, r + 1)
                ps = bank[2 * (r % 2) + 1]
                v.tensor_copy(kh[0:64, 4 * m + 2, :], ps[0:64, 0:T])
                v.tensor_copy(kh[0:64, 4 * m + 3, :], ps[64:128, 0:T]).then_inc(dve_read, 1)
            for t in range(3):
                r = PAIR["uv"] + t
                dve.wait_ge(odd_done, r + 1)
                v.tensor_copy(vt[:, t, 512:1024], bank[2 * (r % 2) + 1][:, :]).then_inc(dve_read, 1)
            rest_next("uv", 0)
            dve.wait_ge(y_lo, 1)
            for p in probs:
                link(v.memset(p[:, SA:S], 0.0))
                link(v.memset(p[:, S + SB:640], 0.0))

            def mask(h, i):
                u = h % 2
                s = bank[4 + u]
                dve.wait_ge(sc_done, h + 1 + 4 * i)
                link(v.scalar_tensor_tensor(s[:, 0:416], s[:, 0:416], MLA_SCALE, mla_mask, ALU.mult, ALU.add))
                link(v.tensor_reduce(soft[:, 2 * u:2 * u + 1], s[:, 0:SA], AX.X, ALU.max, negate=True))
                v.tensor_reduce(soft[:, 2 * u + 1:2 * u + 2], s[:, SA:SA + SB], AX.X, ALU.max, negate=True)\
                 .then_inc(sc_masked, 1)

            def normalise(h, i):
                u = h % 2
                p = probs[u]
                dve.wait_ge(exp_done, 2 * h + 2 + 8 * i)
                link(v.reciprocal(soft[:, 8 + 2 * u:10 + 2 * u], soft[:, 4 + 2 * u:6 + 2 * u]))
                v.tensor_scalar(p[:, 0:SA], p[:, 0:SA], soft[:, 8 + 2 * u:9 + 2 * u], None, ALU.mult).then_inc(p_ready, 1)
                v.tensor_scalar(p[:, 256:256 + SB], p[:, 256:256 + SB], soft[:, 9 + 2 * u:10 + 2 * u], None, ALU.mult)\
                 .then_inc(p_ready, 1)

            def copy_fifth(h, i):
                u = h % 2
                dve.wait_ge(tr_done, h + 1 + 4 * i)
                if h >= 2:
                    dve.wait_ge(pv_done, h - 1 + 4 * i)
                v.tensor_copy(pt[u][:, 512:640], bank[2 + u][:, 0:P]).then_inc(pty, 1)
                if h >= 2 and h % 2 == 0:
                    rest_o(h // 2 - 1, i)

            def rest_o(m, i):
                dve.wait_ge(o_hi, m + 1 + 2 * i)
                v.tensor_tensor(part(op_lo, C * S + S * m, S, i, 2 * S), bank[m % 2][:, 0:S],
                                part(op_hi, C * S + S * m, S, i, 2 * S).bitcast(F32), ALU.subtract).then_inc(o_lo, 1)

            def turn(t, i):
                for u in range(4):
                    mask(4 * t + u, i)
                    if 4 * t + u >= 1:
                        normalise(4 * t + u - 1, i)
                    if 4 * t + u >= 2:
                        copy_fifth(4 * t + u - 2, i)
            turn_links = 12
            turn(0, 0)
            chain.loop(3, turn_links, lambda i: turn(1, i))
            normalise(H - 1, 0)
            copy_fifth(H - 2, 0)
            copy_fifth(H - 1, 0)
            rest_o(H // 2 - 1, 0)

            def mix(k, i, ps):
                r = PAIR["mix"] + k
                dve.wait_ge(act_read, r + 1 + 4 * i)
                if k % 2 == 0:
                    v.tensor_tensor(xf[0][:, 0:S], sg[0], ps[:, 0:S], ALU.mult).then_inc(dve_read, 1)
                    return
                v.tensor_tensor(acc[0][:, 0:S], sg[1], ps[:, 0:S], ALU.mult).then_inc(dve_read, 1)
                dve.wait_ge(dve_read, r + 1 + 4 * i)
                v.tensor_tensor(xf[1][:, 0:S], xf[0][:, 0:S], acc[0][:, 0:S], ALU.add).then_inc(mix_f, 1)
                dve.wait_ge(mix_hi, k // 2 + 1 + 2 * i)
                at = 2 * C * S + S * (k // 2)
                v.tensor_tensor(part(op_lo, at, S, i, 2 * S), xf[1][:, 0:S], part(op_hi, at, S, i, 2 * S).bitcast(F32),
                                ALU.subtract).then_inc(mix_lo, 1)
                dve.wait_ge(mix_lo, k // 2 + 1 + 2 * i)
            pair_stage("mix", mix)
            residual_stage("out1", "n2")
            if stop == "out1":
                return

            norm_apply("n2", hs, S, xq, full=x_f)
            def top16(values, n, best, index, left):
                link(v.max(best[:, 0:8], values))
                yield
                link(v.max_index(index[:, 0:8], best[:, 0:8], values))
                yield
                link(v.match_replace(left, best[:, 0:8], values, -3.0e38))
                yield
                link(v.max(best[:, 8:16], left))
                yield
                link(v.max_index(index[:, 8:16], best[:, 8:16], left))
                yield

            iota = small[:, 0:TOPK]

            def pick(dst, which, values):
                hit = top["hit"].rearrange("p (k a) -> p k a", a=TOPK)
                link(v.tensor_tensor(hit, which.unsqueeze(2).to_broadcast([P, TOPK, TOPK]),
                                     iota.unsqueeze(1).to_broadcast([P, TOPK, TOPK]), ALU.is_equal))
                yield
                link(v.tensor_tensor(hit, hit, values.unsqueeze(1).to_broadcast([P, TOPK, TOPK]), ALU.mult))
                yield
                link(v.tensor_reduce(dst, hit, AX.X, ALU.add))
                yield

            def experts(n):
                h, t = n // 2, n % 2
                ps = bank[2 + h % 2]
                dve.wait_ge(key_done, h + 1)
                for c, (tv, ti, tf) in enumerate((("t1", "i1", "f1"), ("t2", "i2", "f2"))):
                    yield from top16(ps[:, P * (2 * t + c):P * (2 * t + c + 1)], NKEY, top[tv], top[ti].bitcast(U32), top["s"])
                    link(v.tensor_copy(top[tf], top[ti].bitcast(U32)))
                    yield
                cand = top["cand"].rearrange("p (a b) -> p a b", b=TOPK)
                link(v.tensor_tensor(cand, top["t1"].unsqueeze(2).to_broadcast([P, TOPK, TOPK]),
                                     top["t2"].unsqueeze(1).to_broadcast([P, TOPK, TOPK]), ALU.add))
                yield
                if n >= 1:
                    dve.wait_ge(top_exp, n)
                yield from top16(top["cand"], 256, top["best"], top["at"].bitcast(U32), top["left"])
                v.tensor_scalar(top["neg"], top["best"][:, 0:1], -1.0, None, ALU.mult).then_inc(top_max, 1)
                for to, op, by, f in (("hi", ALU.logical_shift_right, 4, "fh"), ("lo", ALU.bitwise_and, 15, "fl")):
                    link(v.tensor_scalar(top[to].bitcast(U32), top["at"].bitcast(U32), by, None, op))
                    yield
                    link(v.tensor_copy(top[f], top[to].bitcast(U32)))
                    yield
                yield from pick(top["e1"], top["fh"], top["f1"])
                yield from pick(top["e2"], top["fl"], top["f2"])
                if n >= 4:
                    dve.wait_ge(row_used, TOPK * (n - 3))
                dve.wait_ge(top_exp, n + 1)
                link(v.reciprocal(top["rs"], top["sum"]))
                yield
                g = gw[h % 2][:, 16 * t:16 * t + 16]
                link(v.tensor_scalar(g, g, top["rs"], None, ALU.mult))
                yield
                v.scalar_tensor_tensor(expert[h % 2][:, 16 * t:16 * t + 16], top["e1"], float(NKEY), top["e2"],
                                       ALU.mult, ALU.add).then_inc(expert_in, 1)
                dve.wait_ge(expert_in, n + 1)

            def dot(n, s, i):
                q = 16 * n + s
                i4 = 0 if isinstance(i, int) else 4 * i
                turns = q // 4 + 1
                dve.wait_ge(gathered[s % 4], 16 * turns + (0 if isinstance(i, int) else 16 * i))
                if q >= 1:
                    dve.wait_ge(dot_done, q + i4)
                v.tensor_tensor_reduce(out=product, in0=pulled[s % 4][:, 0:D], in1=x_tok[:, n % 2, :], scale=1.0, scalar=0.0,
                                       op0=ALU.mult, op1=ALU.add, accum_out=dots[:, s % 4:s % 4 + 1]).then_inc(dot_done, 1)

            def advance(steps, count):
                for _ in range(count):
                    next(steps, None)

            rest_next("pq", 0)
            advance(experts(0), 40)
            for t in range(2):
                dve.wait_ge(xt_ps, t + 1)
                v.tensor_copy(x_tok[:, t, 512:D], bank[5 + 2 * t][:, :]).then_inc(xt_read, 1)
            dve.wait_ge(xt_read, 4)
            rest_next("pq", 1)
            for n in range(2 * PH):
                if n < 2 * PH - 2:
                    steps = experts(1 if n == 0 else n + 2)
                    for s in range(TOPK):
                        if n == 0 and s == 8:
                            steps = experts(2)
                        dot(n, s, 0)
                        advance(steps, 5 if n == 0 else 3)
                else:
                    with dve.Fori(0, 4) as i:
                        for s in range(4):
                            dot(n, s, i)
                if n % 2 and n // 2 + 2 < PH:
                    rest_next("pq", n // 2 + 2)
            for t in range(2):
                dve.wait_ge(row_used, 16 * (2 * PH - 1 + t))
                v.tensor_copy(y_tok[:, t, 512:D], bank[5 + 2 * t][:, :]).then_inc(y_tok_dve, 1)
            dve.wait_ge(y_back, 1)
            a = acc[NORM["final1"] % 2][:, 0:S]
            link(v.memset(a, 0.0))
            for c in range(C):
                hc = hs[:, c, :]
                v.tensor_tensor(hc, hc, bank[c // 2][:, S * (c % 2):S * (c % 2) + S], ALU.add).then_inc(peer_h, 1)
                dve.wait_ge(peer_h, c + 1)
                link(v.tensor_tensor(xf[0][:, 0:S], hc, hc, ALU.mult))
                ins = v.tensor_tensor(a, a, xf[0][:, 0:S], ALU.add)
                ins.then_inc(ss_in, 1) if c == C - 1 else link(ins)
            def norm_in_place(name):
                j = NORM[name]
                a = acc[j % 2][:, 0:S]
                dve.wait_ge(sd_done, j + 1)
                v.reciprocal(a, a).then_inc(rs_done, 1)
                dve.wait_ge(rs_done, j + 1)
                for c in range(C):
                    v.scalar_tensor_tensor(hs[:, c, :], hs[:, c, :], vec(name, c), a, ALU.mult, ALU.mult).then_inc(h_scaled, 1)

            norm_in_place("final1")
            if stop == "pq":
                return
            for c in range(C):
                dve.wait_ge(h_scaled, c + 1)
                square_sum("f0", hs[:, c, :], S, c, C)

            def swiglu(f, norm, following, between=None):
                norm_apply(norm, hs, S, xq)
                if between:
                    between()

                def up(k, i, ps):
                    r, n = PAIR[f"ffi{f}"] + k, NF * f + k
                    dve.wait_ge(act_read, r + 1 + 4 * i)
                    v.tensor_tensor(xf[k % 2][:, 0:S], sg[k % 2], ps[:, 0:S], ALU.mult).then_inc(dve_read, 1)
                    dve.wait_ge(in_hi, n + 1 + 4 * i)
                    v.tensor_tensor(part(op_lo, S * k, S, i, 4 * S), xf[k % 2][:, 0:S],
                                    part(op_hi, S * k, S, i, 4 * S).bitcast(F32), ALU.subtract).then_inc(in_lo, 1)
                    dve.wait_ge(in_lo, n + 1 + 4 * i)
                pair_stage(f"ffi{f}", up)
                residual_stage(f"ffo{f}", following, 0.5)

            swiglu(0, "f0", "mix0")
            if stop == "ffo0":
                return
            norm_apply("mix0", hs, S, xq)

            def qk_in(k, i, ps):
                v.tensor_scalar(part(arena, 2 * S * k + S, S, i, 8 * S), ps[:, 0:S], 1.0, None, ALU.mult).then_inc(dve_read, 1)
            pair_stage("qk", qk_in)
            for k in range(4):
                rest_next("sbv", k)
            for t in range(2):
                r = PAIR["sbv"] + t
                dve.wait_ge(odd_done, r + 1)
                v.tensor_copy(sv[:, t, 512:D], bank[2 * (r % 2) + 1][:, :]).then_inc(dve_read, 1)
            dve.wait_ge(tables2_in, 16)

            def masked_logits(h, i):
                u = h % 4
                dve.wait_ge(z_done, h + 1 + 4 * i)
                if h >= 4:
                    dve.wait_ge(w_done, h - 3 + 4 * i)
                link(v.scalar_tensor_tensor(zm[u], four[u][:, 0:384], SCALE, sb_mask, ALU.mult, ALU.add))
                if h >= 2:
                    dve.wait_ge(sp_done, h - 1 + 4 * i)
                v.scalar_tensor_tensor(az[u % 2], zm[u], -1.0, zm[u], ALU.mult, ALU.min).then_inc(z_mask, 1)

            def exponents(h, i):
                u = h % 4
                dve.wait_ge(suf_done, h + 1 + 4 * i)
                v.tensor_tensor(zm[u], zm[u], bank[6 + u % 2][:, 0:384], ALU.subtract).then_inc(arg_done, 1)

            def softplus(h, i):
                u = h % 4
                dve.wait_ge(soft_in, h + 1 + 4 * i)
                if h >= 2:
                    dve.wait_ge(suf_done, h - 1 + 4 * i)
                v.scalar_tensor_tensor(sp_t[u % 2], zm[u], 0.0, az[u % 2], ALU.max, ALU.add).then_inc(sp_done, 1)

            def sb_rest(m, i):
                dve.wait_ge(sbo_hi, m + 1 + 2 * i)
                v.tensor_tensor(part(op_lo, S * m, S, i, 2 * S), bank[m % 2][:, 0:S],
                                part(op_hi, S * m, S, i, 2 * S).bitcast(F32), ALU.subtract).then_inc(sbo_lo, 1)

            def sb_head(h, i):
                if h + 1 < H:
                    masked_logits(h + 1, i)
                if h >= 1:
                    exponents(h - 1, i)
                softplus(h, i)
                if h >= 5 and h % 2:
                    sb_rest((h - 5) // 2, i)

            masked_logits(0, 0)
            for h in range(4):
                sb_head(h, 0)
            chain.loop(2, 4, lambda i: [sb_head(4 + u, i) for u in range(4)])
            for h in range(H - 4, H):
                sb_head(h, 0)
            exponents(H - 1, 0)
            sb_rest(H // 2 - 2, 0)
            sb_rest(H // 2 - 1, 0)
            residual_stage("sbo", "f1")
            if stop == "sbo":
                return
            swiglu(1, "f1", "kv")
            norm_apply("kv", hs, S, xq)
            pair_stage("kvk", lambda k, i, ps: v.tensor_copy(k_raw[:, 1, :], ps[:, 0:S]).then_inc(dve_read, 1))
            pair_stage("kvv", lambda k, i, ps: v.tensor_copy(v_sh[:, 1, :], ps[:, 0:S]).then_inc(dve_read, 1))

            def rotate_keys():
                dve.wait_ge(act_read, PAIR["kvk"] + 1)
                dve.wait_ge(dve_read, PAIR["kvk"] + 1)
                for base in (0, 64):
                    for dst, src in ((base, base + 32), (base + 32, base)):
                        v.tensor_copy(k_sh[dst:dst + 32, :, :], k_raw[src:src + 32, :, :]).then_inc(k_half, 1)
                dve.wait_ge(k_half, 4)
                both = lambda x: x.unsqueeze(1).to_broadcast([P, 2, S])
                link(v.tensor_tensor(k_sh[:, :, :], k_sh[:, :, :], both(sin2), ALU.mult))
                link(v.tensor_tensor(k_raw[:, :, :], k_raw[:, :, :], both(cos2), ALU.mult))
                v.tensor_tensor(k_sh[:, :, :], k_sh[:, :, :], k_raw[:, :, :], ALU.add).then_inc(k_rot, 1)
                v.tensor_scalar(sinks, small[:, TOPK:TOPK + H], 1.0 / SCALE, None, ALU.mult).then_inc(k_rot, 1)
            swiglu(2, "f2", "mix1", rotate_keys)
            norm_apply("mix1", hs, S, xq)

            def rotate_queries(k):
                dve.wait_ge(q_swap, k + 1)
                q, t = q_sw[:, 2 * k:2 * k + 2, :], q_half[:, 2 * k:2 * k + 2, :]
                both = lambda x: x.unsqueeze(1).to_broadcast([P, 2, S])
                swapped = bank[4 + k % 2].rearrange("p (c t) -> p c t", t=S)
                link(v.tensor_tensor(t, swapped, both(sin2), ALU.mult))
                link(v.tensor_tensor(q, q, both(cos2), ALU.mult))
                v.tensor_tensor(q, q, t, ALU.add).then_inc(q_rot, 1)

            def sq_in(k, i, ps):
                v.tensor_copy(q_sw[:, 2 * k + 1, :], ps[:, 0:S]).then_inc(dve_read, 1)
                if k:
                    rotate_queries(k - 1)
            pair_stage("sq", sq_in)
            rotate_queries(3)

            def sw_mask(h, i):
                u = h % 4
                s_ = four[u][:, 0:385]
                dve.wait_ge(sink_in, h + 1 + 4 * i)
                link(v.scalar_tensor_tensor(s_, s_, SCALE, swa_mask, ALU.mult, ALU.add))
                v.tensor_reduce(soft[:, 2 * u:2 * u + 1], s_[:, 0:P + 1], AX.X, ALU.max, negate=True)
                v.tensor_reduce(soft[:, 2 * u + 1:2 * u + 2], s_[:, P:P + 1 + S], AX.X, ALU.max, negate=True)\
                 .then_inc(w_mask, 1)

            def sw_normalise(h, i):
                u = h % 4
                dve.wait_ge(w_exp, 2 * h + 2 + 8 * i)
                link(v.reciprocal(soft[:, 16 + 2 * u:18 + 2 * u], soft[:, 8 + 2 * u:10 + 2 * u]))
                for t, (at, n) in enumerate(((0, P + 1), (P + 1, S + 1))):
                    p = sw_p[u][:, at:at + n]
                    v.tensor_scalar(p, p, soft[:, 16 + 2 * u + t:17 + 2 * u + t], None, ALU.mult).then_inc(w_p, 1)
                if h >= 3 and h % 2 == 1:
                    sw_rest((h - 3) // 2, i)

            def sw_rest(m, i):
                dve.wait_ge(w_hi_o, m + 1 + 2 * i)
                v.tensor_tensor(part(op_lo, S * m, S, i, 2 * S), bank[m % 2][:, 0:S],
                                part(op_hi, S * m, S, i, 2 * S).bitcast(F32), ALU.subtract).then_inc(w_lo_o, 1)

            def sw_turn(t, i):
                for u in range(4):
                    sw_mask(4 * t + u, i)
                    if 4 * t + u >= 1:
                        sw_normalise(4 * t + u - 1, i)
            sw_turn(0, 0)
            chain.loop(3, 8, lambda i: sw_turn(1, i))
            sw_normalise(H - 1, 0)
            sw_rest(H // 2 - 1, 0)
            residual_stage("swo", "f3")
            swiglu(3, "f3", "final2")
            norm_in_place("final2")

def tiles_of(m, per):
    k, n = m.shape
    return np.ascontiguousarray(m.reshape(k // P, P, n // P // per, per, P).transpose(2, 1, 3, 0, 4)
                                .reshape(n // P // per, P, -1))


def rows_of(m):
    k, n = m.shape
    return m.reshape(k // P, P, n).transpose(1, 0, 2).reshape(P, -1)


def swap_halves(m, width):
    k, n = m.shape
    return m.reshape(k, n // width, 2, width // 2)[:, :, ::-1, :].reshape(k, n)


def rope_tables(n, dim, base, reps):
    half = dim // 2
    inv = np.power(np.float32(base), -np.arange(half, dtype=np.float32) * np.float32(2.0 / dim)).astype(np.float32)
    ang = (np.arange(n, dtype=np.float32)[None, :] * inv[:, None]).astype(np.float32)
    cos, sin = np.cos(ang).astype(np.float32), np.sin(ang).astype(np.float32)
    return np.tile(np.concatenate([cos, cos]), (reps, 1)), np.tile(np.concatenate([-sin, sin]), (reps, 1))


def arrange(a):
    f = np.float32
    w = {}
    x_t = np.concatenate([a["meta_tokens"].T, a["x"][0].T], axis=1)
    w["x_t"] = np.ascontiguousarray(x_t.reshape(C, P, T).transpose(1, 0, 2))
    cuts = np.cumsum([D, D, QL, KVL, ROPE, D, D])
    xr, gr, cq, ckv, kr, g_rnn, g_att, _ = np.split(a["w_in"][0], cuts, axis=1)
    w["xr"] = tiles_of(xr, 2)
    kr4 = np.tile(np.concatenate([kr, swap_halves(kr, ROPE)], axis=1), (1, 2))
    w["lat"] = tiles_of(np.concatenate([ckv, kr4, cq], axis=1), 2)
    w["gates"] = np.stack([a["rg_wa"][0], a["rg_wx"][0]], axis=1).reshape(16, P, P).transpose(1, 0, 2).reshape(1, P, TILE)
    w["gr"] = tiles_of(gr, 2)
    uq = a["w_uq"][0].reshape(QL, H, NOPE + ROPE)
    nope, rope = uq[:, :, :NOPE].reshape(QL, -1), uq[:, :, NOPE:].reshape(QL, -1)
    both = np.stack([rope.reshape(QL, 4, P), swap_halves(rope, ROPE).reshape(QL, 4, P)], axis=2).reshape(QL, -1)
    w["uq"] = tiles_of(np.concatenate([nope, both], axis=1), 4)
    ukv = a["w_ukv"][0].reshape(KVL, H, NOPE + VD)
    w["uk"] = tiles_of(ukv[:, :, :NOPE].reshape(KVL, -1), C)
    w["uv"] = rows_of(ukv[:, :, NOPE:].reshape(KVL, -1))[None]
    g1, y1, g2, y2 = (tiles_of(m, 1) for m in (g_rnn, a["w_rnn_out"][0], g_att, a["w_attn_out"][0]))
    w["mix"] = np.stack([np.concatenate([g1, y1], axis=2), np.concatenate([g2, y2], axis=2)], axis=1).reshape(16, P, TILE)
    w["out1"] = tiles_of(a["w_out"][0], 2)
    w["pq"] = tiles_of(a["peer_wq"][0], 2)
    w["keys"] = np.concatenate([a["peer_keys1"][0].T, a["peer_keys2"][0].T], axis=1)
    w["uv_rows"] = np.concatenate([a["peer_u"][0], a["peer_v"][0]], axis=1)
    for n in range(4):
        layer, which = n // 2, n % 2 + 1
        gate, up = np.split(a[f"ffn{which}_w_in_2"][layer], 2, axis=1)
        w[f"ffi{n}"] = tiles_of(np.stack([gate.reshape(D, NF, P), up.reshape(D, NF, P)], axis=2).reshape(D, -1), 2)
        down = tiles_of(a[f"ffn{which}_w_out_2"][layer], 1)
        w[f"ffo{n}"] = down.reshape(C, P, 2, FH * P).transpose(0, 2, 1, 3).reshape(2 * C, P, FH * P)
    q, k, v2 = np.split(a["sb_w_qkv_2"][0], 3, axis=1)
    w["qk"] = tiles_of(np.concatenate([q, k], axis=1), 2)
    w["sbv"] = v2.reshape(4, 2, P, D).transpose(0, 2, 1, 3).reshape(4, P, TILE)
    w["sbo"] = tiles_of(a["sb_w_o_2"][0], 2)
    kk, kv = np.split(a["kv_w_2"], 2, axis=1)
    w["kvk"] = tiles_of(kk, 2)
    w["kvv"] = rows_of(kv)[None]
    w["sq"] = tiles_of(a["swa_w_q_2"][0].reshape(D, H, 64)[:, HEAD_AT].reshape(D, D), 2)
    w["swo"] = tiles_of(a["swa_w_o_2"][0].reshape(H, 64, D)[HEAD_AT].reshape(D, D), 2)

    cols = lambda m: m.reshape(-1, P).T
    v = {"n1": a["norm1_g"][0], "cq": a["q_norm_g"][0], "ckv": a["kv_norm_g"][0], "cb": a["conv_b"][0],
         "ba": a["rg_ba"][0], "bx": a["rg_bx"][0], "lam": a["rg_lambda"][0], "n2": a["norm2_g"][0],
         "final1": a["final_g"], "f0": a["ffn1_norm_2"][0], "f1": a["ffn2_norm_2"][0], "f2": a["ffn1_norm_2"][1],
         "f3": a["ffn2_norm_2"][1], "mix0": a["mix_norm_2"][0], "mix1": a["mix_norm_2"][1], "kv": a["kv_norm_2"],
         "final2": a["final_norm_2"], **{f"cw{t}": a["conv_w"][0][t] for t in range(4)}}
    w["vecs"] = np.concatenate([cols(v[name]) for name, _ in VECS], axis=1)
    p = np.arange(P)[:, None]
    no = f(-1e30)
    mask = np.concatenate([np.where(np.arange(SA)[None] <= p + META, f(0), no),
                           np.where(np.arange(SB)[None] <= p + META + P, f(0), no)], axis=1)
    cos, sin = rope_tables(T, ROPE, 10000.0, 4)
    w["tables1"] = np.concatenate([mask, cos, sin], axis=1).astype(f)
    w["squares"] = np.concatenate([np.ones((P, P)), np.eye(P), p >= p.T, (p ^ 32) == p.T], axis=1).astype(f)
    sinks = a["swa_sinks_2"][0][HEAD_AT]
    w["small"] = np.concatenate([np.tile(np.arange(TOPK, dtype=f), (P, 1)), np.tile(sinks, (P, 1))], axis=1)
    before = np.where(p < p.T, f(0), no)
    sb_mask = np.concatenate([before, np.zeros((P, P), f), before], axis=1)
    j = np.arange(S)[None]
    swa_mask = np.concatenate([np.where(p.T <= p, f(0), no), np.zeros((P, 1), f), np.where((j > p) & (j <= p + P), f(0), no)], axis=1)
    w["tables2"] = np.concatenate([sb_mask, swa_mask, *rope_tables(S, 64, 10000.0, 2)], axis=1).astype(f)
    return {k: np.ascontiguousarray(m) for k, m in w.items()}


STOP = ORDER[-1]


def kernel(**inputs):
    import concourse.bacc as bacc
    from concourse.bass_utils import run_bass_kernel_spmd

    w = arrange({k: np.asarray(m) for k, m in inputs.items()})
    nc = bacc.Bacc("TRN2", target_bir_lowering=False, num_devices=1)
    aps = {k: nc.dram_tensor(f"in_{k}", m.shape, mybir.dt.from_np(m.dtype), kind="ExternalInput").ap() for k, m in w.items()}
    out = nc.dram_tensor("out_t", (P, C, S), F32, kind="ExternalOutput").ap()
    program(nc, aps, out, STOP)
    r = run_bass_kernel_spmd(nc, [{f"in_{k}": m for k, m in w.items()}], core_ids=[0])
    return r.results[0]["out_t"].transpose(2, 1, 0).reshape(1, S, D)
```

```python
import numpy as np
import concourse.bass as bass
from concourse import mybir
from contextlib import ExitStack

F32 = mybir.dt.float32
F32R = mybir.dt.float32r
U32 = mybir.dt.uint32
ALU = mybir.AluOpType
ACT = mybir.ActivationFunctionType
AX = mybir.AxisListType

P = 128
D = 1024
C = D // P
S = 256
META = 16
T = S + META
TP = 384
EPS = 1e-6
QL, KVL = 384, 256
H, NOPE, ROPE, VD = 16, 64, 32, 64
FF = 2816
NF = FF // P
FH = NF // 2
PH, NKEY, TOPK = 8, 128, 16
TAB = 1281
RAW = 4
TILE = P * 16
MLA_SCALE = float((NOPE + ROPE) ** -0.5)
SCALE = float(64 ** -0.5)
SA, SB = P + META, T
HEAD_AT = [0, 4, 1, 5, 2, 6, 3, 7, 8, 12, 9, 13, 10, 14, 11, 15]


def ring_order():
    stages = [("xr", 4, TILE, 4), ("gates", 1, TILE, 8), ("lat", 3, TILE, 3), ("gr", 4, TILE, 4),
              ("uq", 4, 12 * P, 8), ("uk", 1, TILE, 4), ("uv", 1, TILE, 3),
              ("mix", 16, TILE, 16), ("out1", 4, TILE, 0), ("pq", PH, TILE, 0)]
    def ffn(f):
        return [(f"ffi{f}", NF, TILE, NF), (f"ffo{f}", 2 * C, FH * P, 0)]
    stages += ffn(0) + [("qk", 8, TILE, 8), ("sbv", 4, TILE, 2), ("sbo", 4, TILE, 0)]
    stages += ffn(1) + [("kvk", 1, TILE, 1), ("kvv", 1, TILE, 1)]
    stages += ffn(2) + [("sq", 4, TILE, 4), ("swo", 4, TILE, 0)] + ffn(3)
    b = r = n = m = 0
    first, width, pair, res, count, order, part, pairs_of = {}, {}, {}, {}, {}, [], {}, {}
    for name, blocks, cols, pairs in stages:
        first[name], width[name], pair[name], res[name], count[name] = b, cols, r, n, blocks
        order.append(name)
        part[name], pairs_of[name] = m, pairs
        m += C if name.startswith("ffo") else 3 if name == "sbv" else 0
        b += blocks
        r += pairs
        n += 0 if pairs or name == "pq" else C
    return first, width, pair, res, count, order, part, pairs_of


FIRST, WIDTH, PAIR, RES, BLOCKS, ORDER, PART, PAIRS_OF = ring_order()
END = FIRST[ORDER[-1]] + BLOCKS[ORDER[-1]]

NORMS = [("n1", C), ("cq", QL // P), ("ckv", KVL // P), ("n2", C), ("final1", 0), ("f0", C), ("mix0", C),
         ("f1", C), ("kv", C), ("f2", C), ("mix1", C), ("f3", C), ("final2", 0)]
NORM = {name: j for j, name in enumerate([name for name, _ in NORMS if name != "f2"])}
NORM["f2"] = NORM["kv"]
SPLIT0 = {name: sum(c for _, c in NORMS[:j]) for j, (name, _) in enumerate(NORMS)}
BY_CHUNK = {"n1": 0, "final1": 1, "f0": 2}
SUMMED = {name: sum(NORM[n] <= NORM[name] for n, _ in NORMS if n not in BY_CHUNK and n != "f2") for name in NORM}

AFTER = ("f0", "mix0", "f1", "kv", "f2", "mix1", "f3")

VECS = [("n1", C), ("cq", 3), ("ckv", 2), ("cw0", C), ("cw1", C), ("cw2", C), ("cw3", C), ("cb", C), ("ba", C),
        ("bx", C), ("lam", C), ("n2", C), ("final1", C), ("f0", C), ("f1", C), ("f2", C), ("f3", C), ("mix0", C),
        ("mix1", C), ("kv", C), ("final2", C)]
NV = sum(n for _, n in VECS)


class Chain:

    def __init__(self, eng, sem):
        self.eng, self.sem, self.n, self.off = eng, sem, 0, 0

    def link(self, ins):
        self.n += 1
        ins.then_inc(self.sem, 1)
        self.eng.wait_ge(self.sem, self.n + self.off)

    def loop(self, count, per, body):
        start = self.n
        with self.eng.Fori(0, count) as i:
            self.off = i * per
            body(i)
        self.off = 0
        assert self.n - start == per, (self.n - start, per)
        self.n = start + per * count


def program(nc, w, out, stop):
    ctx = ExitStack()
    with ctx:
        def sb(name, cols, dt=F32):
            return ctx.enter_context(nc.sbuf_tensor(name, [P, cols], dt))

        def sem(name):
            return ctx.enter_context(nc.semaphore(name))

        raw = [sb(f"raw{s}", TILE) for s in range(RAW)]
        w_hi = [sb(f"w_hi{s}", TILE, F32R) for s in range(2)]
        w_lo = [sb(f"w_lo{s}", TILE, F32R) for s in range(2)]
        xn_hi, xn_lo = sb("xn_hi", C * T, F32R), sb("xn_lo", C * T, F32R)
        op_hi, op_lo = sb("op_hi", 24 * S, F32R), sb("op_lo", 24 * S, F32R)
        h_all = sb("h_all", C * T)
        arena = sb("arena", 11520)
        half = sb("half", C * S)
        tmp = sb("tmp", 1088)
        acc = [sb(f"acc{i}", T) for i in range(2)]
        tables = sb("tables", TAB + 4 * P)
        keys = sb("keys", 2 * NKEY)
        small = sb("small", TOPK + H)
        picks = sb("picks", 4 * 2 * TOPK)
        vecs = sb("vecs", NV)
        lam_t = sb("lam_t", 8 * C)
        soft = sb("soft", 24 + 1 + H)
        eps = sb("eps", 1)
        bank = [ctx.enter_context(nc.psum_tensor(f"bank{i}", [P, 512], F32)) for i in range(8)]

        def chunks(t, n, width, at=0):
            return t[:, at:at + n * width].rearrange("p (c t) -> p c t", t=width)

        h_t = chunks(h_all, C, T)
        hs = h_t[:, :, META:T]
        xf = [tmp[:, 0:T], tmp[:, T:2 * T]]
        sg = [tmp[:, 544:800], tmp[:, 800:1056]]
        xn = (chunks(xn_hi, C, T), chunks(xn_lo, C, T))
        xs = (xn[0][:, :, META:T], xn[1][:, :, META:T])
        conv = (chunks(op_hi, C, T), chunks(op_lo, C, T))
        y_rnn = (chunks(op_hi, C, S), chunks(op_lo, C, S))
        o_att = (chunks(op_hi, C, S, C * S), chunks(op_lo, C, S, C * S))
        mixed = (chunks(op_hi, C, S, 2 * C * S), chunks(op_lo, C, S, 2 * C * S))
        cqn = (chunks(op_hi, 3, S, 2 * C * S), chunks(op_lo, 3, S, 2 * C * S))
        ckvn = (chunks(op_hi, 2, TP, 2 * C * S + 3 * S), chunks(op_lo, 2, TP, 2 * C * S + 3 * S))
        inner = (chunks(op_hi, NF, S), chunks(op_lo, NF, S))
        xrp = chunks(arena, C, T + 3)
        a_t = chunks(arena, C, T)
        xc = chunks(arena, C, T, 2200)
        r_t = chunks(arena, C, T, 4400)
        i_t = chunks(arena, C, T, 6600)
        cqf = chunks(arena, 3, S, 8800)
        ckvf = chunks(arena, 2, T, 9568)
        kr_raw = arena[:, 10112:10384]
        kr_rot = arena[:, 10384:10656]
        gr = chunks(half, C, S)
        qh = chunks(arena, H, S)
        kh = chunks(arena, H, T, 4096)
        vt = chunks(arena, 3, D, 8448)
        probs = [half[:, 0:640], half[:, 640:1280]]
        pt = [half[:, 1280:1920], tmp[:, 0:640]]
        mla_mask = tables[:, 0:416]
        cos_t, sin_t = tables[:, 416:416 + T], tables[:, 416 + T:416 + 2 * T]
        ones, ident, tri, swap = (tables[:, TAB + P * i:TAB + P * (i + 1)] for i in range(4))
        sb_mask, swa_mask = tables[:, 0:384], tables[:, 384:769]
        cos2, sin2 = tables[:, 769:769 + S], tables[:, 769 + S:TAB]
        pulled = [arena[:, 2 * D * n:2 * D * (n + 1)] for n in range(4)]
        x_tok = chunks(arena, 2, D, 8 * D)
        x_f = chunks(half, C, S)
        q_s = [half[:, 512 * n:512 * (n + 1)] for n in range(2)]
        q_at = [pulled[3][:, 0:512], q_s[1]] + [q_s[n % 2] for n in range(2, PH)]
        product = half[:, D:2 * D]
        scratch = arena[:, 10 * D:11520]
        diag = [tmp[:, P * n:P * (n + 1)] for n in range(2)]
        y_tok = chunks(arena, 2, D)
        gw = [picks[:, 32 * n:32 * n + 32] for n in range(2)]
        expert = [picks[:, 64 + 32 * n:96 + 32 * n].bitcast(U32) for n in range(2)]
        xq = (xn[0][:, :, 0:S], xn[1][:, :, 0:S])
        squares1, squares2 = xc, chunks(half, C, S)
        qk = chunks(arena, 2 * C, S)
        sv = chunks(arena, 2, D, 4096)
        zm = [arena[:, 6144 + 384 * n:6528 + 384 * n] for n in range(4)]
        az, sp_t, wt = ([arena[:, 7680 + 768 * a + 384 * n:8064 + 768 * a + 384 * n] for n in range(2)] for a in range(3))
        ex = [half[:, 384 * n:384 * (n + 1)] for n in range(2)]
        four = (bank[4], bank[5], bank[2], bank[3])
        o2 = y_rnn
        k_sh, v_sh, k_raw = chunks(arena, 2, S), chunks(arena, 2, S, 512), chunks(arena, 2, S, 1024)
        q_sw, q_half = chunks(arena, C, S, 2048), chunks(arena, C, S, 4096)
        sw_p = [arena[:, 6144 + 386 * n:6530 + 386 * n] for n in range(4)]
        sw_pt = [arena[:, 7688 + 384 * n:8072 + 384 * n] for n in range(2)]
        V_AT, at = {}, 0
        for name, n in VECS:
            V_AT[name] = (at, n)
            at += n
        def vec(name, c):
            return vecs[:, V_AT[name][0] + c:V_AT[name][0] + c + 1]
        sinks = soft[:, 25:25 + H]
        cl, ncl = lam_t[:, 0:C], lam_t[:, C:2 * C]

        names, at = {}, 0
        for name, n in (("s", NKEY), ("cand", 256), ("left", 256), ("hit", 256), ("t1", 16), ("t2", 16), ("i1", 16),
                        ("i2", 16), ("f1", 16), ("f2", 16), ("best", 16), ("at", 16), ("hi", 16), ("lo", 16),
                        ("fh", 16), ("fl", 16), ("e1", 16), ("e2", 16), ("neg", 1), ("sum", 1), ("rs", 1)):
            names[name] = (at, n)
            at += n
        top = {name: scratch[:, a:a + n] for name, (a, n) in names.items()}
        dots, coef = scratch[:, at:at + 4], scratch[:, at + 4:at + 12]
        assert at + 12 <= 1264

        landed = [sem(f"landed{s}") for s in range(RAW)]
        hi_done, lo_done = sem("hi_done"), sem("lo_done")
        even_done, odd_done = sem("even_done"), sem("odd_done")
        act_read, dve_read = sem("act_read"), sem("dve_read")
        res_done = sem("res_done")
        part_done = sem("part_done")
        h_new = sem("h_new")
        sq_done = sem("sq_done")
        ss_in, ss_done = sem("ss_in"), sem("ss_done")
        sd_done, rs_done = sem("sd_done"), sem("rs_done")
        xf_done, xhi_done, xlo_done = sem("xf_done"), sem("xhi_done"), sem("xlo_done")
        first_in, const_in, x_in = sem("first_in"), sem("const_in"), sem("x_in")
        pads = sem("pads")
        lam_e, lam_c = sem("lam_e"), sem("lam_c")
        conv_dve, conv_pool = sem("conv_dve"), sem("conv_pool")
        conv_hi, conv_lo = sem("conv_hi"), sem("conv_lo")
        lru_act, lru_dve, lru_pool = sem("lru_act"), sem("lru_dve"), sem("lru_pool")
        y_f, y_hi, y_lo = sem("y_f"), sem("y_hi"), sem("y_lo")
        kr_in, kr_ready = sem("kr_in"), sem("kr_ready")
        lat_read = sem("lat_read")
        sc_done, sc_masked, exp_done, p_ready = sem("sc_done"), sem("sc_masked"), sem("exp_done"), sem("p_ready")
        tr_done, ptx, pty, pv_done = sem("tr_done"), sem("ptx"), sem("pty"), sem("pv_done")
        o_done, o_hi, o_lo = sem("o_done"), sem("o_hi"), sem("o_lo")
        gate_done, mix_f, mix_hi, mix_lo = sem("gate_done"), sem("mix_f"), sem("mix_hi"), sem("mix_lo")
        rope_in = sem("rope_in")
        dve_step, act_step, pool_step = sem("dve_step"), sem("act_step"), sem("pool_step")
        xt_ps, xt_read = sem("xt_ps"), sem("xt_read")
        q_done, q_read, key_done = sem("q_done"), sem("q_read"), sem("key_done")
        top_max, top_exp, expert_in = sem("top_max"), sem("top_exp"), sem("expert_in")
        gathered = [sem(f"gathered{s}") for s in range(4)]
        dot_done, diag_done, row_used = sem("dot_done"), sem("diag_done"), sem("row_used")
        y_tok_act, y_tok_dve, y_back = sem("y_tok_act"), sem("y_tok_dve"), sem("y_back")
        peer_h, h_scaled = sem("peer_h"), sem("h_scaled")
        gate_in, up_in = sem("gate_in"), sem("up_in")
        in_hi, in_lo = sem("in_hi"), sem("in_lo")
        qk_scaled = sem("qk_scaled")
        z_done, z_mask, soft_in, sp_done = sem("z_done"), sem("z_mask"), sem("soft_in"), sem("sp_done")
        suf_done, arg_done, w_done, sbo_done = sem("suf_done"), sem("arg_done"), sem("w_done"), sem("sbo_done")
        sbo_hi, sbo_lo, soft_exp = sem("sbo_hi"), sem("sbo_lo"), sem("soft_exp")
        tables2_in = sem("tables2_in")
        k_half, k_rot, q_swap, q_rot = sem("k_half"), sem("k_rot"), sem("q_swap"), sem("q_rot")
        sink_in = sem("sink_in")
        w_sc, w_mask, w_exp, w_p = sem("w_sc"), sem("w_mask"), sem("w_exp"), sem("w_p")
        w_tr, w_pt, w_pv, w_hi_o, w_lo_o = sem("w_tr"), sem("w_pt"), sem("w_pv"), sem("w_hi_o"), sem("w_lo_o")
        stored = sem("stored")

        def each(eng, n, body, tail=0, per=RAW, peel=False):
            first = min(RAW, n - tail) if peel else 0
            for k in range(first):
                body(k, 0)
            turns = (n - tail - first) // per
            if turns >= 2:
                with eng.Fori(0, turns) as i:
                    for u in range(first, first + per):
                        body(u, i * (per // RAW) if per > RAW else i)
            else:
                turns = 0
            for k in range(first + per * turns, n):
                body(k, 0)

        block = ctx.enter_context(nc.Block())

        @block.sync
        def _(sp):
            sp.dma_start(h_t[:, :, :], w["x_t"]).then_inc(x_in, 16)
            sp.dma_start(tables[:, TAB:], w["squares"]).then_inc(first_in, 16)
            sp.dma_start(vecs[:, :], w["vecs"]).then_inc(first_in, 16)

            def load(name):
                src, cols = w[name], WIDTH[name]

                def body(k, i):
                    b = FIRST[name] + k
                    if b >= RAW:
                        sp.wait_ge(lo_done, b - RAW + 1 + 4 * i)
                    at = src[bass.ds(k + 4 * i, 1), :, :] if not isinstance(i, int) else src[k:k + 1, :, :]
                    sp.dma_start(raw[b % RAW][:, 0:cols], at.rearrange("a p n -> (a p) n"))\
                      .then_inc(landed[b % RAW], 16)
                each(sp, BLOCKS[name], body)

            for name in ORDER[:ORDER.index(stop) + 1]:
                load(name)
                if name == "xr":
                    sp.dma_start(tables[:, 0:960], w["tables1"]).then_inc(const_in, 16)
                    sp.dma_start(keys[:, :], w["keys"]).then_inc(const_in, 16)
                    sp.dma_start(small[:, :], w["small"]).then_inc(const_in, 16)
                if name == "pq":
                    sp.wait_ge(h_new, RES["out1"] + C)
                    sp.dma_start(tables[:, 0:TAB], w["tables2"]).then_inc(tables2_in, 16)
            sp.wait_ge(*((h_scaled, C) if stop == "pq" else (h_scaled, 2 * C) if stop == ORDER[-1] else (h_new, RES[stop] + C)))
            sp.dma_start(out, hs).then_inc(stored, 16)
            sp.wait_ge(stored, 16)

        @block.gpsimd
        def _(pool):
            chain = Chain(pool, pool_step)
            pool.memset(eps[:, :], EPS).then_inc(pads, 1)
            pool.memset(xrp[:, :, 0:3], 0.0).then_inc(pads, 1)
            pool.wait_ge(pads, 2)
            for part in ckvn:
                pool.memset(part[:, :, T:TP].bitcast(F32), 0.0).then_inc(pads, 1)

            pool.wait_ge(first_in, 32)
            for k in range(C // 2):
                if k < 3:
                    c, y = 2 * k + 1, xc[:, 2 * k + 1, :]
                    tap = arena[:, 8800:8800 + T]
                    pool.wait_ge(dve_read, PAIR["xr"] + k + 1)
                    chain.link(nc.gpsimd.tensor_scalar(y, xrp[:, c, 0:T], vec("cw0", c), vec("cb", c), ALU.mult, ALU.add))
                    for t in (1, 2, 3):
                        chain.link(nc.gpsimd.tensor_scalar(tap, xrp[:, c, t:t + T], vec(f"cw{t}", c), None, ALU.mult))
                        ins = nc.gpsimd.tensor_tensor(y, y, tap, ALU.add)
                        ins.then_inc(conv_pool, 1) if t == 3 else chain.link(ins)
                    pool.wait_ge(conv_pool, k + 1)
                for c in (2 * k, 2 * k + 1):
                    pool.wait_ge(conv_hi, c + 1)
                    nc.gpsimd.tensor_tensor(conv[1][:, c, :], xc[:, c, :], conv[0][:, c, :].bitcast(F32), ALU.subtract)\
                        .then_inc(conv_lo, 1)
            pool.wait_ge(lru_act, 1)
            nc.gpsimd.tensor_tensor(i_t[:, :, :], i_t[:, :, :], xc[:, :, :], ALU.mult).then_inc(lru_pool, 1)
            pool.wait_ge(lru_pool, 1)
            pool.wait_ge(conv_lo, C)
            pool.wait_ge(lru_act, 2)
            nc.gpsimd.tensor_tensor(xc[:, :, :], a_t[:, :, :], a_t[:, :, :], ALU.mult).then_inc(lru_pool, 1)

            pool.wait_ge(ss_in, SUMMED["n2"])
            for n in range(2 * PH):
                pool.wait_ge(expert_in, n + 1)
                for s in range(TOPK):
                    q = TOPK * n + s
                    if q >= 4:
                        pool.wait_ge(row_used, q - 3)
                    at = TOPK * (n % 2) + s
                    pool.indirect_dma_start(pulled[s % 4], None, w["uv_rows"],
                                            bass.IndirectOffsetOnAxis(expert[n // 2 % 2][:, at:at + 1], 0))\
                        .then_inc(gathered[s % 4], 16)

        @block.tensor
        def _(pe):
            def mm3(o, wt, x, first=True, last=True):
                nc.tensor.matmul(o, wt[0], x[1], start=first, stop=False)
                nc.tensor.matmul(o, wt[0], x[0], start=False, stop=False)
                return nc.tensor.matmul(o, wt[1], x[0], start=False, stop=last)

            def tiles(b, n):
                v = w_hi[b % 2][:, n * P:(n + 1) * P], w_lo[b % 2][:, n * P:(n + 1) * P]
                return v

            def split_ready(name, k, i):
                pe.wait_ge(lo_done, FIRST[name] + k + 1 + 4 * i)

            def even_free(r, i=0):
                if r >= 2:
                    pe.wait_ge(act_read, r - 1 + 4 * i)

            def odd_free(r, i=0):
                if r >= 2:
                    pe.wait_ge(dve_read, r - 1 + 4 * i)

            def pair_stage(name, x, n=T, norm=None, after=None):
                def body(k, i):
                    b, r = FIRST[name] + k, PAIR[name] + k
                    split_ready(name, k, i)
                    for c, free, done in ((0, even_free, even_done), (1, odd_free, odd_done)):
                        free(r, i)
                        o = bank[2 * (r % 2) + c][:, 0:n]
                        for kk in range(C):
                            if norm and k == 0 and c == 0:
                                if norm in AFTER and norm not in ("f2", "f0") and kk == C - 1:
                                    norm_sum(norm, S)
                                pe.wait_ge(xlo_done, SPLIT0[norm] + kk + 1)
                            last = mm3(o, tiles(b, C * c + kk), (x[0][:, kk, :], x[1][:, kk, :]), kk == 0, kk == C - 1)
                        last.then_inc(done, 1)
                        if norm == "f0" and k == 0 and c == 0:
                            norm_sum(norm, S)
                    if after:
                        after(k)
                each(pe, BLOCKS[name], body, per=2 * RAW, peel=norm is not None)

            def norm_sum(name, n):
                j = NORM[name]
                a, o = acc[j % 2], bank[6 + j % 2]
                if name in BY_CHUNK:
                    for c in range(C):
                        pe.wait_ge(sq_done, C * BY_CHUNK[name] + c + 1)
                        last = nc.tensor.matmul(o[:, 0:n], ones, (squares1 if name == "n1" else squares2)[:, c, :],
                                                start=c == 0, stop=c == C - 1)
                    last.then_inc(ss_done, 1)
                    return
                pe.wait_ge(ss_in, SUMMED[name])
                if name in ("mix0", "kv"):
                    for t in range(2):
                        nc.tensor.matmul(o[:, S + t:S + t + 1], a[:, P * t:P * t + P], ones[:, 0:1], start=True, stop=True)
                nc.tensor.matmul(o[:, 0:n], ones, a[:, 0:n], start=True, stop=True).then_inc(ss_done, 1)

            def residual_stage(name, x, ready):
                def body(k, i):
                    b = FIRST[name] + k
                    split_ready(name, k, i)
                    for c in range(2):
                        n = RES[name] + 2 * k + c
                        if n >= 2:
                            pe.wait_ge(h_new, n - 1 + 8 * i)
                        for kk in range(C):
                            if k == 0 and c == 0:
                                pe.wait_ge(*ready(kk))
                            last = mm3(bank[4 + n % 2][:, 0:S], tiles(b, C * c + kk), (x[0][:, kk, :], x[1][:, kk, :]),
                                       kk == 0, kk == C - 1)
                        last.then_inc(res_done, 1)
                each(pe, BLOCKS[name], body, per=2 * RAW)

            pe.wait_ge(first_in, 32)
            norm_sum("n1", T)
            pair_stage("xr", xn, norm="n1")
            pe.wait_ge(const_in, 48)
            split_ready("gates", 0, 0)
            for c in range(C):
                r = PAIR["gates"] + c
                pe.wait_ge(conv_lo, c + 1)
                x = conv[0][:, c, :], conv[1][:, c, :]
                even_free(r)
                mm3(bank[2 * (r % 2)][:, 0:T], tiles(FIRST["gates"], 2 * c), x).then_inc(even_done, 1)
                odd_free(r)
                mm3(bank[2 * (r % 2) + 1][:, 0:T], tiles(FIRST["gates"], 2 * c + 1), x).then_inc(odd_done, 1)
            pair_stage("lat", xn)
            pair_stage("gr", xs, n=S, after=lambda k: (norm_sum("cq", S), norm_sum("ckv", T)) if k == 1 else None)
            for k in range(4):
                split_ready("uq", k, 0)
                for c in range(4):
                    r = PAIR["uq"] + 2 * k + c // 2
                    (odd_free if c % 2 else even_free)(r)
                    for kk in range(3):
                        if k == 0 and c == 0:
                            pe.wait_ge(xlo_done, SPLIT0["cq"] + kk + 1)
                        last = mm3(bank[2 * (r % 2) + c % 2][:, 0:S], tiles(FIRST["uq"] + k, 3 * c + kk),
                                   (cqn[0][:, kk, :], cqn[1][:, kk, :]), kk == 0, kk == 2)
                    last.then_inc(odd_done if c % 2 else even_done, 1)
            split_ready("uk", 0, 0)
            for c in range(C):
                r = PAIR["uk"] + c // 2
                (odd_free if c % 2 else even_free)(r)
                for kk in range(2):
                    if c == 0:
                        pe.wait_ge(xlo_done, SPLIT0["ckv"] + kk + 1)
                    last = mm3(bank[2 * (r % 2) + c % 2][:, 0:T], tiles(FIRST["uk"], 2 * c + kk),
                               (ckvn[0][:, kk, 0:T], ckvn[1][:, kk, 0:T]), kk == 0, kk == 1)
                last.then_inc(odd_done if c % 2 else even_done, 1)
            split_ready("uv", 0, 0)
            wv = chunks(w_hi[FIRST["uv"] % 2], 2, D), chunks(w_lo[FIRST["uv"] % 2], 2, D)
            for t in range(3):
                r = PAIR["uv"] + t
                for hf, free, done in ((0, even_free, even_done), (1, odd_free, odd_done)):
                    free(r)
                    for kk in range(2):
                        last = mm3(bank[2 * (r % 2) + hf][:, :],
                                   (ckvn[0][:, kk, P * t:P * t + P], ckvn[1][:, kk, P * t:P * t + P]),
                                   (wv[0][:, kk, 512 * hf:512 * hf + 512], wv[1][:, kk, 512 * hf:512 * hf + 512]),
                                   kk == 0, kk == 1)
                    last.then_inc(done, 1)

            def scores(h):
                if h >= 2:
                    pe.wait_ge(exp_done, 2 * (h - 1))
                nc.tensor.matmul(bank[4 + h % 2][:, 0:SA], qh[0:96, h, 0:P], kh[0:96, h, 0:SA], start=True, stop=True)
                nc.tensor.matmul(bank[4 + h % 2][:, SA:SA + SB], qh[0:96, h, P:S], kh[0:96, h, 0:SB],
                                 start=True, stop=True).then_inc(sc_done, 1)

            def transposes(h):
                pe.wait_ge(p_ready, 2 * h + 2)
                if h >= 2:
                    pe.wait_ge(ptx, h - 1)
                    pe.wait_ge(pty, h - 1)
                p = probs[h % 2]
                for n, at in enumerate((0, 256, P, 256 + P)):
                    nc.tensor.transpose(bank[6 + h % 2][:, P * n:P * n + P], p[:, at:at + P], ident)
                nc.tensor.transpose(bank[2 + h % 2][:, 0:P], p[:, 512:640], ident).then_inc(tr_done, 1)

            def values(h):
                pe.wait_ge(ptx, h + 1)
                pe.wait_ge(pty, h + 1)
                if h >= 4 and h % 2 == 0:
                    pe.wait_ge(o_lo, h // 2 - 1)
                base = 64 * (h % 2)
                o = bank[h // 2 % 2]
                q = pt[h % 2]
                cols = slice(VD * h, VD * h + VD)
                nc.tensor.matmul(o[base:base + 64, 0:S], vt[:, 0, cols], q[:, 0:S], start=True, stop=False)
                nc.tensor.matmul(o[base:base + 64, 0:S], vt[:, 1, cols], q[:, S:2 * S], start=False, stop=False)
                nc.tensor.matmul(o[base:base + 64, P:S], vt[:, 2, cols], q[:, 2 * S:2 * S + P],
                                 start=False, stop=True).then_inc(pv_done, 1)

            r = PAIR["mix"]
            pe.wait_ge(act_read, r)
            pe.wait_ge(dve_read, r)
            pe.wait_ge(kr_ready, 1)
            pe.wait_ge(rope_in, 16)
            for h in range(3):
                scores(h)
            transposes(0)
            for h in range(H):
                if h + 3 < H:
                    scores(h + 3)
                if h + 1 < H:
                    transposes(h + 1)
                values(h)

            def mix(k, i):
                b, r = FIRST["mix"] + k, PAIR["mix"] + k
                split_ready("mix", k, i)
                even_free(r, i)
                for kk in range(C):
                    last = mm3(bank[2 * (r % 2)][:, 0:S], tiles(b, kk), (xs[0][:, kk, :], xs[1][:, kk, :]),
                               kk == 0, kk == C - 1)
                last.then_inc(even_done, 1)
                odd_free(r, i)
                y = y_rnn if k % 2 == 0 else o_att
                for kk in range(C):
                    if k == 0 and kk == 0:
                        pe.wait_ge(y_lo, 1)
                    last = mm3(bank[2 * (r % 2) + 1][:, 0:S], tiles(b, C + kk), (y[0][:, kk, :], y[1][:, kk, :]),
                               kk == 0, kk == C - 1)
                last.then_inc(odd_done, 1)
            pe.wait_ge(o_lo, C)
            each(pe, BLOCKS["mix"], mix, per=2 * RAW)
            residual_stage("out1", mixed, lambda kk: (mix_lo, kk + 1))
            norm_sum("n2", S)

            def token_major():
                for t in range(2):
                    for c in range(C):
                        last = nc.tensor.transpose(bank[4 + 2 * t + c // 4][:, P * (c % 4):P * (c % 4 + 1)],
                                                   x_f[:, c, P * t:P * t + P], ident)
                    last.then_inc(xt_ps, 1)

            def query_part(h, n):
                c, kk = n // C, n % C
                if n == 0:
                    split_ready("pq", h, 0)
                    if h >= 2:
                        pe.wait_ge(q_read, h - 1)
                last = mm3(bank[h % 2][:, S * c:S * c + S], tiles(FIRST["pq"] + h, n),
                           (xq[0][:, kk, :], xq[1][:, kk, :]), kk == 0, kk == C - 1)
                if n == 2 * C - 1:
                    last.then_inc(q_done, 1)

            def key_scores(h):
                pe.wait_ge(q_read, h + 1)
                if h >= 2:
                    pe.wait_ge(expert_in, 2 * (h - 1))
                for t in range(2):
                    for c in range(2):
                        last = nc.tensor.matmul(bank[2 + h % 2][:, P * (2 * t + c):P * (2 * t + c + 1)],
                                                q_at[h][:, S * c + P * t:S * c + P * t + P],
                                                keys[:, NKEY * c:NKEY * (c + 1)], start=True, stop=True)
                last.then_inc(key_done, 1)

            def add_rows(n, s, i):
                q = 16 * n + s
                pe.wait_ge(diag_done, q + 1 + (0 if isinstance(i, int) else 4 * i))
                for f in range(2):
                    last = nc.tensor.matmul(bank[4 + 2 * (n % 2) + f][:, :], diag[s % 2],
                                            pulled[s % 4][:, D + 512 * f:D + 512 * (f + 1)],
                                            start=(n < 2 and s == 0), stop=True, skip_group_check=True)
                last.then_inc(row_used, 1)

            for h in range(2):
                for n in range(2 * C):
                    if h == 0 and n < C:
                        pe.wait_ge(xlo_done, SPLIT0["n2"] + n + 1)
                    query_part(h, n)
                key_scores(h)
                if h == 0:
                    token_major()
            for n in range(2 * PH):
                h = n // 2 + 2
                if n % 2 == 0 and h < PH:
                    for s in range(TOPK):
                        query_part(h, s)
                        add_rows(n, s, 0)
                elif n == 1:
                    for s in range(TOPK):
                        if s == 12:
                            key_scores(h)
                        add_rows(n, s, 0)
                else:
                    with pe.Fori(0, 3) as i:
                        for s in range(4):
                            add_rows(n, s, i)
                    if h < PH:
                        key_scores(h)
                    for s in range(12, TOPK):
                        add_rows(n, s, 0)
            for t in range(2):
                pe.wait_ge(y_tok_act, t + 1)
                pe.wait_ge(y_tok_dve, t + 1)
                for c in range(C):
                    last = nc.tensor.transpose(bank[c // 2][:, S * (c % 2) + P * t:S * (c % 2) + P * t + P],
                                               y_tok[:, t, P * c:P * c + P], ident)
            last.then_inc(y_back, 1)
            pe.wait_ge(peer_h, C)
            norm_sum("final1", S)
            if stop == "pq":
                return

            def swiglu(f, norm):
                pair_stage(f"ffi{f}", xq, n=S, norm=norm)

                def down(k, i):
                    name = f"ffo{f}"
                    c, part = k // 2, k % 2
                    n = RES[name] + c
                    split_ready(name, k, i)
                    if part == 0:
                        pe.wait_ge(h_new, n - 1 + 2 * i)
                    for t in range(FH):
                        kk = FH * part + t
                        if k < 2:
                            pe.wait_ge(in_lo, NF * f + kk + 1)
                        last = mm3(bank[4 + n % 2][:, 0:S], tiles(FIRST[name] + k, t),
                                   (inner[0][:, kk, :], inner[1][:, kk, :]), kk == 0, kk == NF - 1)
                    last.then_inc(res_done if part else part_done, 1)
                each(pe, BLOCKS[f"ffo{f}"], down, per=2 * RAW)

            def values_stage(name, blocks, width, per):
                parts = width // 512 or 1
                cols = min(width, 512)
                for k in range(blocks):
                    split_ready(name, k, 0)
                    b = FIRST[name] + k
                    for t in range(2):
                        for hf in range(parts):
                            r, c = (PAIR[name] + t, hf) if parts == 2 else (PAIR[name], t)
                            if k == 0:
                                (odd_free if c else even_free)(r)
                            for kk in range(per):
                                ci = per * k + kk
                                at = width * kk + 512 * hf
                                last = mm3(bank[2 * (r % 2) + c][:, 0:cols],
                                           (xq[0][:, ci, P * t:P * t + P], xq[1][:, ci, P * t:P * t + P]),
                                           (w_hi[b % 2][:, at:at + cols], w_lo[b % 2][:, at:at + cols]),
                                           ci == 0, ci == C - 1)
                            if k == blocks - 1:
                                last.then_inc(odd_done if c else even_done, 1)
                    if k < blocks - 1:
                        last.then_inc(part_done, 1)

            swiglu(0, "f0")
            if stop == "ffo0":
                return
            pair_stage("qk", xq, n=S, norm="mix0")
            values_stage("sbv", 4, D, 2)

            pe.wait_ge(act_read, PAIR["sbv"] + 2)
            pe.wait_ge(dve_read, PAIR["sbv"] + 2)
            pe.wait_ge(qk_scaled, 8)
            pe.wait_ge(tables2_in, 16)

            def logits(h):
                base, c = 64 * (h % 2), h // 2
                if h >= 4:
                    pe.wait_ge(z_mask, h - 3)
                rows_ = slice(base, base + 64)
                nc.tensor.matmul(four[h % 4][:, 0:S], qk[rows_, C + c, 0:P], qk[rows_, c, :], start=True, stop=True)
                nc.tensor.matmul(four[h % 4][:, S:S + P], qk[rows_, C + c, P:S], qk[rows_, c, P:S],
                                 start=True, stop=True).then_inc(z_done, 1)

            def suffixes(h):
                pe.wait_ge(sp_done, h + 1)
                if h >= 2:
                    pe.wait_ge(arg_done, h - 1)
                s_, o = sp_t[h % 2], bank[6 + h % 2]
                nc.tensor.matmul(o[:, 0:S], tri, s_[:, 0:S], start=True, stop=False)
                nc.tensor.matmul(o[:, P:S], ones, s_[:, S:S + P], start=False, stop=True)
                nc.tensor.matmul(o[:, S:S + P], tri, s_[:, S:S + P], start=True, stop=True).then_inc(suf_done, 1)

            def sb_values(h):
                pe.wait_ge(w_done, h + 1)
                if h >= 4 and h % 2 == 0:
                    pe.wait_ge(sbo_lo, h // 2 - 1)
                base, o = 64 * (h % 2), bank[h // 2 % 2]
                cols = slice(64 * h, 64 * h + 64)
                nc.tensor.matmul(o[base:base + 64, 0:S], sv[:, 0, cols], wt[h % 2][:, 0:S], start=True, stop=False)
                nc.tensor.matmul(o[base:base + 64, P:S], sv[:, 1, cols], wt[h % 2][:, S:S + P], start=False, stop=True)\
                  .then_inc(sbo_done, 1)

            for h in range(4):
                logits(h)
            for m in range(H // 2):
                suffixes(2 * m)
                suffixes(2 * m + 1)
                for h in (2 * m + 4, 2 * m + 5):
                    if h < H:
                        logits(h)
                if m:
                    sb_values(2 * m - 2)
                    sb_values(2 * m - 1)
            sb_values(H - 2)
            sb_values(H - 1)
            residual_stage("sbo", o2, lambda kk: (sbo_lo, kk + 1))
            if stop == "sbo":
                return
            swiglu(1, "f1")
            pair_stage("kvk", xq, n=S, norm="kv")
            values_stage("kvv", 1, S, C)
            swiglu(2, "f2")

            def swap_halves_of(k):
                pe.wait_ge(act_read, PAIR["sq"] + k + 1)
                pe.wait_ge(dve_read, PAIR["sq"] + k + 1)
                if k >= 2:
                    pe.wait_ge(q_rot, k - 1)
                for c in range(2):
                    last = nc.tensor.matmul(bank[4 + k % 2][:, S * c:S * c + S], swap, q_sw[:, 2 * k + c, :],
                                            start=True, stop=True)
                last.then_inc(q_swap, 1)
            pair_stage("sq", xq, n=S, norm="mix1", after=lambda k: swap_halves_of(k - 1) if k else None)
            swap_halves_of(3)

            pe.wait_ge(q_rot, 4)
            pe.wait_ge(k_rot, 1)

            def sw_scores(h):
                base, g = 64 * (h % 2), HEAD_AT[h] // 4
                if h >= 4:
                    pe.wait_ge(w_exp, 2 * (h - 3))
                rows_, o = slice(base, base + 64), four[h % 4]
                nc.tensor.matmul(o[:, 0:P], q_sw[rows_, h // 2, 0:P], k_sh[rows_, g // 2, 0:P], start=True, stop=True)
                nc.tensor.matmul(o[:, P + 1:P + 1 + S], q_sw[rows_, h // 2, P:S], k_sh[rows_, g // 2, :],
                                 start=True, stop=True).then_inc(w_sc, 1)

            def sw_transposes(h):
                pe.wait_ge(w_p, 2 * h + 2)
                if h >= 2:
                    pe.wait_ge(w_pt, h - 1)
                for n, at in enumerate((0, P + 2, 2 * P + 2)):
                    last = nc.tensor.transpose(bank[6 + h % 2][:, P * n:P * n + P], sw_p[h % 4][:, at:at + P], ident)
                last.then_inc(w_tr, 1)

            def sw_values(h):
                pe.wait_ge(w_pt, h + 1)
                if h >= 4 and h % 2 == 0:
                    pe.wait_ge(w_lo_o, h // 2 - 1)
                base, o, g = 64 * (h % 2), bank[h // 2 % 2], HEAD_AT[h] // 4
                cols = slice(64 * g, 64 * g + 64)
                q = sw_pt[h % 2]
                nc.tensor.matmul(o[base:base + 64, 0:S], v_sh[:, 0, cols], q[:, 0:S], start=True, stop=False)
                nc.tensor.matmul(o[base:base + 64, P:S], v_sh[:, 1, cols], q[:, S:S + P], start=False, stop=True)\
                  .then_inc(w_pv, 1)

            for h in range(3):
                sw_scores(h)
            sw_transposes(0)
            for h in range(H):
                if h + 3 < H:
                    sw_scores(h + 3)
                if h + 1 < H:
                    sw_transposes(h + 1)
                sw_values(h)
            residual_stage("swo", o2, lambda kk: (w_lo_o, kk + 1))
            swiglu(3, "f3")
            norm_sum("final2", S)

        @block.scalar
        def _(act):
            chain = Chain(act, act_step)

            def round_block(b, cols, i=0):
                act.wait_ge(landed[b % RAW], 16 * (b // RAW + 1) + 16 * i)
                nc.scalar.activation(w_hi[b % 2][:, 0:cols], raw[b % RAW][:, 0:cols], ACT.Copy).then_inc(hi_done, 1)

            def done_of(name, k, i=0):
                if name.startswith("ffo"):
                    n = RES[name] + k // 2
                    return (res_done, n + 1 + 2 * i) if k % 2 else (part_done, PART[name] + k // 2 + 1 + 2 * i)
                if name == "sbv" and k < 3:
                    return part_done, PART[name] + k + 1
                if name == "pq":
                    return q_done, k + 1
                if PAIRS_OF[name] == 0:
                    return res_done, RES[name] + 2 * (k + 1) + 8 * i
                per = max(1, PAIRS_OF[name] // BLOCKS[name])
                if name == "sbv":
                    return odd_done, PAIR[name] + 2
                return odd_done, PAIR[name] + per * (k + 1) + 4 * per * i

            def round_next(name, k, i=0):
                b = FIRST[name] + k + 1
                if b >= END or (name == stop and k == BLOCKS[name] - 1 and isinstance(i, int)):
                    return
                nxt = name if k + 1 < BLOCKS[name] else ORDER[ORDER.index(name) + 1]
                if k >= 1 or not isinstance(i, int):
                    act.wait_ge(*done_of(name, k - 1, i))
                elif b >= 2:
                    prev = ORDER[ORDER.index(name) - 1]
                    act.wait_ge(*done_of(prev, BLOCKS[prev] - 1))
                round_block(b, WIDTH[nxt], i)

            def stage_start(name):
                prev = ORDER[ORDER.index(name) - 1]
                act.wait_ge(*done_of(prev, BLOCKS[prev] - 1))

            def pair_stage(name, body, start=True, tail=0, before=None, after=None, norm=None):
                if start:
                    stage_start(name)

                def step(k, i):
                    round_next(name, k, i)
                    if before:
                        before(k)
                    if norm and k == 0:
                        norm_root(norm)
                    r = PAIR[name] + k
                    act.wait_ge(even_done, r + 1 + 4 * i)
                    body(k, i, bank[2 * (r % 2)])
                    if after:
                        after(k)
                each(act, BLOCKS[name], step, tail, peel=norm is not None or name == "ffi2")

            def residual_stage(name, norm=None):
                stage_start(name)
                halves = name.startswith("ffo")

                def hi(m, i=0):
                    act.wait_ge(xf_done, SPLIT0[norm] + m + 1 + 2 * i)
                    copy(part(xn_hi, T * m, S, i, 2 * T), sg[m % 2]).then_inc(xhi_done, 1)

                def step(k, i):
                    round_next(name, k, i)
                    if norm and k >= 1 and not (halves and k % 2):
                        for m in (k // 2 - 1,) if halves else (2 * k - 2, 2 * k - 1):
                            hi(m, i)
                each(act, BLOCKS[name], step, 1, peel=norm is not None)
                if norm:
                    for m in (C - 1,) if halves else (C - 2, C - 1):
                        hi(m)

            def copy(o, x):
                return nc.scalar.activation(o, x, ACT.Copy)

            def norm_root(name, n=S, size=D):
                j = NORM[name]
                if name in ("mix0", "kv"):
                    n = S + 2
                act.wait_ge(ss_done, j + 1)
                nc.scalar.activation(acc[j % 2][:, 0:n], bank[6 + j % 2][:, 0:n], ACT.Sqrt, bias=eps[:, :],
                                     scale=1.0 / size).then_inc(sd_done, 1)

            def part(t, at, n, i=0, step=0):
                return t[:, at:at + n] if isinstance(i, int) else t[:, bass.ds(at + step * i, n)]

            def norm_hi(name, n, dst, size=D):
                if name not in AFTER:
                    norm_root(name, n, size)
                for c in range(dict(NORMS)[name]):
                    act.wait_ge(xf_done, SPLIT0[name] + c + 1)
                    copy(dst[0][:, c, 0:n], xf[c % 2][:, 0:n]).then_inc(xhi_done, 1)

            def squares(name, src, n, ready, dst):
                for c in range(C):
                    act.wait_ge(ready, c + 1 if ready is not x_in else 16)
                    nc.scalar.activation(dst[:, c, 0:n], src[:, c, :], ACT.Square).then_inc(sq_done, 1)

            squares("n1", h_t, T, x_in, squares1)
            act.wait_ge(pads, 1)
            round_block(0, TILE)
            norm_hi("n1", T, xn)
            act.wait_ge(first_in, 32)
            lam = vecs[:, V_AT["lam"][0]:V_AT["lam"][0] + C]
            chain.link(nc.scalar.activation(lam_t[:, 0:C], lam, ACT.Abs))
            nc.scalar.activation(lam_t[:, 0:C], lam_t[:, 0:C], ACT.Exp, scale=-1.0).then_inc(lam_e, 1)

            def xr(k, i, ps):
                if k == 0:
                    act.wait_ge(pads, 2)
                copy(xrp[:, 2 * k, 3:3 + T], ps[:, 0:T]).then_inc(act_read, 1)

            def conv_parts(k):
                for c in (2 * k, 2 * k + 1):
                    if c % 2 and k < 3:
                        act.wait_ge(conv_pool, k + 1)
                    else:
                        act.wait_ge(conv_dve, k + 1 + c % 2)
                    copy(conv[0][:, c, :], xc[:, c, :]).then_inc(conv_hi, 1)
            pair_stage("xr", xr, start=False, after=lambda k: conv_parts(k - 2) if k >= 2 else None)
            conv_parts(2)
            conv_parts(3)
            round_next("gates", 0)
            for c in range(C):
                r = PAIR["gates"] + c
                act.wait_ge(even_done, r + 1)
                nc.scalar.activation(r_t[:, c, :], bank[2 * (r % 2)][:, 0:T], ACT.Sigmoid, bias=vec("ba", c))\
                  .then_inc(act_read, 1)
            act.wait_ge(dve_read, PAIR["lat"])
            nc.scalar.activation(i_t[:, :, :], i_t[:, :, :], ACT.Sigmoid).then_inc(lru_act, 1)

            def lat(k, i, ps):
                dst = (ckvf[:, 0, :], kr_raw, cqf[:, 1, :])[k]
                src = ps[:, 0:T] if k < 2 else ps[:, META:T]
                copy(dst, src).then_inc(act_read, 1)

            def decay(k):
                if k == 0:
                    act.wait_ge(lam_c, 2)
                    act.wait_ge(act_read, PAIR["lat"])
                    for c in range(C):
                        last = nc.scalar.activation(a_t[:, c, :], r_t[:, c, :], ACT.Exp, scale=cl[:, c:c + 1])
                    last.then_inc(lru_act, 1)
                if k == 1:
                    act.wait_ge(lru_act, 2)
                    for c in range(C):
                        last = nc.scalar.activation(r_t[:, c, :], r_t[:, c, :], ACT.Tanh, scale=ncl[:, c:c + 1])
                    last.then_inc(lru_act, 1)
            pair_stage("lat", lat, before=decay)

            def gr_in(k, i, ps):
                copy(gr[:, 2 * k, :], ps[:, 0:S]).then_inc(act_read, 1)

            def root(k):
                if k == 1:
                    act.wait_ge(lru_dve, 1)
                    nc.scalar.activation(r_t[:, :, :], r_t[:, :, :], ACT.Sqrt).then_inc(lru_act, 1)
                if k == 3:
                    gelu(0, 6)

            def gelu(first, end):
                act.wait_ge(act_read, PAIR["gr"] + end // 2)
                act.wait_ge(dve_read, PAIR["gr"] + end // 2)
                nc.scalar.activation(gr[:, first:end, :], gr[:, first:end, :], ACT.Gelu_apprx_tanh).then_inc(lru_act, 1)
            pair_stage("gr", gr_in, before=root, after=lambda k: norm_hi("cq", S, cqn, QL) if k == 2 else None)
            round_next("uq", 0)
            gelu(6, C)
            norm_hi("ckv", T, ckvn, KVL)
            act.wait_ge(y_f, 2)
            copy(y_rnn[0], gr[:, :, :]).then_inc(y_hi, 1)

            for k in range(4):
                if k:
                    round_next("uq", k)
                for c in (0, 2):
                    r = PAIR["uq"] + 2 * k + c // 2
                    act.wait_ge(even_done, r + 1)
                    ps = bank[2 * (r % 2)]
                    if k < 2:
                        m = 4 * k + c
                        copy(qh[0:64, 2 * m, :], ps[0:64, 0:S])
                        copy(qh[0:64, 2 * m + 1, :], ps[64:128, 0:S]).then_inc(act_read, 1)
                    else:
                        if r - PAIR["uq"] >= 5:
                            act.wait_ge(rope_in, 4 * (r - PAIR["uq"] - 4))
                        copy(sg[0], ps[:, 0:S]).then_inc(act_read, 1)
            round_next("uk", 0)
            for m in range(4):
                r = PAIR["uk"] + m
                act.wait_ge(even_done, r + 1)
                ps = bank[2 * (r % 2)]
                copy(kh[0:64, 4 * m, :], ps[0:64, 0:T])
                copy(kh[0:64, 4 * m + 1, :], ps[64:128, 0:T]).then_inc(act_read, 1)
            round_next("uv", 0)
            act.wait_ge(kr_ready, 1)
            for t in range(3):
                r = PAIR["uv"] + t
                act.wait_ge(even_done, r + 1)
                copy(vt[:, t, 0:512], bank[2 * (r % 2)][:, :]).then_inc(act_read, 1)
            stage_start("mix")


            def exps(h, i):
                u = h % 2
                p, s = probs[u], bank[4 + u]
                act.wait_ge(sc_masked, h + 1 + 4 * i)
                if h >= 2:
                    act.wait_ge(tr_done, h - 1 + 4 * i)
                for t, (at, n, dst) in enumerate(((0, SA, 0), (SA, SB, 256))):
                    nc.scalar.activation(p[:, dst:dst + n], s[:, at:at + n], ACT.Exp, bias=soft[:, 2 * u + t:2 * u + t + 1],
                                         accum_out=soft[:, 4 + 2 * u + t:5 + 2 * u + t]).then_inc(exp_done, 1)

            def copy_pt(h, i):
                u = h % 2
                act.wait_ge(tr_done, h + 1 + 4 * i)
                if h >= 2:
                    act.wait_ge(pv_done, h - 1 + 4 * i)
                copy(pt[u][:, 0:512], bank[6 + u][:, :]).then_inc(ptx, 1)
                if h >= 2 and h % 2 == 0:
                    take_o(h // 2 - 1, i)

            def take_o(m, i):
                act.wait_ge(pv_done, 2 * m + 2 + 4 * i)
                copy(part(op_hi, C * S + S * m, S, i, 2 * S), bank[m % 2][:, 0:S]).then_inc(o_hi, 1)

            def turn(t, i):
                for u in range(4):
                    exps(4 * t + u, i)
                    if 4 * t + u >= 1:
                        copy_pt(4 * t + u - 1, i)
            act.wait_ge(y_lo, 1)
            turn(0, 0)
            with act.Fori(0, 3) as i:
                turn(1, i)
            copy_pt(H - 1, 0)
            take_o(H // 2 - 1, 0)

            def mix(k, i, ps):
                r = PAIR["mix"] + k
                act.wait_ge(dve_read, r - 1 + 4 * i)
                nc.scalar.activation(sg[k % 2], ps[:, 0:S], ACT.Sigmoid).then_inc(act_read, 1)

            def mix_round(m, i):
                act.wait_ge(mix_f, m + 1 + 2 * i)
                copy(part(op_hi, 2 * C * S + S * m, S, i, 2 * S), xf[1][:, 0:S]).then_inc(mix_hi, 1)

            def step(k, i):
                round_next("mix", k, i)
                if k >= 2 and k % 2 == 0:
                    mix_round(k // 2 - 1, i)
                act.wait_ge(even_done, PAIR["mix"] + k + 1 + 4 * i)
                mix(k, i, bank[2 * ((PAIR["mix"] + k) % 2)])
            each(act, BLOCKS["mix"], step, peel=True)
            mix_round(C - 1, 0)
            residual_stage("out1")
            if stop == "out1":
                return

            def norm_hi_of(name, src, dst):
                norm_root(name, S, D)
                for c in range(C):
                    act.wait_ge(xf_done, SPLIT0[name] + c + 1)
                    copy(dst[0][:, c, :], src[:, c, :]).then_inc(xhi_done, 1)
            norm_hi_of("n2", x_f, xq)
            def take_queries(h):
                act.wait_ge(q_done, h + 1)
                if h >= 2:
                    act.wait_ge(key_done, h - 1)
                copy(q_at[h], bank[h % 2][:, :]).then_inc(q_read, 1)

            def expert_weights(n):
                h, t = n // 2, n % 2
                act.wait_ge(top_max, n + 1)
                nc.scalar.activation(gw[h % 2][:, 16 * t:16 * t + 16], top["best"], ACT.Exp, bias=top["neg"],
                                     accum_out=top["sum"]).then_inc(top_exp, 1)

            def coefficient(n, s, i):
                q = TOPK * n + s
                i4 = 0 if isinstance(i, int) else 4 * i
                act.wait_ge(dot_done, q + 1 + i4)
                chain.link(nc.scalar.activation(coef[:, s % 4:s % 4 + 1], dots[:, s % 4:s % 4 + 1], ACT.Gelu_apprx_tanh))
                at = TOPK * (n % 2) + s
                g = gw[n // 2 % 2]
                weight = g[:, at:at + 1] if isinstance(i, int) else g[:, bass.ds(at + i4, 1)]
                chain.link(nc.scalar.activation(coef[:, 4 + s % 4:5 + s % 4], coef[:, s % 4:s % 4 + 1], ACT.Copy, scale=weight))
                if q >= 2:
                    act.wait_ge(row_used, q - 1 + i4)
                nc.scalar.activation(diag[s % 2], ident, ACT.Copy, scale=coef[:, 4 + s % 4:5 + s % 4]).then_inc(diag_done, 1)

            round_next("pq", 0)
            take_queries(0)
            for t in range(2):
                act.wait_ge(xt_ps, t + 1)
                copy(x_tok[:, t, 0:512], bank[4 + 2 * t][:, :]).then_inc(xt_read, 1)
            take_queries(1)
            round_next("pq", 1)
            expert_weights(0)
            for n in range(2 * PH):
                for s in range(8):
                    if n == 0 and s == 5:
                        expert_weights(1)
                    if n == 0:
                        coefficient(n, s, 0)
                if n > 0:
                    chain.loop(2, 8, lambda i: [coefficient(n, s, i) for s in range(4)])
                if n % 2 and n // 2 + 2 < PH:
                    take_queries(n // 2 + 2)
                if 1 <= n < 2 * PH - 2:
                    expert_weights(n + 2)
                for s in range(8, 16):
                    if n == 0 and s == 13:
                        expert_weights(2)
                    if n == 0:
                        coefficient(n, s, 0)
                if n > 0:
                    chain.loop(2, 8, lambda i: [coefficient(n, 8 + s, i) for s in range(4)])
                if n % 2 and n // 2 + 2 < PH:
                    round_next("pq", n // 2 + 2)
            for t in range(2):
                act.wait_ge(row_used, 16 * (2 * PH - 1 + t))
                copy(y_tok[:, t, 0:512], bank[4 + 2 * t][:, :]).then_inc(y_tok_act, 1)
            squares("final1", hs, S, peer_h, squares2)
            norm_root("final1", S, D)
            if stop == "pq":
                return

            def swiglu(f, norm, following):
                def hi(k, i):
                    act.wait_ge(dve_read, PAIR[f"ffi{f}"] + k + 1 + 4 * i)
                    copy(part(op_hi, S * k, S, i, 4 * S), xf[k % 2][:, 0:S]).then_inc(in_hi, 1)

                def up(k, i, ps):
                    if k:
                        hi(k - 1, i)
                    act.wait_ge(gate_in, NF * f + k + 1 + 4 * i)
                    nc.scalar.activation(sg[k % 2], xf[k % 2][:, 0:S], ACT.Silu).then_inc(act_read, 1)
                if norm == "f2":
                    norm_hi(norm, S, xq)
                pair_stage(f"ffi{f}", up, norm=norm if norm != "f2" else None)
                hi(NF - 1, 0)
                residual_stage(f"ffo{f}", following)

            for c in range(C):
                act.wait_ge(xf_done, SPLIT0["f0"] + c + 1)
                copy(xq[0][:, c, :], xf[c % 2][:, 0:S]).then_inc(xhi_done, 1)
                nc.scalar.activation(squares2[:, c, :], hs[:, c, :], ACT.Square).then_inc(sq_done, 1)
            swiglu(0, "f0", "mix0")
            if stop == "ffo0":
                return

            def qk_in(k, i, ps):
                copy(part(arena, 2 * S * k, S, i, 8 * S), ps[:, 0:S]).then_inc(act_read, 1)
            pair_stage("qk", qk_in, norm="mix0")
            stage_start("sbv")
            for k in range(4):
                round_next("sbv", k)

            def over_rms(norm, o, ps, t):
                act.wait_ge(rs_done, NORM[norm] + 1)
                return nc.scalar.activation(o, ps, ACT.Copy, scale=acc[NORM[norm] % 2][:, S + t:S + t + 1])
            for t in range(2):
                r = PAIR["sbv"] + t
                act.wait_ge(even_done, r + 1)
                over_rms("mix0", sv[:, t, 0:512], bank[2 * (r % 2)][:, :], t).then_inc(act_read, 1)

            def exp_in(h, i):
                act.wait_ge(z_mask, h + 1 + 4 * i)
                nc.scalar.activation(az[h % 2], az[h % 2], ACT.Exp).then_inc(soft_exp, 1)

            def log_part(h, i):
                act.wait_ge(soft_exp, h + 1 + 4 * i)
                nc.scalar.activation(az[h % 2], az[h % 2], ACT.Ln, bias=1.0).then_inc(soft_in, 1)

            def weights(h, i):
                act.wait_ge(arg_done, h + 1 + 4 * i)
                if h >= 2:
                    act.wait_ge(sbo_done, h - 1 + 4 * i)
                nc.scalar.activation(wt[h % 2], ex[h % 2], ACT.Exp).then_inc(w_done, 1)

            def sb_take(m, i):
                act.wait_ge(sbo_done, 2 * m + 2 + 4 * i)
                copy(part(op_hi, S * m, S, i, 2 * S), bank[m % 2][:, 0:S]).then_inc(sbo_hi, 1)

            def sb_pair(m, i, last=False):
                log_part(2 * m, i)
                log_part(2 * m + 1, i)
                if m:
                    weights(2 * m - 2, i)
                    weights(2 * m - 1, i)
                if m >= 2:
                    sb_take(m - 2, i)
                if not last:
                    exp_in(2 * m + 2, i)
                    exp_in(2 * m + 3, i)
            exp_in(0, 0)
            exp_in(1, 0)
            sb_pair(0, 0)
            sb_pair(1, 0)
            with act.Fori(0, 2) as i:
                sb_pair(2, i)
                sb_pair(3, i)
            sb_pair(6, 0)
            sb_pair(7, 0, last=True)
            weights(H - 2, 0)
            weights(H - 1, 0)
            sb_take(H // 2 - 2, 0)
            sb_take(H // 2 - 1, 0)
            residual_stage("sbo", "f1")
            if stop == "sbo":
                return
            swiglu(1, "f1", "kv")
            pair_stage("kvk", lambda k, i, ps: copy(k_raw[:, 0, :], ps[:, 0:S]).then_inc(act_read, 1), norm="kv")
            pair_stage("kvv", lambda k, i, ps: over_rms("kv", v_sh[:, 0, :], ps[:, 0:S], 0).then_inc(act_read, 1))
            swiglu(2, "f2", "mix1")
            pair_stage("sq", lambda k, i, ps: copy(q_sw[:, 2 * k, :], ps[:, 0:S]).then_inc(act_read, 1), norm="mix1")
            act.wait_ge(k_rot, 2)

            def sink(h, i):
                act.wait_ge(w_sc, h + 1 + 4 * i)
                src = sinks[:, h:h + 1] if isinstance(i, int) else soft[:, bass.ds(25 + h + 4 * i, 1)]
                copy(four[h % 4][:, P:P + 1], src).then_inc(sink_in, 1)

            def sw_exps(h, i):
                u = h % 4
                act.wait_ge(w_mask, h + 1 + 4 * i)
                if h >= 4:
                    act.wait_ge(w_tr, h - 3 + 4 * i)
                for t, (at, n, dst) in enumerate(((0, P + 1, 0), (P, S + 1, P + 1))):
                    nc.scalar.activation(sw_p[u][:, dst:dst + n], four[u][:, at:at + n], ACT.Exp,
                                         bias=soft[:, 2 * u + t:2 * u + t + 1],
                                         accum_out=soft[:, 8 + 2 * u + t:9 + 2 * u + t]).then_inc(w_exp, 1)

            def sw_copy(h, i):
                act.wait_ge(w_tr, h + 1 + 4 * i)
                if h >= 2:
                    act.wait_ge(w_pv, h - 1 + 4 * i)
                copy(sw_pt[h % 2], bank[6 + h % 2][:, 0:384]).then_inc(w_pt, 1)
                if h >= 2 and h % 2 == 0:
                    sw_take(h // 2 - 1, i)

            def sw_take(m, i):
                act.wait_ge(w_pv, 2 * m + 2 + 4 * i)
                copy(part(op_hi, S * m, S, i, 2 * S), bank[m % 2][:, 0:S]).then_inc(w_hi_o, 1)

            def sw_head(h, i):
                sw_exps(h, i)
                sink(h + 2, i)
                if h >= 1:
                    sw_copy(h - 1, i)
            sink(0, 0)
            sink(1, 0)
            for h in range(4):
                sw_head(h, 0)
            with act.Fori(0, 2) as i:
                for h in range(4, 8):
                    sw_head(h, i)
            for h in range(H - 4, H):
                sw_exps(h, 0)
                if h + 2 < H:
                    sink(h + 2, 0)
                sw_copy(h - 1, 0)
            sw_copy(H - 1, 0)
            sw_take(H // 2 - 1, 0)
            residual_stage("swo", "f3")
            swiglu(3, "f3", None)
            norm_root("final2", S, D)

        @block.vector
        def _(dve):
            v = nc.vector
            chain = Chain(dve, dve_step)
            link = chain.link

            def part(t, at, n, i=0, step=0):
                return t[:, at:at + n] if isinstance(i, int) else t[:, bass.ds(at + step * i, n)]

            def rest_of_block(b, cols, i=0):
                dve.wait_ge(hi_done, b + 1 + 4 * i)
                v.tensor_tensor(w_lo[b % 2][:, 0:cols], raw[b % RAW][:, 0:cols], w_hi[b % 2][:, 0:cols].bitcast(F32),
                                ALU.subtract).then_inc(lo_done, 1)

            def rest_next(name, k, i=0):
                b = FIRST[name] + k + 1
                if b >= END or (name == stop and k == BLOCKS[name] - 1 and isinstance(i, int)):
                    return
                nxt = name if k + 1 < BLOCKS[name] else ORDER[ORDER.index(name) + 1]
                rest_of_block(b, WIDTH[nxt], i)

            def pair_stage(name, body, tail=0, before=None, after=None, norm=None):
                def step(k, i):
                    rest_next(name, k, i)
                    if norm and k == 0:
                        inverse_rms(norm)
                    if before:
                        before(k)
                    r = PAIR[name] + k
                    dve.wait_ge(odd_done, r + 1 + 4 * i)
                    body(k, i, bank[2 * (r % 2) + 1])
                    if after:
                        after(k)
                each(dve, BLOCKS[name], step, tail, peel=norm is not None)

            def square_sum(name, src, n, c, count):
                j = NORM[name]
                a = acc[j % 2][:, 0:n]
                if c == 0:
                    ins = v.tensor_tensor(a, src, src, ALU.mult)
                else:
                    link(v.tensor_tensor(xf[0][:, 0:n], src, src, ALU.mult))
                    ins = v.tensor_tensor(a, a, xf[0][:, 0:n], ALU.add)
                if c == count - 1:
                    ins.then_inc(ss_in, 1)
                else:
                    link(ins)

            def inverse_rms(name, n=S):
                j = NORM[name]
                a = acc[j % 2][:, 0:S + 2 if name in ("mix0", "kv") else n]
                dve.wait_ge(sd_done, j + 1)
                v.reciprocal(a, a).then_inc(rs_done, 1)
                dve.wait_ge(rs_done, j + 1)

            def norm_apply(name, src, n, dst, full=None):
                def whole(c):
                    return xf[c % 2][:, 0:n] if full is None else full[:, c, :]
                j, s0 = NORM[name], SPLIT0[name]
                a = acc[j % 2][:, 0:n]
                if name not in AFTER:
                    inverse_rms(name, n)
                count = dict(NORMS)[name]

                def rest(c):
                    dve.wait_ge(xhi_done, s0 + c + 1)
                    v.tensor_tensor(dst[1][:, c, 0:n], whole(c), dst[0][:, c, 0:n].bitcast(F32), ALU.subtract)\
                     .then_inc(xlo_done, 1)
                for c in range(count):
                    if c >= 2:
                        rest(c - 2)
                        dve.wait_ge(xlo_done, s0 + c - 1)
                    if name in AFTER:
                        ins = v.tensor_scalar(whole(c), src[:, c, :], vec(name, c), None, ALU.mult)
                    else:
                        ins = v.scalar_tensor_tensor(whole(c), src[:, c, :], vec(name, c), a, ALU.mult, ALU.mult)
                    ins.then_inc(xf_done, 1)
                for c in range(max(0, count - 2), count):
                    rest(c)
                dve.wait_ge(xlo_done, s0 + count)

            def residual_stage(name, norm, scale=1.0):
                j = NORM[norm]
                a = acc[j % 2][:, 0:S]
                link(v.memset(a, 0.0))
                halves = name.startswith("ffo")
                after = norm in AFTER

                def chunk(m, i):
                    n = RES[name] + m
                    dve.wait_ge(res_done, n + 1 + 2 * i)
                    hc = h_t[:, m, META:T] if isinstance(i, int) else h_all[:, bass.ds(T * m + META + 2 * T * i, S)]
                    v.scalar_tensor_tensor(hc, bank[4 + n % 2][:, 0:S], scale, hc, ALU.mult, ALU.add).then_inc(h_new, 1)
                    dve.wait_ge(h_new, n + 1 + 2 * i)
                    if after:
                        gain = vec(norm, m) if isinstance(i, int) else vecs[:, bass.ds(V_AT[norm][0] + m + 2 * i, 1)]
                        v.tensor_scalar(sg[m % 2], hc, gain, None, ALU.mult).then_inc(xf_done, 1)
                    link(v.tensor_tensor(xf[0][:, 0:S], hc, hc, ALU.mult))
                    ins = v.tensor_tensor(a, a, xf[0][:, 0:S], ALU.add)
                    if m == C - 1 and isinstance(i, int):
                        ins.then_inc(ss_in, 1)
                    else:
                        link(ins)

                def lo(m, i=0):
                    dve.wait_ge(xhi_done, SPLIT0[norm] + m + 1 + 2 * i)
                    v.tensor_tensor(part(xn_lo, T * m, S, i, 2 * T), sg[m % 2],
                                    part(xn_hi, T * m, S, i, 2 * T).bitcast(F32), ALU.subtract).then_inc(xlo_done, 1)
                    dve.wait_ge(xlo_done, SPLIT0[norm] + m + 1 + 2 * i)

                def step(k, i):
                    rest_next(name, k, i)
                    if after and k >= 1 and not (halves and k % 2):
                        for m in (k // 2 - 1,) if halves else (2 * k - 2, 2 * k - 1):
                            lo(m, i)
                    for m in () if halves and k % 2 == 0 else (k // 2,) if halves else (2 * k, 2 * k + 1):
                        chunk(m, i)
                if halves:
                    for k in range(RAW):
                        step(k, 0)
                    chain.loop(2, 4, lambda i: [step(RAW + k, i) for k in range(RAW)])
                for k in range(3 * RAW if halves else 0, BLOCKS[name]):
                    step(k, 0)
                if after:
                    for m in (C - 1,) if halves else (C - 2, C - 1):
                        lo(m)

            dve.wait_ge(x_in, 16)
            dve.wait_ge(first_in, 32)
            rest_of_block(0, TILE)
            norm_apply("n1", h_t, T, xn)

            def xr(k, i, ps):
                v.tensor_copy(xrp[:, 2 * k + 1, 3:3 + T], ps[:, 0:T]).then_inc(dve_read, 1)

            def convolve(k):
                dve.wait_ge(act_read, PAIR["xr"] + k + 1)
                dve.wait_ge(dve_read, PAIR["xr"] + k + 1)
                dve.wait_ge(pads, 2)
                for c in (2 * k,) if k < 3 else (2 * k, 2 * k + 1):
                    y = xc[:, c, :]
                    link(v.tensor_scalar(y, xrp[:, c, 0:T], vec("cw0", c), vec("cb", c), ALU.mult, ALU.add))
                    for t in (1, 2, 3):
                        ins = v.scalar_tensor_tensor(y, xrp[:, c, t:t + T], vec(f"cw{t}", c), y, ALU.mult, ALU.add)
                        ins.then_inc(conv_dve, 1) if t == 3 else link(ins)

            def after_xr(k):
                if k >= 1:
                    convolve(k - 1)
            pair_stage("xr", xr, after=after_xr)
            convolve(3)
            rest_next("gates", 0)
            for c in range(C):
                r = PAIR["gates"] + c
                dve.wait_ge(odd_done, r + 1)
                v.tensor_scalar(i_t[:, c, :], bank[2 * (r % 2) + 1][:, 0:T], vec("bx", c), None, ALU.add)\
                 .then_inc(dve_read, 1)

            dve.wait_ge(lam_e, 1)
            e, z, z2, q, lam = (lam_t[:, C * n:C * n + C] for n in (0, 2, 3, 4, 5))
            link(v.tensor_scalar(z2, e, 2.0, None, ALU.add))
            link(v.reciprocal(z2, z2))
            link(v.tensor_tensor(z, z2, e, ALU.mult))
            link(v.tensor_tensor(z2, z, z, ALU.mult))
            link(v.tensor_scalar(q, z2, 1.0 / 17, None, ALU.mult))
            for n in (15, 13, 11, 9, 7, 5, 3):
                link(v.scalar_tensor_tensor(q, q, 1.0 / n, z2, ALU.add, ALU.mult))
            link(v.scalar_tensor_tensor(q, q, 1.0, z, ALU.add, ALU.mult))
            link(v.tensor_scalar(lam, vecs[:, V_AT["lam"][0]:V_AT["lam"][0] + C], -1.0, 0.0, ALU.mult, ALU.max))
            link(v.scalar_tensor_tensor(lam, q, 2.0, lam, ALU.mult, ALU.add))
            v.tensor_scalar(ncl, lam, 8.0, None, ALU.mult).then_inc(lam_c, 1)
            v.tensor_scalar(cl, lam, -8.0, None, ALU.mult).then_inc(lam_c, 1)

            dve.wait_ge(const_in, 48)

            def lat(k, i, ps):
                dst = (ckvf[:, 1, :], cqf[:, 0, :], cqf[:, 2, :])[k]
                v.tensor_copy(dst, ps[:, 0:T] if k < 1 else ps[:, META:T]).then_inc(dve_read, 1)
            pair_stage("lat", lat)

            def recurrence(k):
                if k == 0:
                    dve.wait_ge(lru_act, 3)
                    dve.wait_ge(lru_pool, 2)
                    v.scalar_tensor_tensor(r_t[:, :, :], xc[:, :, :], 1.0, r_t[:, :, :], ALU.add, ALU.mult)\
                     .then_inc(lru_dve, 1)
                    dve.wait_ge(dve_read, PAIR["gr"])
                    dve.wait_ge(act_read, PAIR["gr"])
                    for c in range(3):
                        square_sum("cq", cqf[:, c, :], S, c, 3)
                    for c in range(2):
                        square_sum("ckv", ckvf[:, c, :], T, c, 2)
                if k == 1:
                    dve.wait_ge(lru_act, 4)
                    link(v.tensor_tensor(i_t[:, :, :], i_t[:, :, :], r_t[:, :, :], ALU.mult))
                    for c in range(C):
                        ins = v.tensor_tensor_scan(xc[:, c, :], a_t[:, c, :], i_t[:, c, :], 0.0, ALU.mult, ALU.add)
                    link(ins)
                if k == 2:
                    dve.wait_ge(pads, 4)
                    norm_apply("cq", cqf, S, cqn)

            def gr_in(k, i, ps):
                v.tensor_copy(gr[:, 2 * k + 1, :], ps[:, 0:S]).then_inc(dve_read, 1)
            def branch(first, end, count):
                dve.wait_ge(lru_act, count)
                v.tensor_tensor(gr[:, first:end, :], gr[:, first:end, :], xc[:, first:end, META:T], ALU.mult).then_inc(y_f, 1)
            pair_stage("gr", gr_in, after=recurrence, before=lambda k: branch(0, 6, 5) if k == 3 else None)
            branch(6, C, 6)
            rest_next("uq", 0)
            norm_apply("ckv", ckvf, T, ckvn)
            link(v.tensor_tensor(kr_rot[0:32, :], kr_raw[0:32, :], cos_t[0:32, :], ALU.mult))
            link(v.tensor_tensor(xf[0][0:32, :], kr_raw[32:64, :], sin_t[32:64, :], ALU.mult))
            link(v.tensor_tensor(kr_rot[0:32, :], kr_rot[0:32, :], xf[0][0:32, :], ALU.add))
            for g in range(H // 8):
                ins = v.tensor_copy(kh[64:96, 8 * g:8 * g + 8, :],
                                    kr_rot[0:32, :].unsqueeze(1).to_broadcast([32, 8, T]))
            ins.then_inc(kr_ready, 1)
            dve.wait_ge(y_hi, 1)
            v.tensor_tensor(y_rnn[1], gr[:, :, :], y_rnn[0].bitcast(F32), ALU.subtract).then_inc(y_lo, 1)

            for k in range(4):
                if k:
                    rest_next("uq", k)
                for c in (1, 3):
                    r = PAIR["uq"] + 2 * k + c // 2
                    dve.wait_ge(odd_done, r + 1)
                    ps = bank[2 * (r % 2) + 1]
                    if k < 2:
                        m = 4 * k + c
                        v.tensor_copy(qh[0:64, 2 * m, :], ps[0:64, 0:S])
                        v.tensor_copy(qh[0:64, 2 * m + 1, :], ps[64:128, 0:S]).then_inc(dve_read, 1)
                    else:
                        g = r - PAIR["uq"] - 4
                        v.tensor_tensor(sg[1], ps[:, 0:S], sin_t[:, META:T], ALU.mult).then_inc(dve_read, 1)
                        dve.wait_ge(act_read, r + 1)
                        link(v.tensor_tensor(xf[0][:, 0:S], sg[0], cos_t[:, META:T], ALU.mult))
                        dve.wait_ge(dve_read, r + 1)
                        for a in range(4):
                            rows = slice(32 * a, 32 * a + 32)
                            v.tensor_tensor(qh[64:96, 4 * g + a, :], xf[0][rows, 0:S], sg[1][rows, :], ALU.add)\
                             .then_inc(rope_in, 1)
                        dve.wait_ge(rope_in, 4 * g + 4)
            rest_next("uk", 0)
            for m in range(4):
                r = PAIR["uk"] + m
                dve.wait_ge(odd_done, r + 1)
                ps = bank[2 * (r % 2) + 1]
                v.tensor_copy(kh[0:64, 4 * m + 2, :], ps[0:64, 0:T])
                v.tensor_copy(kh[0:64, 4 * m + 3, :], ps[64:128, 0:T]).then_inc(dve_read, 1)
            for t in range(3):
                r = PAIR["uv"] + t
                dve.wait_ge(odd_done, r + 1)
                v.tensor_copy(vt[:, t, 512:1024], bank[2 * (r % 2) + 1][:, :]).then_inc(dve_read, 1)
            rest_next("uv", 0)
            dve.wait_ge(y_lo, 1)
            for p in probs:
                link(v.memset(p[:, SA:S], 0.0))
                link(v.memset(p[:, S + SB:640], 0.0))

            def mask(h, i):
                u = h % 2
                s = bank[4 + u]
                dve.wait_ge(sc_done, h + 1 + 4 * i)
                link(v.scalar_tensor_tensor(s[:, 0:416], s[:, 0:416], MLA_SCALE, mla_mask, ALU.mult, ALU.add))
                link(v.tensor_reduce(soft[:, 2 * u:2 * u + 1], s[:, 0:SA], AX.X, ALU.max, negate=True))
                v.tensor_reduce(soft[:, 2 * u + 1:2 * u + 2], s[:, SA:SA + SB], AX.X, ALU.max, negate=True)\
                 .then_inc(sc_masked, 1)

            def normalise(h, i):
                u = h % 2
                p = probs[u]
                dve.wait_ge(exp_done, 2 * h + 2 + 8 * i)
                link(v.reciprocal(soft[:, 8 + 2 * u:10 + 2 * u], soft[:, 4 + 2 * u:6 + 2 * u]))
                v.tensor_scalar(p[:, 0:SA], p[:, 0:SA], soft[:, 8 + 2 * u:9 + 2 * u], None, ALU.mult).then_inc(p_ready, 1)
                v.tensor_scalar(p[:, 256:256 + SB], p[:, 256:256 + SB], soft[:, 9 + 2 * u:10 + 2 * u], None, ALU.mult)\
                 .then_inc(p_ready, 1)

            def copy_fifth(h, i):
                u = h % 2
                dve.wait_ge(tr_done, h + 1 + 4 * i)
                if h >= 2:
                    dve.wait_ge(pv_done, h - 1 + 4 * i)
                v.tensor_copy(pt[u][:, 512:640], bank[2 + u][:, 0:P]).then_inc(pty, 1)
                if h >= 2 and h % 2 == 0:
                    rest_o(h // 2 - 1, i)

            def rest_o(m, i):
                dve.wait_ge(o_hi, m + 1 + 2 * i)
                v.tensor_tensor(part(op_lo, C * S + S * m, S, i, 2 * S), bank[m % 2][:, 0:S],
                                part(op_hi, C * S + S * m, S, i, 2 * S).bitcast(F32), ALU.subtract).then_inc(o_lo, 1)

            def turn(t, i):
                for u in range(4):
                    mask(4 * t + u, i)
                    if 4 * t + u >= 1:
                        normalise(4 * t + u - 1, i)
                    if 4 * t + u >= 2:
                        copy_fifth(4 * t + u - 2, i)
            turn_links = 12
            turn(0, 0)
            chain.loop(3, turn_links, lambda i: turn(1, i))
            normalise(H - 1, 0)
            copy_fifth(H - 2, 0)
            copy_fifth(H - 1, 0)
            rest_o(H // 2 - 1, 0)

            def mix(k, i, ps):
                r = PAIR["mix"] + k
                dve.wait_ge(act_read, r + 1 + 4 * i)
                if k % 2 == 0:
                    v.tensor_tensor(xf[0][:, 0:S], sg[0], ps[:, 0:S], ALU.mult).then_inc(dve_read, 1)
                    return
                v.tensor_tensor(acc[0][:, 0:S], sg[1], ps[:, 0:S], ALU.mult).then_inc(dve_read, 1)
                dve.wait_ge(dve_read, r + 1 + 4 * i)
                v.tensor_tensor(xf[1][:, 0:S], xf[0][:, 0:S], acc[0][:, 0:S], ALU.add).then_inc(mix_f, 1)

            def mix_rest(m, i):
                dve.wait_ge(mix_hi, m + 1 + 2 * i)
                at = 2 * C * S + S * m
                v.tensor_tensor(part(op_lo, at, S, i, 2 * S), xf[1][:, 0:S], part(op_hi, at, S, i, 2 * S).bitcast(F32),
                                ALU.subtract).then_inc(mix_lo, 1)
                dve.wait_ge(mix_lo, m + 1 + 2 * i)

            def step(k, i):
                rest_next("mix", k, i)
                if k >= 2 and k % 2 == 0:
                    mix_rest(k // 2 - 1, i)
                dve.wait_ge(odd_done, PAIR["mix"] + k + 1 + 4 * i)
                mix(k, i, bank[2 * ((PAIR["mix"] + k) % 2) + 1])
            each(dve, BLOCKS["mix"], step, peel=True)
            mix_rest(C - 1, 0)
            residual_stage("out1", "n2")
            if stop == "out1":
                return

            norm_apply("n2", hs, S, xq, full=x_f)
            def top16(values, n, best, index, left):
                link(v.max(best[:, 0:8], values))
                yield
                link(v.max_index(index[:, 0:8], best[:, 0:8], values))
                yield
                link(v.match_replace(left, best[:, 0:8], values, -3.0e38))
                yield
                link(v.max(best[:, 8:16], left))
                yield
                link(v.max_index(index[:, 8:16], best[:, 8:16], left))
                yield

            iota = small[:, 0:TOPK]

            def pick(dst, which, values):
                hit = top["hit"].rearrange("p (k a) -> p k a", a=TOPK)
                link(v.tensor_tensor(hit, which.unsqueeze(2).to_broadcast([P, TOPK, TOPK]),
                                     iota.unsqueeze(1).to_broadcast([P, TOPK, TOPK]), ALU.is_equal))
                yield
                link(v.tensor_tensor(hit, hit, values.unsqueeze(1).to_broadcast([P, TOPK, TOPK]), ALU.mult))
                yield
                link(v.tensor_reduce(dst, hit, AX.X, ALU.add))
                yield

            def experts(n):
                h, t = n // 2, n % 2
                ps = bank[2 + h % 2]
                dve.wait_ge(key_done, h + 1)
                for c, (tv, ti, tf) in enumerate((("t1", "i1", "f1"), ("t2", "i2", "f2"))):
                    yield from top16(ps[:, P * (2 * t + c):P * (2 * t + c + 1)], NKEY, top[tv], top[ti].bitcast(U32), top["s"])
                    link(v.tensor_copy(top[tf], top[ti].bitcast(U32)))
                    yield
                cand = top["cand"].rearrange("p (a b) -> p a b", b=TOPK)
                link(v.tensor_tensor(cand, top["t1"].unsqueeze(2).to_broadcast([P, TOPK, TOPK]),
                                     top["t2"].unsqueeze(1).to_broadcast([P, TOPK, TOPK]), ALU.add))
                yield
                if n >= 1:
                    dve.wait_ge(top_exp, n)
                yield from top16(top["cand"], 256, top["best"], top["at"].bitcast(U32), top["left"])
                v.tensor_scalar(top["neg"], top["best"][:, 0:1], -1.0, None, ALU.mult).then_inc(top_max, 1)
                for to, op, by, f in (("hi", ALU.logical_shift_right, 4, "fh"), ("lo", ALU.bitwise_and, 15, "fl")):
                    link(v.tensor_scalar(top[to].bitcast(U32), top["at"].bitcast(U32), by, None, op))
                    yield
                    link(v.tensor_copy(top[f], top[to].bitcast(U32)))
                    yield
                yield from pick(top["e1"], top["fh"], top["f1"])
                yield from pick(top["e2"], top["fl"], top["f2"])
                if n >= 4:
                    dve.wait_ge(row_used, TOPK * (n - 3))
                dve.wait_ge(top_exp, n + 1)
                link(v.reciprocal(top["rs"], top["sum"]))
                yield
                g = gw[h % 2][:, 16 * t:16 * t + 16]
                link(v.tensor_scalar(g, g, top["rs"], None, ALU.mult))
                yield
                v.scalar_tensor_tensor(expert[h % 2][:, 16 * t:16 * t + 16], top["e1"], float(NKEY), top["e2"],
                                       ALU.mult, ALU.add).then_inc(expert_in, 1)
                dve.wait_ge(expert_in, n + 1)

            def dot(n, s, i):
                q = 16 * n + s
                i4 = 0 if isinstance(i, int) else 4 * i
                turns = q // 4 + 1
                dve.wait_ge(gathered[s % 4], 16 * turns + (0 if isinstance(i, int) else 16 * i))
                if q >= 1:
                    dve.wait_ge(dot_done, q + i4)
                v.tensor_tensor_reduce(out=product, in0=pulled[s % 4][:, 0:D], in1=x_tok[:, n % 2, :], scale=1.0, scalar=0.0,
                                       op0=ALU.mult, op1=ALU.add, accum_out=dots[:, s % 4:s % 4 + 1]).then_inc(dot_done, 1)

            def advance(steps, count):
                for _ in range(count):
                    next(steps, None)

            rest_next("pq", 0)
            advance(experts(0), 40)
            for t in range(2):
                dve.wait_ge(xt_ps, t + 1)
                v.tensor_copy(x_tok[:, t, 512:D], bank[5 + 2 * t][:, :]).then_inc(xt_read, 1)
            dve.wait_ge(xt_read, 4)
            rest_next("pq", 1)
            for n in range(2 * PH):
                if n < 2 * PH - 2:
                    steps = experts(1 if n == 0 else n + 2)
                    for s in range(TOPK):
                        if n == 0 and s == 8:
                            steps = experts(2)
                        dot(n, s, 0)
                        advance(steps, 5 if n == 0 else 3)
                else:
                    with dve.Fori(0, 4) as i:
                        for s in range(4):
                            dot(n, s, i)
                if n % 2 and n // 2 + 2 < PH:
                    rest_next("pq", n // 2 + 2)
            for t in range(2):
                dve.wait_ge(row_used, 16 * (2 * PH - 1 + t))
                v.tensor_copy(y_tok[:, t, 512:D], bank[5 + 2 * t][:, :]).then_inc(y_tok_dve, 1)
            dve.wait_ge(y_back, 1)
            for c in range(C):
                v.tensor_tensor(hs[:, c, :], hs[:, c, :], bank[c // 2][:, S * (c % 2):S * (c % 2) + S], ALU.add)\
                 .then_inc(peer_h, 1)
            dve.wait_ge(peer_h, C)

            def norm_in_place(name):
                j = NORM[name]
                a = acc[j % 2][:, 0:S]
                dve.wait_ge(sd_done, j + 1)
                v.reciprocal(a, a).then_inc(rs_done, 1)
                dve.wait_ge(rs_done, j + 1)
                for c in range(C):
                    v.scalar_tensor_tensor(hs[:, c, :], hs[:, c, :], vec(name, c), a, ALU.mult, ALU.mult).then_inc(h_scaled, 1)

            inverse_rms("final1")
            rms = acc[NORM["final1"] % 2][:, 0:S]
            s0 = SPLIT0["f0"]

            def f0_rest(c):
                dve.wait_ge(xhi_done, s0 + c + 1)
                v.tensor_tensor(xq[1][:, c, :], xf[c % 2][:, 0:S], xq[0][:, c, :].bitcast(F32), ALU.subtract)\
                 .then_inc(xlo_done, 1)
                dve.wait_ge(xlo_done, s0 + c + 1)
            for c in range(C):
                v.scalar_tensor_tensor(hs[:, c, :], hs[:, c, :], vec("final1", c), rms, ALU.mult, ALU.mult)\
                 .then_inc(h_scaled, 1)
                if c >= 2:
                    f0_rest(c - 2)
                dve.wait_ge(h_scaled, c + 1)
                v.tensor_scalar(xf[c % 2][:, 0:S], hs[:, c, :], vec("f0", c), None, ALU.mult).then_inc(xf_done, 1)
            f0_rest(C - 2)
            f0_rest(C - 1)
            if stop == "pq":
                return

            def swiglu(f, norm, following, between=None):
                rms, u = acc[NORM[norm] % 2][:, 0:S], acc[(NORM[norm] + 1) % 2][:, 0:S]
                if norm == "f2":
                    norm_apply(norm, hs, S, xq)
                    between()

                def up(k, i, ps):
                    r, n = PAIR[f"ffi{f}"] + k, NF * f + k
                    dve.wait_ge(even_done, r + 1 + 4 * i)
                    v.tensor_tensor(xf[k % 2][:, 0:S], bank[2 * (r % 2)][:, 0:S], rms, ALU.mult).then_inc(gate_in, 1)
                    dve.wait_ge(odd_done, r + 1 + 4 * i)
                    v.tensor_tensor(u, ps[:, 0:S], rms, ALU.mult).then_inc(up_in, 1)
                    dve.wait_ge(up_in, n + 1 + 4 * i)
                    dve.wait_ge(act_read, r + 1 + 4 * i)
                    v.tensor_tensor(xf[k % 2][:, 0:S], sg[k % 2], u, ALU.mult).then_inc(dve_read, 1)

                def lo(k, i):
                    n = NF * f + k
                    dve.wait_ge(in_hi, n + 1 + 4 * i)
                    v.tensor_tensor(part(op_lo, S * k, S, i, 4 * S), xf[k % 2][:, 0:S],
                                    part(op_hi, S * k, S, i, 4 * S).bitcast(F32), ALU.subtract).then_inc(in_lo, 1)
                    dve.wait_ge(in_lo, n + 1 + 4 * i)

                def step(k, i):
                    rest_next(f"ffi{f}", k, i)
                    if k:
                        lo(k - 1, i)
                    if k == 0 and norm != "f2":
                        inverse_rms(norm)
                    up(k, i, bank[2 * ((PAIR[f"ffi{f}"] + k) % 2) + 1])
                each(dve, NF, step, peel=True)
                lo(NF - 1, 0)
                residual_stage(f"ffo{f}", following, 0.5)

            swiglu(0, "f0", "mix0")
            if stop == "ffo0":
                return
            inverse = acc[NORM["mix0"] % 2]

            def qk_in(k, i, ps):
                v.tensor_tensor(part(arena, 2 * S * k + S, S, i, 8 * S), ps[:, 0:S], inverse[:, 0:S], ALU.mult)\
                 .then_inc(dve_read, 1)
                dve.wait_ge(act_read, PAIR["qk"] + k + 1 + 4 * i)
                q = part(arena, 2 * S * k, S, i, 8 * S)
                v.tensor_tensor(q, q, inverse[:, 0:S], ALU.mult).then_inc(qk_scaled, 1)
            pair_stage("qk", qk_in, norm="mix0")
            for k in range(4):
                rest_next("sbv", k)
            for t in range(2):
                r = PAIR["sbv"] + t
                dve.wait_ge(odd_done, r + 1)
                v.tensor_scalar(sv[:, t, 512:D], bank[2 * (r % 2) + 1][:, :], inverse[:, S + t:S + t + 1], None, ALU.mult)\
                 .then_inc(dve_read, 1)
            dve.wait_ge(tables2_in, 16)

            def masked_logits(h, i):
                u = h % 4
                dve.wait_ge(z_done, h + 1 + 4 * i)
                if h >= 4:
                    dve.wait_ge(arg_done, h - 3 + 4 * i)
                link(v.scalar_tensor_tensor(zm[u], four[u][:, 0:384], SCALE, sb_mask, ALU.mult, ALU.add))
                if h >= 2:
                    dve.wait_ge(sp_done, h - 1 + 4 * i)
                v.scalar_tensor_tensor(az[u % 2], zm[u], -1.0, zm[u], ALU.mult, ALU.min).then_inc(z_mask, 1)

            def exponents(h, i):
                u = h % 4
                dve.wait_ge(suf_done, h + 1 + 4 * i)
                if h >= 2:
                    dve.wait_ge(w_done, h - 1 + 4 * i)
                v.tensor_tensor(ex[u % 2], zm[u], bank[6 + u % 2][:, 0:384], ALU.subtract).then_inc(arg_done, 1)

            def softplus(h, i):
                u = h % 4
                dve.wait_ge(soft_in, h + 1 + 4 * i)
                if h >= 2:
                    dve.wait_ge(suf_done, h - 1 + 4 * i)
                v.scalar_tensor_tensor(sp_t[u % 2], zm[u], 0.0, az[u % 2], ALU.max, ALU.add).then_inc(sp_done, 1)

            def sb_rest(m, i):
                dve.wait_ge(sbo_hi, m + 1 + 2 * i)
                v.tensor_tensor(part(op_lo, S * m, S, i, 2 * S), bank[m % 2][:, 0:S],
                                part(op_hi, S * m, S, i, 2 * S).bitcast(F32), ALU.subtract).then_inc(sbo_lo, 1)

            def sb_pair(m, i, last=False):
                softplus(2 * m, i)
                softplus(2 * m + 1, i)
                if not last:
                    masked_logits(2 * m + 2, i)
                    masked_logits(2 * m + 3, i)
                exponents(2 * m, i)
                exponents(2 * m + 1, i)
                if m >= 2:
                    sb_rest(m - 2, i)

            masked_logits(0, 0)
            masked_logits(1, 0)
            sb_pair(0, 0)
            sb_pair(1, 0)
            chain.loop(2, 4, lambda i: (sb_pair(2, i), sb_pair(3, i)))
            sb_pair(6, 0)
            sb_pair(7, 0, last=True)
            sb_rest(H // 2 - 2, 0)
            sb_rest(H // 2 - 1, 0)
            residual_stage("sbo", "f1")
            if stop == "sbo":
                return
            swiglu(1, "f1", "kv")
            inverse_kv = acc[NORM["kv"] % 2]
            pair_stage("kvk", lambda k, i, ps: v.tensor_copy(k_raw[:, 1, :], ps[:, 0:S]).then_inc(dve_read, 1), norm="kv")
            pair_stage("kvv", lambda k, i, ps: v.tensor_scalar(v_sh[:, 1, :], ps[:, 0:S], inverse_kv[:, S + 1:S + 2], None,
                                                               ALU.mult).then_inc(dve_read, 1))

            def rotate_keys():
                dve.wait_ge(act_read, PAIR["kvk"] + 1)
                dve.wait_ge(dve_read, PAIR["kvk"] + 1)
                over = inverse_kv[:, 0:S].unsqueeze(1).to_broadcast([P, 2, S])
                link(v.tensor_tensor(k_raw[:, :, :], k_raw[:, :, :], over, ALU.mult))
                for base in (0, 64):
                    for dst, src in ((base, base + 32), (base + 32, base)):
                        v.tensor_copy(k_sh[dst:dst + 32, :, :], k_raw[src:src + 32, :, :]).then_inc(k_half, 1)
                dve.wait_ge(k_half, 4)
                both = lambda x: x.unsqueeze(1).to_broadcast([P, 2, S])
                link(v.tensor_tensor(k_sh[:, :, :], k_sh[:, :, :], both(sin2), ALU.mult))
                link(v.tensor_tensor(k_raw[:, :, :], k_raw[:, :, :], both(cos2), ALU.mult))
                v.tensor_tensor(k_sh[:, :, :], k_sh[:, :, :], k_raw[:, :, :], ALU.add).then_inc(k_rot, 1)
                v.tensor_scalar(sinks, small[:, TOPK:TOPK + H], 1.0 / SCALE, None, ALU.mult).then_inc(k_rot, 1)
            swiglu(2, "f2", "mix1", rotate_keys)
            inverse_mix1 = acc[NORM["mix1"] % 2][:, 0:S]

            def rotate_queries(k):
                if k == 0:
                    link(v.tensor_tensor(sin2, sin2, inverse_mix1, ALU.mult))
                    link(v.tensor_tensor(cos2, cos2, inverse_mix1, ALU.mult))
                dve.wait_ge(q_swap, k + 1)
                q, t = q_sw[:, 2 * k:2 * k + 2, :], q_half[:, 2 * k:2 * k + 2, :]
                both = lambda x: x.unsqueeze(1).to_broadcast([P, 2, S])
                swapped = bank[4 + k % 2].rearrange("p (c t) -> p c t", t=S)
                link(v.tensor_tensor(t, swapped, both(sin2), ALU.mult))
                link(v.tensor_tensor(q, q, both(cos2), ALU.mult))
                v.tensor_tensor(q, q, t, ALU.add).then_inc(q_rot, 1)

            def sq_in(k, i, ps):
                v.tensor_copy(q_sw[:, 2 * k + 1, :], ps[:, 0:S]).then_inc(dve_read, 1)
                if k:
                    rotate_queries(k - 1)
            pair_stage("sq", sq_in, norm="mix1")
            rotate_queries(3)

            def sw_mask(h, i):
                u = h % 4
                s_ = four[u][:, 0:385]
                dve.wait_ge(sink_in, h + 1 + 4 * i)
                link(v.scalar_tensor_tensor(s_, s_, SCALE, swa_mask, ALU.mult, ALU.add))
                v.tensor_reduce(soft[:, 2 * u:2 * u + 1], s_[:, 0:P + 1], AX.X, ALU.max, negate=True)
                v.tensor_reduce(soft[:, 2 * u + 1:2 * u + 2], s_[:, P:P + 1 + S], AX.X, ALU.max, negate=True)\
                 .then_inc(w_mask, 1)

            def sw_normalise(h, i):
                u = h % 4
                dve.wait_ge(w_exp, 2 * h + 2 + 8 * i)
                link(v.reciprocal(soft[:, 16 + 2 * u:18 + 2 * u], soft[:, 8 + 2 * u:10 + 2 * u]))
                for t, (at, n) in enumerate(((0, P + 1), (P + 1, S + 1))):
                    p = sw_p[u][:, at:at + n]
                    v.tensor_scalar(p, p, soft[:, 16 + 2 * u + t:17 + 2 * u + t], None, ALU.mult).then_inc(w_p, 1)
                if h >= 3 and h % 2 == 1:
                    sw_rest((h - 3) // 2, i)

            def sw_rest(m, i):
                dve.wait_ge(w_hi_o, m + 1 + 2 * i)
                v.tensor_tensor(part(op_lo, S * m, S, i, 2 * S), bank[m % 2][:, 0:S],
                                part(op_hi, S * m, S, i, 2 * S).bitcast(F32), ALU.subtract).then_inc(w_lo_o, 1)

            def sw_turn(t, i):
                for u in range(4):
                    sw_mask(4 * t + u, i)
                    if 4 * t + u >= 1:
                        sw_normalise(4 * t + u - 1, i)
            sw_turn(0, 0)
            chain.loop(3, 8, lambda i: sw_turn(1, i))
            sw_normalise(H - 1, 0)
            sw_rest(H // 2 - 1, 0)
            residual_stage("swo", "f3")
            swiglu(3, "f3", "final2")
            norm_in_place("final2")

def tiles_of(m, per):
    k, n = m.shape
    return np.ascontiguousarray(m.reshape(k // P, P, n // P // per, per, P).transpose(2, 1, 3, 0, 4)
                                .reshape(n // P // per, P, -1))


def rows_of(m):
    k, n = m.shape
    return m.reshape(k // P, P, n).transpose(1, 0, 2).reshape(P, -1)


def swap_halves(m, width):
    k, n = m.shape
    return m.reshape(k, n // width, 2, width // 2)[:, :, ::-1, :].reshape(k, n)


def rope_tables(n, dim, base, reps):
    half = dim // 2
    inv = np.power(np.float32(base), -np.arange(half, dtype=np.float32) * np.float32(2.0 / dim)).astype(np.float32)
    ang = (np.arange(n, dtype=np.float32)[None, :] * inv[:, None]).astype(np.float32)
    cos, sin = np.cos(ang).astype(np.float32), np.sin(ang).astype(np.float32)
    return np.tile(np.concatenate([cos, cos]), (reps, 1)), np.tile(np.concatenate([-sin, sin]), (reps, 1))


def arrange(a):
    f = np.float32
    w = {}
    x_t = np.concatenate([a["meta_tokens"].T, a["x"][0].T], axis=1)
    w["x_t"] = np.ascontiguousarray(x_t.reshape(C, P, T).transpose(1, 0, 2))
    cuts = np.cumsum([D, D, QL, KVL, ROPE, D, D])
    xr, gr, cq, ckv, kr, g_rnn, g_att, _ = np.split(a["w_in"][0], cuts, axis=1)
    w["xr"] = tiles_of(xr, 2)
    kr4 = np.tile(np.concatenate([kr, swap_halves(kr, ROPE)], axis=1), (1, 2))
    w["lat"] = tiles_of(np.concatenate([ckv, kr4, cq], axis=1), 2)
    w["gates"] = np.stack([a["rg_wa"][0], a["rg_wx"][0]], axis=1).reshape(16, P, P).transpose(1, 0, 2).reshape(1, P, TILE)
    w["gr"] = tiles_of(gr, 2)
    uq = a["w_uq"][0].reshape(QL, H, NOPE + ROPE)
    nope, rope = uq[:, :, :NOPE].reshape(QL, -1), uq[:, :, NOPE:].reshape(QL, -1)
    both = np.stack([rope.reshape(QL, 4, P), swap_halves(rope, ROPE).reshape(QL, 4, P)], axis=2).reshape(QL, -1)
    w["uq"] = tiles_of(np.concatenate([nope, both], axis=1), 4)
    ukv = a["w_ukv"][0].reshape(KVL, H, NOPE + VD)
    w["uk"] = tiles_of(ukv[:, :, :NOPE].reshape(KVL, -1), C)
    w["uv"] = rows_of(ukv[:, :, NOPE:].reshape(KVL, -1))[None]
    g1, y1, g2, y2 = (tiles_of(m, 1) for m in (g_rnn, a["w_rnn_out"][0], g_att, a["w_attn_out"][0]))
    w["mix"] = np.stack([np.concatenate([g1, y1], axis=2), np.concatenate([g2, y2], axis=2)], axis=1).reshape(16, P, TILE)
    w["out1"] = tiles_of(a["w_out"][0], 2)
    w["pq"] = tiles_of(a["peer_wq"][0], 2)
    w["keys"] = np.concatenate([a["peer_keys1"][0].T, a["peer_keys2"][0].T], axis=1)
    w["uv_rows"] = np.concatenate([a["peer_u"][0], a["peer_v"][0]], axis=1)
    for n in range(4):
        layer, which = n // 2, n % 2 + 1
        gate, up = np.split(a[f"ffn{which}_w_in_2"][layer], 2, axis=1)
        w[f"ffi{n}"] = tiles_of(np.stack([gate.reshape(D, NF, P), up.reshape(D, NF, P)], axis=2).reshape(D, -1), 2)
        down = tiles_of(a[f"ffn{which}_w_out_2"][layer], 1)
        w[f"ffo{n}"] = down.reshape(C, P, 2, FH * P).transpose(0, 2, 1, 3).reshape(2 * C, P, FH * P)
    q, k, v2 = np.split(a["sb_w_qkv_2"][0], 3, axis=1)
    w["qk"] = tiles_of(np.concatenate([q, k], axis=1), 2)
    w["sbv"] = v2.reshape(4, 2, P, D).transpose(0, 2, 1, 3).reshape(4, P, TILE)
    w["sbo"] = tiles_of(a["sb_w_o_2"][0], 2)
    kk, kv = np.split(a["kv_w_2"], 2, axis=1)
    w["kvk"] = tiles_of(kk, 2)
    w["kvv"] = rows_of(kv)[None]
    w["sq"] = tiles_of(a["swa_w_q_2"][0].reshape(D, H, 64)[:, HEAD_AT].reshape(D, D), 2)
    w["swo"] = tiles_of(a["swa_w_o_2"][0].reshape(H, 64, D)[HEAD_AT].reshape(D, D), 2)

    cols = lambda m: m.reshape(-1, P).T
    v = {"n1": a["norm1_g"][0], "cq": a["q_norm_g"][0], "ckv": a["kv_norm_g"][0], "cb": a["conv_b"][0],
         "ba": a["rg_ba"][0], "bx": a["rg_bx"][0], "lam": a["rg_lambda"][0], "n2": a["norm2_g"][0],
         "final1": a["final_g"], "f0": a["ffn1_norm_2"][0], "f1": a["ffn2_norm_2"][0], "f2": a["ffn1_norm_2"][1],
         "f3": a["ffn2_norm_2"][1], "mix0": a["mix_norm_2"][0], "mix1": a["mix_norm_2"][1], "kv": a["kv_norm_2"],
         "final2": a["final_norm_2"], **{f"cw{t}": a["conv_w"][0][t] for t in range(4)}}
    w["vecs"] = np.concatenate([cols(v[name]) for name, _ in VECS], axis=1)
    p = np.arange(P)[:, None]
    no = f(-1e30)
    mask = np.concatenate([np.where(np.arange(SA)[None] <= p + META, f(0), no),
                           np.where(np.arange(SB)[None] <= p + META + P, f(0), no)], axis=1)
    cos, sin = rope_tables(T, ROPE, 10000.0, 4)
    w["tables1"] = np.concatenate([mask, cos, sin], axis=1).astype(f)
    w["squares"] = np.concatenate([np.ones((P, P)), np.eye(P), p >= p.T, (p ^ 32) == p.T], axis=1).astype(f)
    sinks = a["swa_sinks_2"][0][HEAD_AT]
    w["small"] = np.concatenate([np.tile(np.arange(TOPK, dtype=f), (P, 1)), np.tile(sinks, (P, 1))], axis=1)
    before = np.where(p < p.T, f(0), no)
    sb_mask = np.concatenate([before, np.zeros((P, P), f), before], axis=1)
    j = np.arange(S)[None]
    swa_mask = np.concatenate([np.where(p.T <= p, f(0), no), np.zeros((P, 1), f), np.where((j > p) & (j <= p + P), f(0), no)], axis=1)
    w["tables2"] = np.concatenate([sb_mask, swa_mask, *rope_tables(S, 64, 10000.0, 2)], axis=1).astype(f)
    return {k: np.ascontiguousarray(m) for k, m in w.items()}


STOP = ORDER[-1]


def kernel(**inputs):
    import concourse.bacc as bacc
    from concourse.bass_utils import run_bass_kernel_spmd

    w = arrange({k: np.asarray(m) for k, m in inputs.items()})
    nc = bacc.Bacc("TRN2", target_bir_lowering=False, num_devices=1)
    aps = {k: nc.dram_tensor(f"in_{k}", m.shape, mybir.dt.from_np(m.dtype), kind="ExternalInput").ap() for k, m in w.items()}
    out = nc.dram_tensor("out_t", (P, C, S), F32, kind="ExternalOutput").ap()
    program(nc, aps, out, STOP)
    r = run_bass_kernel_spmd(nc, [{f"in_{k}": m for k, m in w.items()}], core_ids=[0])
    return r.results[0]["out_t"].transpose(2, 1, 0).reshape(1, S, D)
```
